# Optimizing a Trainium2 kernel written in Bass

```python
import math
import jax, jax.numpy as jnp
from jax import lax
import numpy as np

D_MODEL = 1024
BATCH = 1
SEQ = 256
DEPTH = 1

CHUNK = 64
Q_BLOCK = 128
EPS = 1e-6
D_FF = 2816
N_MOD = 9
MLA_HEADS = 8
MLA_Q_RANK = 768
MLA_KV_RANK = 256
MLA_NOPE = 128
MLA_ROPE = 64
MLA_V = 128
ROPE_THETA = 10000.0
GDN_HEADS = 8
GDN_DK = 128
GDN_DV = 128
CONV_W = 4
N_BRANCH = 2
IN_SPLITS = (MLA_Q_RANK, MLA_KV_RANK, MLA_ROPE, GDN_HEADS * GDN_DK, GDN_HEADS * GDN_DK, GDN_HEADS * GDN_DV, GDN_HEADS, GDN_HEADS, GDN_HEADS * GDN_DV, N_BRANCH * D_MODEL)
D_IN = sum(IN_SPLITS)


def rmsnorm(x, g):
    xf = x.astype(jnp.float32)
    xf = xf * lax.rsqrt(jnp.mean(xf * xf, axis=-1, keepdims=True) + EPS)
    return (xf * g.astype(jnp.float32)).astype(x.dtype)

def modulate(x, g, shift, scale):
    return rmsnorm(x, g) * (1.0 + scale[:, None, :]) + shift[:, None, :]

def swiglu(h, w_gate, w_up, w_down):
    return (jax.nn.silu(h @ w_gate) * (h @ w_up)) @ w_down

def l2norm(t):
    return t * lax.rsqrt(jnp.sum(t * t, axis=-1, keepdims=True) + EPS)

def rope(x, cos, sin):
    xf = x.astype(jnp.float32)
    x1, x2 = jnp.split(xf, 2, axis=-1)
    return jnp.concatenate([x1 * cos - x2 * sin, x2 * cos + x1 * sin], axis=-1).astype(x.dtype)

def mla_branch(q_lat, kv_lat, k_pe, g_q, w_uq, g_kv, w_ukv, cos, sin):
    B, S, _ = q_lat.shape
    H = MLA_HEADS
    q = (rmsnorm(q_lat, g_q) @ w_uq).reshape(B, S, H, MLA_NOPE + MLA_ROPE)
    q_nope = q[..., :MLA_NOPE]
    q_pe = rope(q[..., MLA_NOPE:], cos[:, None, :], sin[:, None, :])
    kv = (rmsnorm(kv_lat, g_kv) @ w_ukv).reshape(B, S, H, MLA_NOPE + MLA_V)
    k_nope = kv[..., :MLA_NOPE]
    v = kv[..., MLA_NOPE:]
    k_pe = rope(k_pe, cos, sin)
    scale = (MLA_NOPE + MLA_ROPE) ** -0.5
    nb = S // Q_BLOCK
    qn_blk = q_nope.reshape(B, nb, Q_BLOCK, H, MLA_NOPE).transpose(1, 0, 2, 3, 4)
    qp_blk = q_pe.reshape(B, nb, Q_BLOCK, H, MLA_ROPE).transpose(1, 0, 2, 3, 4)
    k_chunk = jnp.arange(S) // CHUNK

    def attend(args):
        qn, qp, blk = args
        s = jnp.einsum('bqhd,bkhd->bhqk', qn, k_nope) + jnp.einsum('bqhr,bkr->bhqk', qp, k_pe)
        s = s.astype(jnp.float32) * scale
        q_chunk = (blk * Q_BLOCK + jnp.arange(Q_BLOCK)) // CHUNK
        mask = k_chunk[None, :] <= q_chunk[:, None]
        s = jnp.where(mask, s, -jnp.inf)
        p = jax.nn.softmax(s, axis=-1).astype(v.dtype)
        return jnp.einsum('bhqk,bkhd->bqhd', p, v)

    o = lax.map(attend, (qn_blk, qp_blk, jnp.arange(nb)))
    return o.transpose(1, 0, 2, 3, 4).reshape(B, S, H * MLA_V)

def causal_depthwise_conv(x, w):
    C = x.shape[-1]
    xp = jnp.pad(x, ((0, 0), (CONV_W - 1, 0), (0, 0)))
    return lax.conv_general_dilated(xp, w[:, None, :].astype(x.dtype), window_strides=(1,), padding='VALID', dimension_numbers=('NWC', 'WIO', 'NWC'), feature_group_count=C)

def gated_deltanet_branch(qkv, a, b, z, w_conv, a_log, dt_bias, g_out):
    B, S, _ = qkv.shape
    N = S // CHUNK
    H, DK, DV = GDN_HEADS, GDN_DK, GDN_DV
    f32 = jnp.float32
    qkv = jax.nn.silu(causal_depthwise_conv(qkv, w_conv))
    q, k, v = jnp.split(qkv, [H * DK, 2 * H * DK], axis=-1)

    def to_chunks(t, d):
        return t.reshape(B, N, CHUNK, H, d).transpose(0, 3, 1, 2, 4).astype(f32)

    q = l2norm(to_chunks(q, DK)) * (DK ** -0.5)
    k = l2norm(to_chunks(k, DK))
    v = to_chunks(v, DV)
    beta = jax.nn.sigmoid(b.astype(f32)).reshape(B, N, CHUNK, H).transpose(0, 3, 1, 2)
    g = -jnp.exp(a_log.astype(f32)) * jax.nn.softplus(a.astype(f32) + dt_bias.astype(f32))
    g = g.reshape(B, N, CHUNK, H).transpose(0, 3, 1, 2)
    decay = jnp.cumsum(g, axis=-1)
    idx = jnp.arange(CHUNK)
    causal = idx[:, None] >= idx[None, :]
    strict = idx[:, None] > idx[None, :]
    L = jnp.exp(jnp.where(causal, decay[..., :, None] - decay[..., None, :], -jnp.inf))
    k_beta = k * beta[..., None]
    A = jnp.where(strict, jnp.einsum('bhnid,bhnjd->bhnij', k_beta, k) * L, 0.0)
    eye = jnp.eye(CHUNK, dtype=f32)
    T = lax.linalg.triangular_solve(A + eye, jnp.broadcast_to(eye, A.shape), left_side=True, lower=True, unit_diagonal=True)
    w = jnp.einsum('bhnij,bhnjd->bhnid', T, k_beta * jnp.exp(decay)[..., None])
    u = jnp.einsum('bhnij,bhnje->bhnie', T, v * beta[..., None])
    attn_intra = jnp.einsum('bhnid,bhnjd->bhnij', q, k) * L
    q_dec = q * jnp.exp(decay)[..., None]
    k_dec = k * jnp.exp(decay[..., -1:] - decay)[..., None]
    chunk_decay = jnp.exp(decay[..., -1])
    xs = tuple(jnp.moveaxis(t, 2, 0) for t in (q_dec, k_dec, w, u, attn_intra, chunk_decay))

    def step(state, inp):
        qd, kd, w_n, u_n, a_n, cd = inp
        v_new = u_n - jnp.einsum('bhcd,bhde->bhce', w_n, state)
        o = jnp.einsum('bhcd,bhde->bhce', qd, state) + jnp.einsum('bhij,bhje->bhie', a_n, v_new)
        state = state * cd[..., None, None] + jnp.einsum('bhcd,bhce->bhde', kd, v_new)
        return state, o

    state0 = jnp.zeros((B, H, DK, DV), f32)
    _, o = lax.scan(step, state0, xs)
    o = o.transpose(1, 0, 3, 2, 4).reshape(B, S, H, DV)
    o = rmsnorm(o, g_out) * jax.nn.silu(z.reshape(B, S, H, DV).astype(f32))
    return o.reshape(B, S, H * DV).astype(z.dtype)

def first_inputs(seed: int = 0) -> dict:
    key = jax.random.key(seed)
    ks = jax.random.split(key, 32)
    f32 = jnp.float32
    L = DEPTH

    def dense(k, shape, fan_in, mult=1.0):
        return jax.random.normal(k, shape, f32) * (mult * fan_in ** -0.5)

    def gain(k, shape):
        return 1.0 + 0.05 * jax.random.normal(k, shape, f32)

    dt = jnp.exp(jax.random.uniform(ks[17], (L, GDN_HEADS), f32, math.log(1e-3), math.log(1e-1)))
    return {
        'x': jax.random.normal(ks[0], (BATCH, SEQ, D_MODEL), f32),
        'c': jax.random.normal(ks[1], (BATCH, D_MODEL), f32),
        'w_ada': dense(ks[2], (L, D_MODEL, N_MOD * D_MODEL), D_MODEL, 0.5),
        'b_ada': 0.01 * jax.random.normal(ks[3], (L, N_MOD * D_MODEL), f32),
        'g_ffn1': gain(ks[4], (L, D_MODEL)),
        'w1_gate': dense(ks[5], (L, D_MODEL, D_FF), D_MODEL),
        'w1_up': dense(ks[6], (L, D_MODEL, D_FF), D_MODEL),
        'w1_down': dense(ks[7], (L, D_FF, D_MODEL), D_FF),
        'g_mix': gain(ks[8], (L, D_MODEL)),
        'w_in': dense(ks[9], (L, D_MODEL, D_IN), D_MODEL),
        'g_q_lat': gain(ks[10], (L, MLA_Q_RANK)),
        'w_uq': dense(ks[11], (L, MLA_Q_RANK, MLA_HEADS * (MLA_NOPE + MLA_ROPE)), MLA_Q_RANK),
        'g_kv_lat': gain(ks[12], (L, MLA_KV_RANK)),
        'w_ukv': dense(ks[13], (L, MLA_KV_RANK, MLA_HEADS * (MLA_NOPE + MLA_V)), MLA_KV_RANK),
        'w_conv': dense(ks[14], (L, CONV_W, 3 * GDN_HEADS * GDN_DK), CONV_W),
        'a_log': jnp.log(jax.random.uniform(ks[15], (L, GDN_HEADS), f32, 1.0, 16.0)),
        'dt_bias': dt + jnp.log(-jnp.expm1(-dt)),
        'g_gdn_out': gain(ks[16], (L, GDN_DV)),
        'w_o_mla': dense(ks[18], (L, MLA_HEADS * MLA_V, D_MODEL), MLA_HEADS * MLA_V),
        'w_o_gdn': dense(ks[19], (L, GDN_HEADS * GDN_DV, D_MODEL), GDN_HEADS * GDN_DV),
        'w_out': dense(ks[20], (L, D_MODEL, D_MODEL), D_MODEL),
        'g_ffn2': gain(ks[21], (L, D_MODEL)),
        'w2_gate': dense(ks[22], (L, D_MODEL, D_FF), D_MODEL),
        'w2_up': dense(ks[23], (L, D_MODEL, D_FF), D_MODEL),
        'w2_down': dense(ks[24], (L, D_FF, D_MODEL), D_FF),
        'g_final': gain(ks[25], (D_MODEL,)),
    }

def first_block(x, c, w_ada, b_ada, g_ffn1, w1_gate, w1_up, w1_down, g_mix, w_in, g_q_lat, w_uq, g_kv_lat, w_ukv, w_conv, a_log, dt_bias, g_gdn_out, w_o_mla, w_o_gdn, w_out, g_ffn2, w2_gate, w2_up, w2_down, g_final):
    S = x.shape[1]
    pos = jnp.arange(S, dtype=jnp.float32)
    inv_freq = ROPE_THETA ** (-jnp.arange(0, MLA_ROPE, 2, dtype=jnp.float32) / MLA_ROPE)
    ang = pos[:, None] * inv_freq[None, :]
    cos, sin = jnp.cos(ang), jnp.sin(ang)
    split_at = np.cumsum(IN_SPLITS)[:-1].tolist()
    c_act = jax.nn.silu(c)
    for l in range(DEPTH):
        ada = c_act @ w_ada[l] + b_ada[l]
        sh1, sc1, gt1, sh2, sc2, gt2, sh3, sc3, gt3 = jnp.split(ada, N_MOD, axis=-1)
        h = modulate(x, g_ffn1[l], sh1, sc1)
        x = x + 0.5 * gt1[:, None, :] * swiglu(h, w1_gate[l], w1_up[l], w1_down[l])
        h = modulate(x, g_mix[l], sh2, sc2)
        proj = h @ w_in[l]
        q_lat, kv_lat, k_pe, gq, gk, gv, ga, gb, gz, gates = jnp.split(proj, split_at, axis=-1)
        y_mla = mla_branch(q_lat, kv_lat, k_pe, g_q_lat[l], w_uq[l], g_kv_lat[l], w_ukv[l], cos, sin) @ w_o_mla[l]
        y_gdn = gated_deltanet_branch(jnp.concatenate([gq, gk, gv], axis=-1), ga, gb, gz, w_conv[l], a_log[l], dt_bias[l], g_gdn_out[l]) @ w_o_gdn[l]
        gate_mla, gate_gdn = jnp.split(jax.nn.sigmoid(gates), N_BRANCH, axis=-1)
        mixed = (gate_mla * y_mla + gate_gdn * y_gdn) @ w_out[l]
        x = x + gt2[:, None, :] * mixed
        h = modulate(x, g_ffn2[l], sh3, sc3)
        x = x + 0.5 * gt3[:, None, :] * swiglu(h, w2_gate[l], w2_up[l], w2_down[l])
    return rmsnorm(x, g_final)


DEPTH_2 = 2

PLE_DIM = 256
SC_WIDTH = D_MODEL
SC_KERNEL = 3
SSM_INNER = 2 * D_MODEL
SSM_HEADDIM = 64
SSM_HEADS = SSM_INNER // SSM_HEADDIM
SSM_GROUPS = 4
SSM_STATE = 128
SSM_CONV = 4
SSM_CHUNK = 128
SSM_CONV_DIM = SSM_INNER + 2 * SSM_GROUPS * SSM_STATE
PROJ_SIZES = (SC_WIDTH, SC_WIDTH, SC_WIDTH,
              SSM_INNER, SSM_CONV_DIM, SSM_HEADS,
              D_MODEL, D_MODEL)
PROJ_DIM = sum(PROJ_SIZES)
PROJ_SPLITS = tuple(int(v) for v in np.cumsum(PROJ_SIZES)[:-1])


def rmsnorm_2(x, g):
    xf = x.astype(jnp.float32)
    y = xf * lax.rsqrt(jnp.mean(xf * xf, axis=-1, keepdims=True) + EPS)
    return y.astype(x.dtype) * g

def grouped_rmsnorm(x, g, groups):
    shp = x.shape
    xf = x.astype(jnp.float32).reshape(shp[:-1] + (groups, shp[-1] // groups))
    y = xf * lax.rsqrt(jnp.mean(xf * xf, axis=-1, keepdims=True) + EPS)
    return y.reshape(shp).astype(x.dtype) * g

def swiglu_2(x, wg, wu, wd):
    return (jax.nn.silu(x @ wg) * (x @ wu)) @ wd

def causal_depthwise_conv_2(x, w):
    k, c = w.shape
    return lax.conv_general_dilated(
        x, w.reshape(k, 1, c).astype(x.dtype), window_strides=(1,), padding=[(k - 1, 0)],
        dimension_numbers=("NWC", "WIO", "NWC"), feature_group_count=c)

def ssd_chunked(xdt, a, bm, cm):
    b, s, h, p = xdt.shape
    g, n = bm.shape[2], bm.shape[3]
    r = h // g
    nc, L = s // SSM_CHUNK, SSM_CHUNK
    dt_ = xdt.dtype
    X = xdt.reshape(b, nc, L, g, r, p)
    A = a.reshape(b, nc, L, g, r).astype(jnp.float32)
    Bc = bm.reshape(b, nc, L, g, n)
    Cc = cm.reshape(b, nc, L, g, n)
    a_cum = jnp.cumsum(A, axis=2)
    causal = jnp.tril(jnp.ones((L, L), dtype=bool))[None, None, :, :, None, None]
    diff = a_cum[:, :, :, None] - a_cum[:, :, None, :]
    decay = jnp.exp(jnp.where(causal, diff, -jnp.inf)).astype(dt_)
    cb = jnp.einsum("bclgn,bcsgn->bclsg", Cc, Bc)
    y_diag = jnp.einsum("bclsg,bclsgr,bcsgrp->bclgrp", cb, decay, X)
    decay_to_end = jnp.exp(a_cum[:, :, -1:] - a_cum).astype(dt_)
    states = jnp.einsum("bclgn,bclgr,bclgrp->bcgrpn", Bc, decay_to_end, X)
    chunk_decay = jnp.exp(a_cum[:, :, -1]).astype(dt_)

    def step(carry, inp):
        st, dec = inp
        return carry * dec[..., None, None] + st, carry

    init = jnp.zeros((b, g, r, p, n), dtype=states.dtype)
    _, prev = lax.scan(step, init, (jnp.swapaxes(states, 0, 1), jnp.swapaxes(chunk_decay, 0, 1)))
    prev = jnp.swapaxes(prev, 0, 1)
    y_off = jnp.einsum("bclgn,bcgrpn,bclgr->bclgrp", Cc, prev, jnp.exp(a_cum).astype(dt_))
    return (y_diag + y_off).reshape(b, s, h, p)

def hybrid_mixer(u, w_in, sc_conv_w, sc_w_out, m_conv_w, m_conv_b, m_dt_bias, m_A_log, m_D,
                 m_norm, m_w_out, w_o):
    b, s, _ = u.shape
    proj = u @ w_in
    sc_b, sc_c, sc_x, m_z, m_xbc, m_dt, gate_a, gate_m = jnp.split(proj, PROJ_SPLITS, axis=-1)
    y_a = (sc_b * causal_depthwise_conv_2(sc_c * sc_x, sc_conv_w)) @ sc_w_out
    xbc = jax.nn.silu(causal_depthwise_conv_2(m_xbc, m_conv_w) + m_conv_b)
    xs, bm, cm = jnp.split(xbc, (SSM_INNER, SSM_INNER + SSM_GROUPS * SSM_STATE), axis=-1)
    dt = jax.nn.softplus((m_dt + m_dt_bias).astype(jnp.float32))
    A = -jnp.exp(m_A_log.astype(jnp.float32))
    xh = xs.reshape(b, s, SSM_HEADS, SSM_HEADDIM)
    y = ssd_chunked(xh * dt.astype(xh.dtype)[..., None], A * dt,
                    bm.reshape(b, s, SSM_GROUPS, SSM_STATE), cm.reshape(b, s, SSM_GROUPS, SSM_STATE))
    y = (y + m_D[:, None] * xh).reshape(b, s, SSM_INNER)
    y_m = grouped_rmsnorm(y * jax.nn.silu(m_z), m_norm, SSM_GROUPS) @ m_w_out
    merged = jax.nn.sigmoid(gate_a) * y_a + jax.nn.sigmoid(gate_m) * y_m
    return merged @ w_o

def second_inputs(seed: int = 0) -> dict:
    key = jax.random.key(seed)
    ks = iter(jax.random.split(key, 40))

    def nrm(shape, fan_in):
        return jax.random.normal(next(ks), shape, jnp.float32) * (fan_in ** -0.5)

    def gain(shape):
        return 1.0 + 0.05 * jax.random.normal(next(ks), shape, jnp.float32)

    dt0 = jnp.exp(jax.random.uniform(next(ks), (DEPTH_2, SSM_HEADS), jnp.float32)
                  * (np.log(0.1) - np.log(0.001)) + np.log(0.001))
    return {
        "x": jax.random.normal(next(ks), (BATCH, SEQ, D_MODEL), jnp.float32),
        "p": jax.random.normal(next(ks), (DEPTH_2, BATCH, SEQ, PLE_DIM), jnp.float32),
        "ffn1_norm": gain((DEPTH_2, D_MODEL)),
        "ffn1_wg": nrm((DEPTH_2, D_MODEL, D_FF), D_MODEL),
        "ffn1_wu": nrm((DEPTH_2, D_MODEL, D_FF), D_MODEL),
        "ffn1_wd": nrm((DEPTH_2, D_FF, D_MODEL), D_FF),
        "mix_norm": gain((DEPTH_2, D_MODEL)),
        "w_in": nrm((DEPTH_2, D_MODEL, PROJ_DIM), D_MODEL),
        "sc_conv_w": nrm((DEPTH_2, SC_KERNEL, SC_WIDTH), SC_KERNEL),
        "sc_w_out": nrm((DEPTH_2, SC_WIDTH, D_MODEL), SC_WIDTH),
        "m_conv_w": nrm((DEPTH_2, SSM_CONV, SSM_CONV_DIM), SSM_CONV),
        "m_conv_b": 0.02 * jax.random.normal(next(ks), (DEPTH_2, SSM_CONV_DIM), jnp.float32),
        "m_dt_bias": dt0 + jnp.log(-jnp.expm1(-dt0)),
        "m_A_log": jnp.log(jax.random.uniform(next(ks), (DEPTH_2, SSM_HEADS), jnp.float32, 1.0, 16.0)),
        "m_D": gain((DEPTH_2, SSM_HEADS)),
        "m_norm": gain((DEPTH_2, SSM_INNER)),
        "m_w_out": nrm((DEPTH_2, SSM_INNER, D_MODEL), SSM_INNER),
        "w_o": nrm((DEPTH_2, D_MODEL, D_MODEL), D_MODEL),
        "ffn2_norm": gain((DEPTH_2, D_MODEL)),
        "ffn2_wg": nrm((DEPTH_2, D_MODEL, D_FF), D_MODEL),
        "ffn2_wu": nrm((DEPTH_2, D_MODEL, D_FF), D_MODEL),
        "ffn2_wd": nrm((DEPTH_2, D_FF, D_MODEL), D_FF),
        "ple_norm": gain((DEPTH_2, D_MODEL)),
        "ple_w_gate": nrm((DEPTH_2, D_MODEL, D_MODEL), D_MODEL),
        "ple_w_proj": nrm((DEPTH_2, PLE_DIM, D_MODEL), PLE_DIM),
        "final_norm": gain((D_MODEL,)),
    }

def second_block(x, p, ffn1_norm, ffn1_wg, ffn1_wu, ffn1_wd, mix_norm, w_in, sc_conv_w, sc_w_out,
              m_conv_w, m_conv_b, m_dt_bias, m_A_log, m_D, m_norm, m_w_out, w_o,
              ffn2_norm, ffn2_wg, ffn2_wu, ffn2_wd, ple_norm, ple_w_gate, ple_w_proj, final_norm):
    h = x
    for i in range(DEPTH_2):
        h = h + 0.5 * swiglu_2(rmsnorm_2(h, ffn1_norm[i]), ffn1_wg[i], ffn1_wu[i], ffn1_wd[i])
        h = h + hybrid_mixer(rmsnorm_2(h, mix_norm[i]), w_in[i], sc_conv_w[i], sc_w_out[i],
                             m_conv_w[i], m_conv_b[i], m_dt_bias[i], m_A_log[i], m_D[i],
                             m_norm[i], m_w_out[i], w_o[i])
        h = h + 0.5 * swiglu_2(rmsnorm_2(h, ffn2_norm[i]), ffn2_wg[i], ffn2_wu[i], ffn2_wd[i])
        gate = jax.nn.sigmoid(rmsnorm_2(h, ple_norm[i]) @ ple_w_gate[i])
        h = h + gate * (p[i] @ ple_w_proj[i])
    return rmsnorm_2(h, final_norm)


def setup_inputs(seed=0):
    out = dict(first_inputs(seed))
    for name, value in second_inputs(seed + 1).items():
        if name != "x":
            out[name + "_2"] = value
    return out


def reference(
    x, c, w_ada, b_ada, g_ffn1, w1_gate, w1_up, w1_down, g_mix, w_in, g_q_lat, w_uq, g_kv_lat,
    w_ukv, w_conv, a_log, dt_bias, g_gdn_out, w_o_mla, w_o_gdn, w_out, g_ffn2, w2_gate, w2_up,
    w2_down, g_final, p_2, ffn1_norm_2, ffn1_wg_2, ffn1_wu_2, ffn1_wd_2, mix_norm_2, w_in_2,
    sc_conv_w_2, sc_w_out_2, m_conv_w_2, m_conv_b_2, m_dt_bias_2, m_A_log_2, m_D_2, m_norm_2,
    m_w_out_2, w_o_2, ffn2_norm_2, ffn2_wg_2, ffn2_wu_2, ffn2_wd_2, ple_norm_2, ple_w_gate_2,
    ple_w_proj_2, final_norm_2,
):
    x = first_block(
        x, c, w_ada, b_ada, g_ffn1, w1_gate, w1_up, w1_down, g_mix, w_in, g_q_lat, w_uq,
        g_kv_lat, w_ukv, w_conv, a_log, dt_bias, g_gdn_out, w_o_mla, w_o_gdn, w_out, g_ffn2,
        w2_gate, w2_up, w2_down, g_final,
    )
    return second_block(
        x, p_2, ffn1_norm_2, ffn1_wg_2, ffn1_wu_2, ffn1_wd_2, mix_norm_2, w_in_2, sc_conv_w_2,
        sc_w_out_2, m_conv_w_2, m_conv_b_2, m_dt_bias_2, m_A_log_2, m_D_2, m_norm_2, m_w_out_2,
        w_o_2, ffn2_norm_2, ffn2_wg_2, ffn2_wu_2, ffn2_wd_2, ple_norm_2, ple_w_gate_2,
        ple_w_proj_2, final_norm_2,
    )


_drawn_inputs = setup_inputs


def setup_inputs(seed=0):
    import zlib

    import numpy as np

    out = dict(_drawn_inputs(seed))
    spreads = {}
    factors = {'b_ada': 4.859,
     'g_ffn1': 5.027,
     'g_mix': 4.327,
     'g_q_lat': 8.0,
     'g_kv_lat': 8.0,
     'a_log': 3.646,
     'g_gdn_out': 6.224,
     'g_ffn2': 4.767,
     'm_conv_b_2': 3.576,
     'm_D_2': 2.981,
     'ple_norm_2': 5.355}
    for name, (base, spread) in spreads.items():
        noise = np.random.default_rng([zlib.crc32(name.encode()), seed]).standard_normal(out[name].shape)
        drawn = base * np.exp(spread * noise) if base else spread * noise
        out[name] = __import__('jax').numpy.asarray(drawn.astype(out[name].dtype))
    for name, factor in factors.items():
        out[name] = (out[name] * factor).astype(out[name].dtype)
    return out
```

```python
from contextlib import ExitStack, contextmanager

import numpy as np

import concourse.bass as bass
from concourse import mybir

F32 = mybir.dt.float32
F32R = mybir.dt.float32r
ALU = mybir.AluOpType
ACT = mybir.ActivationFunctionType
AX = mybir.AxisListType

P = 128
T = 256
D = 1024
DT = D // P
FT = 2816 // P
N_ADA = 9 * DT
LAYERS = 2
EPS = 1e-6
H = 8
QT, KVT = 6, 2
ROPE = 64
SMALL1 = ROPE + 2 * H
SSM_H = 32
SSM_G = 4
XT = 16
CONVT = 24
RING = 3
AHEAD = 2
U = 8 * P

FFN_UNITS = 3 * FT
BLOCK1_UNITS = N_ADA + 2 * FFN_UNITS + 1 + 8 + 9 + 2 + 2 + 8 + CONVT + 8 + 8 + 16 + 8
BLOCK1_PAD = -BLOCK1_UNITS % RING
LAYER_UNITS = 2 * FFN_UNITS + 1 + 24 + 8 + CONVT + 16 + 16 + 16 + 8 + 8 + 1 + 2
LAYER_PAD = -LAYER_UNITS % RING
UNITS = BLOCK1_UNITS + BLOCK1_PAD + LAYERS * (LAYER_UNITS + LAYER_PAD) + RING

PER_PE = {
    "lo_ready": 258, "units_begun": 258, "lin_ready": 120, "lin_evac": 120, "gu_ready": 44, "a_ready": 44,
    "a_lo": 44, "y_ready": 2, "sq_ready": 4, "ms_ready": 4, "h_ready": 32, "z_lo": 34,
    "pe_act": 4, "pe_dve": 44, "act_pe": 5, "dve_pe": 42,
}
PER_ACT = {
    "hi_ready": 258, "units_begun": 258, "lin_ready": 120, "lin_evac": 120, "gu_ready": 44, "sg_ready": 44,
    "a_ready": 44, "a_hi": 44, "sq_ready": 4, "ms_ready": 4, "std_ready": 4, "h_scaled": 32,
    "h_hi": 32, "x_ready": 3, "z_hi": 34, "pe_act": 4, "act_dve": 44, "dve_act": 82,
    "act_pe": 5, "act_done": 11,
}
PER_DVE = {
    "hi_ready": 258, "lo_ready": 258, "lin_ready": 120, "lin_evac": 120, "sg_ready": 44, "a_ready": 44,
    "a_hi": 44, "a_lo": 44, "y_ready": 2, "std_ready": 4, "h_scaled": 32, "h_hi": 32,
    "h_ready": 32, "x_ready": 3, "z_hi": 34, "z_lo": 34, "pe_dve": 44, "act_dve": 44,
    "dve_act": 82, "dve_pe": 42, "dve_done": 185,
}
LAYER_PER = {"pe": PER_PE, "act": PER_ACT, "dve": PER_DVE}


def columns(names):
    at, out = 0, {}
    for name, n in names:
        out[name] = (at, n)
        at += n
    return out, at


V1, V1_N = columns([("c", DT), ("b_ada", N_ADA), ("g_ffn1", DT), ("g_mix", DT), ("g_q", QT), ("g_kv", KVT),
                    ("conv", CONVT * 4), ("g_out", 1), ("g_ffn2", DT), ("g_final", DT), ("final_norm", DT),
                    ("dt_bias", H), ("a_log", H)])
V2, V2_N = columns([("ffn1", DT), ("mix", DT), ("sc_conv", DT * 3), ("conv", CONVT * 4), ("conv_b", CONVT),
                    ("m_D", XT), ("m_norm", XT), ("ffn2", DT), ("ple", DT), ("dt_bias", SSM_H), ("A_log", SSM_H)])
C, C_N = columns([("ident", P), ("ones", P), ("cum64", P), ("all64", P)] + [(f"level{i}", P) for i in range(6)]
                 + [("cum", P), ("after", P), ("swap", P), ("cosT", T), ("sinT", T), ("cos", 64), ("sin", 64),
                    ("mask", 384)])


def constants():
    j, i = np.mgrid[0:P, 0:P]
    same = j // 64 == i // 64
    inv_freq = np.float32(10000.0) ** (-np.arange(0, ROPE, 2, dtype=np.float32) / np.float32(ROPE))
    ang = np.arange(T, dtype=np.float32)[:, None] * inv_freq[None, :]
    cos, sin = np.cos(ang), np.sin(ang)
    parts = {
        "ident": j == i, "ones": j >= 0, "cum64": same & (j <= i), "all64": same, "cum": j <= i, "after": j > i,
        "swap": (j ^ 32) == i,
        "cosT": np.tile(cos.T, (4, 1)), "sinT": np.tile(np.concatenate([-sin.T, sin.T]), (2, 1)),
        "cos": cos.reshape(2, P, 32).transpose(1, 0, 2).reshape(P, 64),
        "sin": sin.reshape(2, P, 32).transpose(1, 0, 2).reshape(P, 64),
    }
    for n in range(6):
        parts[f"level{n}"] = (j >> (n + 1) == i >> (n + 1)) & (i >> n & 1 == 1) & (j >> n & 1 == 0)
    q, k = np.arange(P)[:, None], np.arange(T)[None, :]
    parts["mask"] = np.concatenate([np.where((k[:, :P] // 64) <= q // 64, 0.0, -1e30),
                                    np.where((k // 64) <= (q + P) // 64, 0.0, -1e30)], 1)
    return np.concatenate([np.asarray(parts[n], np.float32).reshape(P, -1) for n in C], 1)


class Side:

    def __init__(self, sems, who):
        self.n = dict.fromkeys(sems, 0)
        self.turns = []
        self.new_unit = False
        self.who = who

    def value(self, name, back=0):
        v = self.n[name] - back
        assert v > 0, name
        for reg, per in self.turns:
            if per.get(name, 0):
                v = reg * per[name] + v
        return v

    def step(self, name, k=1):
        self.n[name] += k

    def next(self, name, k=1):
        self.step(name, k)
        return self.value(name)

    def up(self, name, k=1):
        self.step(name, k)
        return k

    @contextmanager
    def loop(self, eng, turns, per):
        with eng.Fori(0, turns) as reg:
            before = dict(self.n)
            self.turns.append((reg, per))
            yield reg
            self.turns.pop()
            got = {k: v - before[k] for k, v in self.n.items() if v != before[k]}
            assert got == per, got
        for k, v in per.items():
            self.n[k] = before[k] + v * turns


def build(nc, stream, x_in, consts, vec1, vec2, out):
    ctx = ExitStack()
    with ctx:
        def sb(name, n, dt=F32):
            return ctx.enter_context(nc.sbuf_tensor("sb_" + name, [P, n], dt))[:, :]

        def cut(ap, *dims):
            names = "abcd"[:len(dims)]
            return ap.rearrange(f"p ({' '.join(names)}) -> p {' '.join(names)}", **dict(zip(names, dims)))

        def bank(name):
            return ctx.enter_context(nc.psum_tensor(name, [P, 512], F32))[:, :]

        raw = cut(sb("raw", RING * U), RING, U)
        w_hi, w_lo = (cut(sb(n, RING * U, F32R), RING, U) for n in ("w_hi", "w_lo"))
        x = cut(sb("x", DT * T), DT, T)
        hh, hl = (cut(sb(n, DT * T, F32R), DT, T) for n in ("h_hi", "h_lo"))
        zh, zl = (cut(sb(n, XT * T, F32R), XT, T) for n in ("z_hi", "z_lo"))
        con, v1, v2 = sb("con", C_N), sb("v1", V1_N), sb("v2", LAYERS * V2_N)
        lv = sb("layer_vec", V2_N)
        sq, ht = sb("sq", DT * T), sb("ht", DT * T)
        std, rstd = sb("std", 512), sb("rstd", 512)
        sg = sb("silu_gate", 512)
        pad = cut(sb("pad", 2 * 259), 2, 259)
        padu = sb("padu", 258)
        conv = cut(sb("conv_out", 2 * T), 2, T)
        eps = sb("eps", 1)
        cs, ada, cc = sb("c_silu", DT), sb("ada", N_ADA), cut(sb("c_cut", 2 * DT, F32R), DT, 2)
        gsc = sb("gains", 5 * DT)
        ar = sb("arena", 18400)
        banks = [bank(f"bank{i}") for i in range(8)]
        Y, G, N = banks[0:4], banks[4:6], banks[6:8]

        def vec(table, where, name, i=0, n=None):
            at, size = where[name]
            return table[:, at + i:at + i + (size if n is None else n)]

        def cst(name, i=0, n=None):
            return vec(con, C, name, i, n)

        def bc(ap, n):
            return ap.unsqueeze(len(ap.shape)).broadcast_to([*ap.shape, n])

        def rep(ap, n):
            return ap.unsqueeze(1).broadcast_to([ap.shape[0], n, *ap.shape[1:]])

        sems = {}

        def sem(name):
            sems[name] = ctx.enter_context(nc.semaphore(name))
            return sems[name]

        loaded = sem("loaded")
        cleared = sem("cleared")
        hi_ready = sem("hi_ready")
        lo_ready = sem("lo_ready")
        units_begun = sem("units_begun")
        lin_ready = sem("lin_ready")
        lin_evac = sem("lin_evac")
        gu_ready = sem("gu_ready")
        sg_ready = sem("sg_ready")
        a_ready = sem("a_ready")
        a_hi = sem("a_hi")
        a_lo = sem("a_lo")
        y_ready = sem("y_ready")
        sq_ready = sem("sq_ready")
        ms_ready = sem("ms_ready")
        std_ready = sem("std_ready")
        h_scaled = sem("h_scaled")
        h_hi = sem("h_hi")
        h_ready = sem("h_ready")
        x_ready = sem("x_ready")
        z_hi = sem("z_hi")
        z_lo = sem("z_lo")
        pe_act = sem("pe_act")
        pe_dve = sem("pe_dve")
        act_dve = sem("act_dve")
        dve_act = sem("dve_act")
        act_pe = sem("act_pe")
        dve_pe = sem("dve_pe")
        act_done = sem("act_done")
        dve_done = sem("dve_done")
        result_ready = sem("result_ready")
        stored = sem("stored")
        raw_loaded = [ctx.enter_context(nc.semaphore(f"raw_loaded{i}")) for i in range(RING)]
        block = ctx.enter_context(nc.Block())
        pe, act, dve = nc.tensor, nc.scalar, nc.vector


        def split_act(S):
            u = S.n["hi_ready"]
            v = 16 * (u // RING + 1)
            for reg, per in S.turns:
                v = reg * (16 * per["hi_ready"] // RING) + v
            act.wait_ge(raw_loaded[u % RING], v)
            S.n["units_begun"] = u
            if u > 1:
                act.wait_ge(units_begun, S.value("units_begun", 1))
            act.activation(w_hi[:, u % RING, :], raw[:, u % RING, :], ACT.Copy).then_inc(hi_ready, S.up("hi_ready"))

        def split_dve(S):
            u = S.n["lo_ready"]
            dve.wait_ge(hi_ready, S.next("hi_ready"))
            dve.tensor_tensor(w_lo[:, u % RING, :], raw[:, u % RING, :],
                              w_hi[:, u % RING, :].bitcast(F32), ALU.subtract).then_inc(lo_ready, S.up("lo_ready"))

        def unit(S):
            pe.wait_ge(lo_ready, S.next("lo_ready"))
            S.new_unit = True
            return (S.n["lo_ready"] - 1) % RING

        def begun(S, ins):
            if S.new_unit:
                ins.then_inc(units_begun, S.up("units_begun"))
                S.new_unit = False

        def product(S, acc, slot, tile, hi, lo, start, stop):
            a, b = w_hi[:, slot, tile * P:(tile + 1) * P], w_lo[:, slot, tile * P:(tile + 1) * P]
            begun(S, pe.matmul(acc, a, hi, start=start, stop=False, skip_group_check=True))
            pe.matmul(acc, a, lo, start=False, stop=False, skip_group_check=True)
            return pe.matmul(acc, b, hi, start=False, stop=stop, skip_group_check=True)

        def turned(S, acc, slot, at, n, hi, lo, start, stop):
            a, b = w_hi[:, slot, at:at + n], w_lo[:, slot, at:at + n]
            begun(S, pe.matmul(acc, hi, a, start=start, stop=False, skip_group_check=True))
            pe.matmul(acc, lo, a, start=False, stop=False, skip_group_check=True)
            return pe.matmul(acc, hi, b, start=False, stop=stop, skip_group_check=True)

        def filler_pe(S, n):
            for _ in range(n):
                slot = unit(S)
                begun(S, pe.matmul(N[1][:, 0:2], w_hi[:, slot, 0:P], w_lo[:, slot, 0:2], start=True, stop=True,
                                      skip_group_check=True))

        def split(S, n=1):
            for _ in range(n):
                (split_act if "act" == S.who else split_dve)(S)


        def lin_pe(S, tiles, hi, lo, kt=DT, fresh=None):
            slot = 0
            for t in range(tiles):
                acc = Y[S.n["lin_ready"] % 3][:, 0:T]
                S.step("lin_evac")
                if S.n["lin_evac"] > 3:
                    pe.wait_ge(lin_evac, S.value("lin_evac", 3))
                for k in range(kt):
                    if (t * kt + k) % 8 == 0:
                        slot = unit(S)
                    if t == 0 and fresh:
                        pe.wait_ge(sems[fresh], S.next(fresh))
                    last = product(S, acc, slot, (t * kt + k) % 8, hi[:, k, :], lo[:, k, :], k == 0, k == kt - 1)
                last.then_inc(lin_ready, S.up("lin_ready"))

        def bank_of(S):
            return Y[(S.n["lin_ready"] - 1) % 3][:, 0:T]

        def lin_copy_tile(S, dst, t, kt):
            if S.who == "act":
                act.wait_ge(lin_ready, S.next("lin_ready"))
                act.activation(dst, bank_of(S), ACT.Copy).then_inc(lin_evac, S.up("lin_evac"))
            else:
                S.step("lin_ready")
                S.step("lin_evac")
            split(S, (t + 1) * kt // 8 - t * kt // 8)

        def lin_copy(S, dst, tiles, kt=DT):
            for t in range(tiles):
                lin_copy_tile(S, None if S.who == "dve" else dst[:, t, :], t, kt)


        def norm_act(S, src, nt, hi=None, shift=None):
            ins = act.activation(sq[:, 0:nt * T], src.rearrange("p a b -> p (a b)"), ACT.Square)
            ins.then_inc(sq_ready, S.up("sq_ready"))
            act.wait_ge(ms_ready, S.next("ms_ready"))
            ins = act.activation(std[:, 0:T], N[0][:, 0:T], ACT.Sqrt, bias=eps, scale=1.0 / (nt * P))
            ins.then_inc(std_ready, S.up("std_ready"))
            if hi is None:
                return
            for t in range(nt):
                act.wait_ge(h_scaled, S.next("h_scaled"))
                if shift is None:
                    act.activation(hi[:, t, :], ht[:, t * T:(t + 1) * T], ACT.Copy).then_inc(h_hi, S.up("h_hi"))
                else:
                    ins = act.activation(hi[:, t, :], ht[:, t * T:(t + 1) * T], ACT.Identity, bias=shift[:, t:t + 1])
                    ins.then_inc(h_hi, S.up("h_hi"))

        def norm_pe(S, nt):
            pe.wait_ge(sq_ready, S.next("sq_ready"))
            for t in range(nt):
                last = pe.matmul(N[0][:, 0:T], cst("ones"), sq[:, t * T:(t + 1) * T], start=t == 0, stop=t == nt - 1)
            last.then_inc(ms_ready, S.up("ms_ready"))

        def norm_dve(S, src, nt, g, hi=None, lo=None, shift=None, dst=None, done="h_scaled"):
            dve.wait_ge(std_ready, S.next("std_ready"))
            dve.reciprocal(rstd[:, 0:T], std[:, 0:T]).then_inc(dve_done, S.up("dve_done"))
            dve.wait_ge(dve_done, S.value("dve_done"))
            for t in range(nt):
                to = ht[:, t * T:(t + 1) * T] if dst is None else dst[:, t, :]
                last = dve.scalar_tensor_tensor(to, src[:, t, :], g[:, t:t + 1], rstd[:, 0:T], ALU.mult, ALU.mult)
                if hi is not None or t == nt - 1:
                    last.then_inc(sems[done], S.up(done))
            if hi is None:
                return
            for t in range(nt):
                dve.wait_ge(h_hi, S.next("h_hi"))
                h, a = ht[:, t * T:(t + 1) * T], hi[:, t, :].bitcast(F32)
                if shift is None:
                    dve.tensor_tensor(lo[:, t, :], h, a, ALU.subtract).then_inc(h_ready, S.up("h_ready"))
                else:
                    ins = dve.scalar_tensor_tensor(lo[:, t, :], h, shift[:, t:t + 1], a, ALU.add, ALU.subtract)
                    ins.then_inc(h_ready, S.up("h_ready"))


        sg_t, at_t = sg[:, 0:T], sg[:, T:2 * T]

        def gate_up_pe(S, par, first=False):
            S.step("a_ready")
            if S.n["a_ready"] > 2:
                pe.wait_ge(a_ready, S.value("a_ready", 2))
            for half in (0, 1):
                slot = unit(S)
                for k in range(DT):
                    if first and not half:
                        pe.wait_ge(h_ready, S.next("h_ready"))
                    last = product(S, G[par][:, half * T:(half + 1) * T], slot, k, hh[:, k, :], hl[:, k, :],
                                   k == 0, k == DT - 1)
            last.then_inc(gu_ready, S.up("gu_ready"))

        def down_pe(S, par, first=False, final=False):
            slot = unit(S)
            pe.wait_ge(a_lo, S.next("a_lo"))
            for o in range(DT):
                last = product(S, Y[o // 2][:, o % 2 * T:(o % 2 + 1) * T], slot, o, zh[:, par, :], zl[:, par, :],
                               first and o % 2 == 0, final)
            if final:
                last.then_inc(y_ready, S.up("y_ready"))

        PAIR = dict(hi_ready=6, lo_ready=6, units_begun=6, gu_ready=2, sg_ready=2, a_ready=2, a_hi=2, a_lo=2)

        def per(*names, **more):
            return {n: PAIR[n] for n in names} | more

        def ffn_pe(S):
            gate_up_pe(S, 0, True)
            gate_up_pe(S, 1)
            down_pe(S, 0, first=True)
            with S.loop(pe, FT // 2 - 1, per("lo_ready", "units_begun", "gu_ready", "a_ready", "a_lo")):
                for par in (0, 1):
                    gate_up_pe(S, par)
                    down_pe(S, 1 - par)
            down_pe(S, 1, final=True)

        def ffn_step_act(S, par, units=3):
            split(S, 2)
            act.wait_ge(gu_ready, S.next("gu_ready"))
            act.activation(sg_t, G[par][:, 0:T], ACT.Silu).then_inc(sg_ready, S.up("sg_ready"))
            split(S, units - 2)
            act.wait_ge(a_ready, S.next("a_ready"))
            act.activation(zh[:, par, :], at_t, ACT.Copy).then_inc(a_hi, S.up("a_hi"))

        def ffn_act(S):
            ffn_step_act(S, 0, 2)
            ffn_step_act(S, 1)
            with S.loop(act, FT // 2 - 1, per("hi_ready", "units_begun", "gu_ready", "sg_ready", "a_ready", "a_hi")):
                ffn_step_act(S, 0)
                ffn_step_act(S, 1)
            split(S)

        def ffn_step_dve(S, par, units=3):
            split(S, 2)
            dve.wait_ge(sg_ready, S.next("sg_ready"))
            if S.n["a_lo"]:
                dve.wait_ge(a_lo, S.value("a_lo"))
            dve.tensor_tensor(at_t, sg_t, G[par][:, T:2 * T], ALU.mult).then_inc(a_ready, S.up("a_ready"))
            dve.wait_ge(a_ready, S.value("a_ready"))
            split(S, units - 2)
            dve.wait_ge(a_hi, S.next("a_hi"))
            ins = dve.tensor_tensor(zl[:, par, :], at_t, zh[:, par, :].bitcast(F32), ALU.subtract)
            ins.then_inc(a_lo, S.up("a_lo"))

        def ffn_dve(S, scale):
            ffn_step_dve(S, 0, 2)
            ffn_step_dve(S, 1)
            with S.loop(dve, FT // 2 - 1, per("hi_ready", "lo_ready", "sg_ready", "a_ready", "a_hi", "a_lo")):
                ffn_step_dve(S, 0)
                ffn_step_dve(S, 1)
            split(S)
            dve.wait_ge(y_ready, S.next("y_ready"))
            for o in range(DT):
                s = scale if isinstance(scale, float) else scale[:, o:o + 1]
                last = dve.scalar_tensor_tensor(x[:, o, :], Y[o // 2][:, o % 2 * T:(o % 2 + 1) * T], s, x[:, o, :],
                                                  ALU.mult, ALU.add)
            last.then_inc(x_ready, S.up("x_ready"))

        def x_norm_act(S, hi=None, shift=None, after="x_ready"):
            if after == "x_ready":
                act.wait_ge(sems[after], S.next(after))
            else:
                act.wait_ge(sems[after], S.value(after))
            norm_act(S, x, DT, hi, shift)

        def x_norm_dve(S, g, hi=None, lo=None, shift=None, dst=None, after="x_ready", done="h_scaled"):
            dve.wait_ge(sems[after], S.value(after))
            norm_dve(S, x, DT, g, hi, lo, shift, dst, done)


        def ada_pe(S):
            pe.wait_ge(dve_pe, S.next("dve_pe"))
            with S.loop(pe, N_ADA // RING, dict(lo_ready=RING, units_begun=RING)) as turn:
                for s in range(RING):
                    slot = unit(S)
                    acc = N[1][:, bass.ds(turn * (2 * RING) + 2 * s, 2)]
                    for k in range(DT):
                        tile = slice(k * P, (k + 1) * P)
                        begun(S, pe.matmul(acc, w_hi[:, slot, tile], cc[:, k, :], start=k == 0, stop=False,
                                              skip_group_check=True))
                        last = pe.matmul(acc, w_lo[:, slot, tile], cc[:, k, :], start=False, stop=k == DT - 1,
                                            skip_group_check=True)
            pe.drain().then_inc(pe_dve, 1)
            S.step("pe_dve")

        def ada_act(S):
            act.activation(cs, vec(v1, V1, "c"), ACT.Silu).then_inc(act_done, S.up("act_done"))
            act.wait_ge(act_done, S.value("act_done"))
            act.activation(cc[:, :, 0], cs, ACT.Copy).then_inc(act_dve, S.up("act_dve"))
            with S.loop(act, N_ADA // RING, dict(hi_ready=RING, units_begun=RING)):
                split(S, RING)

        def ada_dve(S):
            dve.wait_ge(act_dve, S.next("act_dve"))
            dve.tensor_tensor(cc[:, :, 1], cs, cc[:, :, 0].bitcast(F32), ALU.subtract).then_inc(dve_pe, S.up("dve_pe"))
            with S.loop(dve, N_ADA // RING, dict(hi_ready=RING, lo_ready=RING)):
                split(S, RING)
            dve.wait_ge(pe_dve, S.next("pe_dve"))
            sums = N[1][:, 0:2 * N_ADA].rearrange("p (a b) -> p a b", b=2)
            dve.tensor_tensor(ada, sums[:, :, 0], vec(v1, V1, "b_ada"), ALU.add).then_inc(dve_done, S.up("dve_done"))
            dve.wait_ge(dve_done, S.value("dve_done"))
            dve.tensor_tensor(ada, ada, sums[:, :, 1], ALU.add).then_inc(dve_done, S.up("dve_done"))
            dve.wait_ge(dve_done, S.value("dve_done"))
            for n, g in enumerate(("g_ffn1", "g_mix", "g_ffn2")):
                dve.scalar_tensor_tensor(gsc[:, n * DT:(n + 1) * DT], ada[:, (3 * n + 1) * DT:(3 * n + 2) * DT], 1.0,
                                           vec(v1, V1, g), ALU.add, ALU.mult)
            dve.tensor_scalar(gsc[:, 3 * DT:4 * DT], ada[:, 2 * DT:3 * DT], 0.5, None, ALU.mult)
            ins = dve.tensor_scalar(gsc[:, 4 * DT:5 * DT], ada[:, 8 * DT:9 * DT], 0.5, None, ALU.mult)
            ins.then_inc(x_ready, S.up("x_ready"))
            dve.wait_ge(x_ready, S.value("x_ready"))

        shifts = [ada[:, 3 * n * DT:(3 * n + 1) * DT] for n in range(3)]
        gains = [gsc[:, n * DT:(n + 1) * DT] for n in range(3)]
        half_gate1, half_gate3 = gsc[:, 3 * DT:4 * DT], gsc[:, 4 * DT:5 * DT]
        gate2 = ada[:, 5 * DT:6 * DT]


        def hi_lo_act(S, t, src, after="dve_act"):
            act.wait_ge(sems[after], S.next(after))
            act.activation(zh[:, t, :], src, ACT.Copy).then_inc(z_hi, S.up("z_hi"))

        def lo_dve(S, t, src):
            dve.wait_ge(z_hi, S.next("z_hi"))
            dve.tensor_tensor(zl[:, t, :], src, zh[:, t, :].bitcast(F32), ALU.subtract).then_inc(z_lo, S.up("z_lo"))
            dve.wait_ge(z_lo, S.value("z_lo"))

        PER6 = dict(hi_ready=6, lo_ready=6, units_begun=6, lin_ready=6, lin_evac=6, act_dve=6, dve_act=6, dve_done=18)

        def six(*names):
            return {n: PER6[n] for n in names}

        def conv_act(S, dst, bias=None):
            with S.loop(act, CONVT // 6, six("hi_ready", "units_begun", "lin_ready", "lin_evac", "act_dve", "dve_act")) as turn:
                for k in range(6):
                    t = turn * 6 + k
                    act.wait_ge(lin_ready, S.next("lin_ready"))
                    act.activation(pad[:, k % 2, 3:], bank_of(S), ACT.Copy).then_inc(lin_evac, S.up("lin_evac"))
                    split(S)
                    act.wait_ge(dve_act, S.next("dve_act"))
                    b = 0.0 if bias is None else bias[:, bass.ds(t, 1)]
                    act.activation(dst[:, t, :], conv[:, k % 2, :], ACT.Silu, bias=b).then_inc(act_dve, S.up("act_dve"))

        def conv_dve(S, w):
            with S.loop(dve, CONVT // 6, six("hi_ready", "lo_ready", "lin_ready", "lin_evac", "act_dve", "dve_act", "dve_done")) as turn:
                for k in range(6):
                    t = turn * 6 + k
                    S.step("lin_ready")
                    dve.wait_ge(lin_evac, S.next("lin_evac"))
                    to, src = conv[:, k % 2, :], pad[:, k % 2, :]
                    ins = dve.tensor_scalar(to, src[:, 0:T], w[:, bass.ds(t * 4, 1)], None, ALU.mult)
                    ins.then_inc(dve_done, S.up("dve_done"))
                    dve.wait_ge(dve_done, S.value("dve_done"))
                    for j in (1, 2, 3):
                        signal = "dve_done" if j < 3 else "dve_act"
                        dve.scalar_tensor_tensor(to, src[:, j:j + T], w[:, bass.ds(t * 4 + j, 1)], to,
                                                 ALU.mult, ALU.add).then_inc(sems[signal], S.up(signal))
                        dve.wait_ge(sems[signal], S.value(signal))
                    split(S)
                    dve.wait_ge(act_dve, S.next("act_dve"))

        def lin_pe_turns(S, turns, hi, lo, fresh=None):
            lin_pe(S, 6, hi, lo, fresh=fresh)
            with S.loop(pe, turns - 1, dict(lo_ready=6, units_begun=6, lin_ready=6, lin_evac=6)):
                lin_pe(S, 6, hi, lo)

        def gates_act(S, ya, yb):
            for t in range(DT):
                for half in (0, 1):
                    act.wait_ge(lin_ready, S.next("lin_ready"))
                    act.activation(conv[:, half, :], bank_of(S), ACT.Sigmoid).then_inc(lin_evac, S.up("lin_evac"))
                    act.wait_ge(lin_evac, S.value("lin_evac"))
                    split(S)
                hi_lo_act(S, t, ya[:, t, :])

        def gates_dve(S, ya, yb):
            for t in range(DT):
                for half, y in enumerate((ya, yb)):
                    S.step("lin_ready")
                    dve.wait_ge(lin_evac, S.next("lin_evac"))
                    dve.tensor_tensor(y[:, t, :], y[:, t, :], conv[:, half, :], ALU.mult).then_inc(dve_done, S.up("dve_done"))
                    dve.wait_ge(dve_done, S.value("dve_done"))
                    split(S)
                dve.tensor_tensor(ya[:, t, :], ya[:, t, :], yb[:, t, :], ALU.add).then_inc(dve_act, S.up("dve_act"))
                dve.wait_ge(dve_act, S.value("dve_act"))
                lo_dve(S, t, ya[:, t, :])

        def add_act(S):
            for t in range(DT):
                S.step("lin_ready")
                S.step("lin_evac")
                split(S)

        def add_dve(S, scale=1.0):
            for t in range(DT):
                dve.wait_ge(lin_ready, S.next("lin_ready"))
                s = scale if isinstance(scale, float) else scale[:, t:t + 1]
                ins = dve.scalar_tensor_tensor(x[:, t, :], bank_of(S), s, x[:, t, :], ALU.mult, ALU.add)
                ins.then_inc(lin_evac, S.up("lin_evac"))
                dve.wait_ge(lin_evac, S.value("lin_evac"))
                split(S)


        def area(at, *dims):
            n = int(np.prod(dims))
            assert at + n <= 18400, (at, dims)
            return cut(ar[:, at:at + n], *dims) if len(dims) > 1 else ar[:, at:at + n]

        xs = area(0, CONVT, T)
        y_sc = area(6144, DT, T)
        xdt = area(8192, 2, SSM_H, 64)
        y_ssm = area(8192, DT, T)
        xe = cut(sq, SSM_H, 64)
        st = ht
        b_tok = area(12288, 4 * P)
        cb = area(12800, 2, 4, P)
        au = area(13824, 4, P)
        gg = area(14336, 2, 4, P)
        cd = area(15360, 4, P)
        d_t, dt_t, a_t, e_t = (area(15872 + 64 * i, 2, SSM_H) for i in range(4))
        acum = area(16128, 96)
        dte, ea = area(16224, SSM_H), area(16256, SSM_H)
        xs_tmp = area(16288, T)
        ya_tmp = area(16544, T)
        gate_ple = area(0, DT, T)
        ple_tmp = area(2048, T)

        def dt_pe(S):
            for half in (0, 1):
                for k in range(DT):
                    if not half:
                        if not k:
                            slot = unit(S)
                        pe.wait_ge(h_ready, S.next("h_ready"))
                    last = turned(S, N[1][:, half * SSM_H:(half + 1) * SSM_H], slot, k * SSM_H, SSM_H,
                                  hh[:, k, half * P:(half + 1) * P], hl[:, k, half * P:(half + 1) * P],
                                  k == 0, k == DT - 1)
            last.then_inc(pe_dve, S.up("pe_dve"))
            pe.wait_ge(dve_pe, S.next("dve_pe"))
            pe.matmul(N[0][:, 0:64], cst("cum"), a_t.rearrange("p a b -> p (a b)"), start=True, stop=True,
                         skip_group_check=True)
            pe.matmul(N[0][:, 64:96], cst("after"), a_t[:, 0, :], start=True, stop=True,
                      skip_group_check=True).then_inc(pe_dve, S.up("pe_dve"))

        def softplus_act(S, src, tmp):
            act.activation(tmp, src, ACT.Abs).then_inc(act_done, S.up("act_done"))
            act.wait_ge(act_done, S.value("act_done"))
            act.activation(tmp, tmp, ACT.Exp, scale=-1.0).then_inc(act_done, S.up("act_done"))
            act.wait_ge(act_done, S.value("act_done"))
            act.activation(tmp, tmp, ACT.Ln, bias=1.0).then_inc(act_done, S.up("act_done"))
            act.wait_ge(act_done, S.value("act_done"))

        def dt_act(S):
            split(S)
            act.wait_ge(dve_act, S.next("dve_act"))
            softplus_act(S, d_t, e_t)
            act.activation(ea, vec(lv, V2, "A_log"), ACT.Exp).then_inc(act_dve, S.up("act_dve"))
            act.wait_ge(dve_act, S.next("dve_act"))
            act.activation(dte, acum[:, 64:96], ACT.Exp).then_inc(act_dve, S.up("act_dve"))

        def dt_dve(S):
            split(S)
            dve.wait_ge(pe_dve, S.next("pe_dve"))
            ins = dve.tensor_tensor(d_t, cut(N[1][:, 0:64], 2, SSM_H), rep(vec(lv, V2, "dt_bias"), 2), ALU.add)
            ins.then_inc(dve_act, S.up("dve_act"))
            dve.wait_ge(dve_act, S.value("dve_act"))
            dve.wait_ge(act_dve, S.next("act_dve"))
            dve.scalar_tensor_tensor(dt_t, d_t, 0.0, e_t, ALU.max, ALU.add).then_inc(dve_done, S.up("dve_done"))
            dve.wait_ge(dve_done, S.value("dve_done"))
            dve.scalar_tensor_tensor(a_t, dt_t, -1.0, rep(ea, 2), ALU.mult, ALU.mult).then_inc(dve_pe, S.up("dve_pe"))
            dve.wait_ge(dve_pe, S.value("dve_pe"))
            dve.wait_ge(pe_dve, S.next("pe_dve"))
            dve.tensor_copy(acum, N[0][:, 0:96]).then_inc(dve_act, S.up("dve_act"))
            S.step("act_dve")

        SC = dict(hi_ready=6, lo_ready=6, units_begun=6, lin_ready=6, lin_evac=6, z_hi=2, z_lo=2, dve_done=6)

        def sc_act(S):
            with S.loop(act, DT // 2, {n: SC[n] for n in ("hi_ready", "units_begun", "lin_ready", "lin_evac", "z_hi")}) as turn:
                for k in (0, 1):
                    act.wait_ge(lin_ready, S.next("lin_ready"))
                    act.activation(xs_tmp, bank_of(S), ACT.Copy).then_inc(lin_evac, S.up("lin_evac"))
                    split(S)
                    S.step("lin_ready", 2)
                    S.step("lin_evac", 2)
                    split(S)
                    act.wait_ge(lin_evac, S.value("lin_evac"))
                    act.activation(zh[:, turn * 2 + k, :], ya_tmp, ACT.Copy).then_inc(z_hi, S.up("z_hi"))
                    split(S)

        def sc_dve(S):
            w = vec(lv, V2, "sc_conv")
            with S.loop(dve, DT // 2, {n: SC[n] for n in ("hi_ready", "lo_ready", "lin_ready", "lin_evac", "z_hi", "z_lo", "dve_done")}) as turn:
                for k in (0, 1):
                    t = turn * 2 + k
                    S.step("lin_ready")
                    dve.wait_ge(lin_evac, S.next("lin_evac"))
                    split(S)
                    dve.wait_ge(lin_ready, S.next("lin_ready"))
                    dve.tensor_tensor(padu[:, 2:], bank_of(S), xs_tmp, ALU.mult).then_inc(lin_evac, S.up("lin_evac"))
                    dve.wait_ge(lin_evac, S.value("lin_evac"))
                    split(S)
                    to = ple_conv
                    ins = dve.tensor_scalar(to, padu[:, 0:T], w[:, bass.ds(t * 3, 1)], None, ALU.mult)
                    ins.then_inc(dve_done, S.up("dve_done"))
                    dve.wait_ge(dve_done, S.value("dve_done"))
                    for j in (1, 2):
                        dve.scalar_tensor_tensor(to, padu[:, j:j + T], w[:, bass.ds(t * 3 + j, 1)], to,
                                                 ALU.mult, ALU.add).then_inc(dve_done, S.up("dve_done"))
                        dve.wait_ge(dve_done, S.value("dve_done"))
                    dve.wait_ge(lin_ready, S.next("lin_ready"))
                    dve.tensor_tensor(ya_tmp, bank_of(S), to, ALU.mult).then_inc(lin_evac, S.up("lin_evac"))
                    dve.wait_ge(lin_evac, S.value("lin_evac"))
                    split(S)
                    dve.wait_ge(z_hi, S.next("z_hi"))
                    ins = dve.tensor_tensor(zl[:, t, :], ya_tmp, zh[:, t, :].bitcast(F32), ALU.subtract)
                    ins.then_inc(z_lo, S.up("z_lo"))
                    dve.wait_ge(z_lo, S.value("z_lo"))

        ple_conv = conv[:, 0, :]

        def ssd_pe(S):
            n = 0
            for c in (0, 1):
                for q in range(XT // 4):
                    for i in range(4):
                        last = pe.transpose(Y[n % 4][:, i * P:(i + 1) * P], xs[:, 4 * q + i, c * P:(c + 1) * P],
                                               cst("ident"))
                    last.then_inc(pe_dve, S.up("pe_dve"))
                    n += 1
                    if n >= 4:
                        pe.wait_ge(dve_pe, S.next("dve_pe"))
            pe.wait_ge(dve_pe, S.next("dve_pe", 3))
            for g in range(SSM_G):
                last = pe.transpose(N[0][:, g * P:(g + 1) * P], xs[:, XT + g, 0:P], cst("ident"))
            last.then_inc(pe_act, S.up("pe_act"))
            for c in (0, 1):
                for g in range(SSM_G):
                    last = pe.matmul(G[c][:, g * P:(g + 1) * P], xs[:, XT + g, c * P:(c + 1) * P],
                                        xs[:, XT + SSM_G + g, c * P:(c + 1) * P], start=True, stop=True,
                                        skip_group_check=True)
                last.then_inc(pe_dve, S.up("pe_dve"))
            pe.wait_ge(act_pe, S.next("act_pe"))
            pe.wait_ge(dve_pe, S.next("dve_pe"))
            for g in range(SSM_G):
                last = pe.matmul(Y[g], b_tok[:, g * P:(g + 1) * P],
                                    xe.rearrange("p a b -> p (a b)")[:, g * 512:(g + 1) * 512], start=True, stop=True)
            last.then_inc(pe_act, S.up("pe_act"))
            pe.wait_ge(act_pe, S.next("act_pe"))
            for c in (0, 1):
                for q in range(SSM_H // 4):
                    pe.wait_ge(dve_pe, S.next("dve_pe"))
                    ins = pe.matmul(G[q % 2], cst("ones"), au.rearrange("p a b -> p (a b)"), start=True, stop=True)
                    ins.then_inc(pe_dve, S.up("pe_dve"))
                    pe.wait_ge(dve_pe, S.next("dve_pe"))
                    for i in range(4):
                        h, part = 4 * q + i, slice(i % 2 * 64, i % 2 * 64 + 64)
                        acc = N[q % 2][part, i // 2 * P:(i // 2 + 1) * P]
                        last = pe.matmul(acc, xdt[:, c, h, :], gg[:, q % 2, i, :], start=True, stop=c == 0,
                                            skip_group_check=True)
                        if c:
                            last = pe.matmul(acc, st[:, h * 64:(h + 1) * 64], cd[:, i, :], start=False, stop=True,
                                                skip_group_check=True)
                    last.then_inc(pe_dve, S.up("pe_dve"))

        def ssd_act(S):
            act.wait_ge(pe_act, S.next("pe_act"))
            act.activation(b_tok, N[0], ACT.Copy).then_inc(act_pe, S.up("act_pe"))
            act.wait_ge(pe_act, S.next("pe_act"))
            for g in range(SSM_G):
                last = act.activation(st[:, g * 512:(g + 1) * 512], Y[g], ACT.Copy)
            last.then_inc(act_pe, S.up("act_pe"))
            for c in (0, 1):
                for q in range(SSM_H // 4):
                    act.wait_ge(dve_act, S.next("dve_act"))
                    flat = gg[:, q % 2, :, :].rearrange("p a b -> p (a b)")
                    signal = "act_done" if c else "act_dve"
                    act.activation(flat, flat, ACT.Exp).then_inc(sems[signal], S.up(signal))
                    act.wait_ge(sems[signal], S.value(signal))
                    if c:
                        ins = act.activation(cd.rearrange("p a b -> p (a b)"), G[q % 2], ACT.Exp)
                        ins.then_inc(act_dve, S.up("act_dve"))
                        act.wait_ge(act_dve, S.value("act_dve"))

        def ssd_dve(S):
            n = 0
            for c in (0, 1):
                for q in range(XT // 4):
                    dve.wait_ge(pe_dve, S.next("pe_dve"))
                    dve.tensor_tensor(xdt[:, c, 8 * q:8 * q + 8, :], cut(Y[n % 4], 8, 64),
                                      bc(dt_t[:, c, 8 * q:8 * q + 8], 64), ALU.mult).then_inc(dve_pe, S.up("dve_pe"))
                    dve.wait_ge(dve_pe, S.value("dve_pe"))
                    n += 1
            dve.tensor_tensor(xe, xdt[:, 0, :, :], bc(dte, 64), ALU.mult).then_inc(dve_pe, S.up("dve_pe"))
            dve.wait_ge(dve_pe, S.value("dve_pe"))
            for c in (0, 1):
                dve.wait_ge(pe_dve, S.next("pe_dve"))
                ins = dve.tensor_tensor(cb[:, c, :, :], cut(G[c], 4, P), rep(cst("cum"), 4), ALU.mult)
                ins.then_inc(dve_done, S.up("dve_done"))
                dve.wait_ge(dve_done, S.value("dve_done"))
            for c in (0, 1):
                for q in range(SSM_H // 4):
                    heads = slice(4 * q, 4 * q + 4)
                    ins = dve.tensor_tensor(au, rep(cst("cum"), 4), bc(a_t[:, c, heads], P), ALU.mult)
                    ins.then_inc(dve_pe, S.up("dve_pe"))
                    dve.wait_ge(dve_pe, S.value("dve_pe"))
                    dve.wait_ge(pe_dve, S.next("pe_dve"))
                    g = gg[:, q % 2, :, :]
                    sums = acum[:, c * SSM_H + 4 * q:c * SSM_H + 4 * q + 4]
                    dve.tensor_tensor(g, cut(G[q % 2], 4, P), bc(sums, P), ALU.subtract).then_inc(dve_done, S.up("dve_done"))
                    dve.wait_ge(dve_done, S.value("dve_done"))
                    dve.tensor_scalar(g, g, 0.0, None, ALU.min).then_inc(dve_act, S.up("dve_act"))
                    dve.wait_ge(dve_act, S.value("dve_act"))
                    dve.wait_ge(act_dve, S.next("act_dve"))
                    grp = q // 2
                    if c:
                        ins = dve.tensor_tensor(cd, cd, rep(xs[:, XT + SSM_G + grp, P:T], 4), ALU.mult)
                        ins.then_inc(dve_done, S.up("dve_done"))
                        dve.wait_ge(dve_done, S.value("dve_done"))
                    dve.tensor_tensor(g, g, rep(cb[:, c, grp, :], 4), ALU.mult).then_inc(dve_pe, S.up("dve_pe"))
                    dve.wait_ge(dve_pe, S.value("dve_pe"))
                    dve.wait_ge(pe_dve, S.next("pe_dve"))
                    for i in (0, 1):
                        t = 2 * q + i
                        part = xs[:, t, c * P:(c + 1) * P]
                        ins = dve.scalar_tensor_tensor(part, part, vec(lv, V2, "m_D", t, 1),
                                                       N[q % 2][:, i * P:(i + 1) * P], ALU.mult, ALU.add)
                        ins.then_inc(dve_done, S.up("dve_done"))
                        dve.wait_ge(dve_done, S.value("dve_done"))

        def z_act(S):
            for t in range(XT):
                act.wait_ge(lin_ready, S.next("lin_ready"))
                act.activation(conv[:, t % 2, :], bank_of(S), ACT.Silu).then_inc(lin_evac, S.up("lin_evac"))
                split(S)
                act.wait_ge(dve_act, S.next("dve_act"))
            for half in (0, 1):
                ins = act.activation(sq, xs[:, half * 8:half * 8 + 8, :].rearrange("p a b -> p (a b)"), ACT.Square)
                ins.then_inc(act_pe, S.up("act_pe"))
                act.wait_ge(pe_act, S.next("pe_act"))
                act.activation(std, N[half], ACT.Sqrt, bias=eps, scale=1.0 / 512).then_inc(act_dve, S.up("act_dve"))
                for t in range(half * 8, half * 8 + 8):
                    act.wait_ge(dve_act, S.next("dve_act"))
                    act.activation(zh[:, t, :], xs[:, t, :], ACT.Copy).then_inc(z_hi, S.up("z_hi"))

        def z_dve(S):
            for t in range(XT):
                S.step("lin_ready")
                dve.wait_ge(lin_evac, S.next("lin_evac"))
                ins = dve.tensor_tensor(xs[:, t, :], xs[:, t, :], conv[:, t % 2, :], ALU.mult)
                ins.then_inc(dve_act, S.up("dve_act"))
                dve.wait_ge(dve_act, S.value("dve_act"))
                split(S)
            for half in (0, 1):
                dve.wait_ge(act_dve, S.next("act_dve"))
                dve.reciprocal(rstd, std).then_inc(dve_done, S.up("dve_done"))
                dve.wait_ge(dve_done, S.value("dve_done"))
                for t in range(half * 8, half * 8 + 8):
                    r = rstd[:, t % 8 // 4 * T:(t % 8 // 4 + 1) * T]
                    dve.scalar_tensor_tensor(xs[:, t, :], xs[:, t, :], vec(lv, V2, "m_norm", t, 1), r,
                                             ALU.mult, ALU.mult).then_inc(dve_act, S.up("dve_act"))
                    dve.wait_ge(dve_act, S.value("dve_act"))
                for t in range(half * 8, half * 8 + 8):
                    dve.wait_ge(z_hi, S.next("z_hi"))
                    ins = dve.tensor_tensor(zl[:, t, :], xs[:, t, :], zh[:, t, :].bitcast(F32), ALU.subtract)
                    ins.then_inc(z_lo, S.up("z_lo"))
                    dve.wait_ge(z_lo, S.value("z_lo"))

        def z_pe(S):
            lin_pe(S, XT, hh, hl)
            for half in (0, 1):
                pe.wait_ge(act_pe, S.next("act_pe"))
                for g in (0, 1):
                    for i in range(4):
                        k = g * 4 + i
                        last = pe.matmul(N[half][:, g * T:(g + 1) * T], cst("ones"), sq[:, k * T:(k + 1) * T],
                                            start=i == 0, stop=i == 3, skip_group_check=True)
                last.then_inc(pe_act, S.up("pe_act"))

        def layer_mixer_pe(S):
            norm_pe(S, DT)
            dt_pe(S)
            lin_pe_turns(S, 4, hh, hl)
            lin_pe(S, DT, zh, zl, fresh="z_lo")
            lin_pe_turns(S, 4, hh, hl)
            pe.wait_ge(act_pe, S.next("act_pe"))
            ssd_pe(S)
            z_pe(S)
            lin_pe(S, DT, zh, zl, kt=XT, fresh="z_lo")
            lin_pe(S, 2 * DT, hh, hl)
            lin_pe(S, DT, zh, zl, fresh="z_lo")

        def layer_mixer_act(S):
            x_norm_act(S, hh)
            dt_act(S)
            sc_act(S)
            lin_copy(S, y_sc, DT)
            conv_act(S, xs, vec(lv, V2, "conv_b"))
            act.drain().then_inc(act_pe, S.up("act_pe"))
            ssd_act(S)
            z_act(S)
            lin_copy(S, y_ssm, DT, kt=XT)
            gates_act(S, y_sc, y_ssm)
            add_act(S)

        def layer_mixer_dve(S):
            x_norm_dve(S, vec(lv, V2, "mix"), hh, hl)
            dt_dve(S)
            sc_dve(S)
            lin_copy(S, y_sc, DT)
            conv_dve(S, vec(lv, V2, "conv"))
            ssd_dve(S)
            z_dve(S)
            lin_copy(S, y_ssm, DT, kt=XT)
            gates_dve(S, y_sc, y_ssm)
            add_dve(S)


        def ple_pe(S):
            norm_pe(S, DT)
            filler_pe(S, 1)
            pe.wait_ge(z_lo, S.next("z_lo", 2))
            lin_pe(S, DT, hh, hl, fresh="h_ready")
            lin_pe(S, DT, zh[:, 8:10, :], zl[:, 8:10, :], kt=2)
            filler_pe(S, LAYER_PAD)

        def ple_act(S):
            slot = (S.n["hi_ready"] - AHEAD) % RING
            act.wait_ge(hi_ready, S.value("hi_ready", AHEAD - 1))
            for k in (0, 1):
                ins = act.activation(zh[:, 8 + k, :], w_hi[:, slot, k * T:(k + 1) * T].bitcast(F32), ACT.Copy)
                ins.then_inc(z_hi, S.up("z_hi"))
            split(S)
            for t in range(DT):
                act.wait_ge(lin_ready, S.next("lin_ready"))
                act.activation(gate_ple[:, t, :], bank_of(S), ACT.Sigmoid).then_inc(lin_evac, S.up("lin_evac"))
                split(S)
            for t in range(DT):
                S.step("lin_ready")
                S.step("lin_evac")
                split(S, 2 * (t + 1) // 8 - 2 * t // 8)
            split(S, LAYER_PAD)

        def ple_dve(S):
            slot = (S.n["lo_ready"] - AHEAD) % RING
            dve.wait_ge(lo_ready, S.value("lo_ready", AHEAD - 1))
            for k in (0, 1):
                dve.wait_ge(z_hi, S.next("z_hi"))
                ins = dve.tensor_copy(zl[:, 8 + k, :], w_lo[:, slot, k * T:(k + 1) * T].bitcast(F32))
                ins.then_inc(z_lo, S.up("z_lo"))
            split(S)
            for t in range(DT):
                S.step("lin_ready")
                S.step("lin_evac")
                split(S)
            dve.wait_ge(lin_evac, S.value("lin_evac"))
            for t in range(DT):
                dve.wait_ge(lin_ready, S.next("lin_ready"))
                S.step("lin_evac")
                dve.tensor_tensor(ple_tmp, bank_of(S), gate_ple[:, t, :], ALU.mult).then_inc(lin_evac, 1)
                dve.wait_ge(lin_evac, S.value("lin_evac"))
                signal = "dve_done" if t < DT - 1 else "x_ready"
                dve.tensor_tensor(x[:, t, :], x[:, t, :], ple_tmp, ALU.add).then_inc(sems[signal], S.up(signal))
                dve.wait_ge(sems[signal], S.value(signal))
                split(S, 2 * (t + 1) // 8 - 2 * t // 8)
            split(S, LAYER_PAD)


        y_mla = area(0, DT, T)
        lat = area(2048, QT + KVT, T)
        qn = area(4096, H, T)
        qr = area(6144, H // 2, T)
        kn = area(7168, H, T)
        val = area(9216, 2, D)
        ss, pb, pt = (area(11264 + 768 * i, 2, 384) for i in range(3))
        kr2, krT = area(13568, 2, P), area(13824, T)
        rope_a, rope_b = area(14080, 512), area(14592, 512)
        small = area(18000, 2, SMALL1)
        nm, rs = area(18160, 2, 2), area(18164, 2, 2)
        SCALE = float(P + ROPE) ** -0.5

        def small_pe(S):
            for half in (0, 1):
                for k in range(DT):
                    if not half:
                        if not k:
                            slot = unit(S)
                        pe.wait_ge(h_ready, S.next("h_ready"))
                    last = turned(S, N[1][:, half * SMALL1:(half + 1) * SMALL1], slot, k * SMALL1, SMALL1,
                                  hh[:, k, half * P:(half + 1) * P], hl[:, k, half * P:(half + 1) * P],
                                  k == 0, k == DT - 1)
            last.then_inc(pe_dve, S.up("pe_dve"))
            pe.wait_ge(dve_pe, S.next("dve_pe"))
            for c in (0, 1):
                last = pe.transpose(N[0][:, c * P:(c + 1) * P], kr2[:, c, :], cst("ident"))
            last.then_inc(pe_dve, S.up("pe_dve"))

        def small_dve(S):
            split(S)
            dve.wait_ge(pe_dve, S.next("pe_dve"))
            dve.tensor_copy(small, cut(N[1][:, 0:2 * SMALL1], 2, SMALL1)).then_inc(dve_done, S.up("dve_done"))
            dve.wait_ge(dve_done, S.value("dve_done"))
            k1, k2 = small[:, :, 0:32], small[:, :, 32:64]
            cos, sin = cut(cst("cos"), 2, 32), cut(cst("sin"), 2, 32)
            a, b = cut(rope_a[:, 0:64], 2, 32), cut(rope_b[:, 0:64], 2, 32)
            for to, u, v, op in ((kr2[:, :, 0:32], k1, k2, ALU.subtract), (kr2[:, :, 32:64], k2, k1, ALU.add)):
                dve.tensor_tensor(a, u, cos, ALU.mult).then_inc(dve_done, S.up("dve_done"))
                dve.wait_ge(dve_done, S.value("dve_done"))
                dve.tensor_tensor(b, v, sin, ALU.mult).then_inc(dve_done, S.up("dve_done"))
                dve.wait_ge(dve_done, S.value("dve_done"))
                dve.tensor_tensor(to, a, b, op).then_inc(dve_done, S.up("dve_done"))
                dve.wait_ge(dve_done, S.value("dve_done"))
            dve.tensor_copy(kr2[:, :, 64:128], kr2[:, :, 0:64]).then_inc(dve_pe, S.up("dve_pe"))
            dve.wait_ge(dve_pe, S.value("dve_pe"))
            dve.wait_ge(pe_dve, S.next("pe_dve"))
            dve.tensor_copy(krT, N[0][:, 0:T]).then_inc(dve_pe, S.up("dve_pe"))
            dve.wait_ge(dve_pe, S.value("dve_pe"))

        def values_pe(S):
            for k in (0, 1):
                slot = unit(S)
                for c in (0, 1):
                    for half in (0, 1):
                        last = turned(S, (G[0], G[1], N[0], N[1])[2 * c + half], slot, half * 512, 512,
                                      zh[:, QT + k, c * P:(c + 1) * P], zl[:, QT + k, c * P:(c + 1) * P],
                                      k == 0, k == 1)
            last.then_inc(pe_act, S.up("pe_act"))

        def values_act(S):
            act.wait_ge(pe_act, S.next("pe_act"))
            for c in (0, 1):
                for half in (0, 1):
                    last = act.activation(val[:, c, half * 512:(half + 1) * 512], (G[0], G[1], N[0], N[1])[2 * c + half],
                                            ACT.Copy)
            last.then_inc(act_pe, S.up("act_pe"))
            split(S, 2)

        def rope_pe(S):
            pe.wait_ge(act_pe, S.next("act_pe"))
            for m in range(4):
                last = pe.matmul(G[m // 2][:, m % 2 * T:(m % 2 + 1) * T], cst("swap"), qr[:, m, :], start=True,
                                    stop=True, skip_group_check=True)
            last.then_inc(pe_dve, S.up("pe_dve"))

        def rope_dve(S):
            dve.wait_ge(pe_dve, S.next("pe_dve"))
            for m in (0, 1):
                q = qr[:, 2 * m:2 * m + 2, :]
                dve.tensor_tensor(cut(rope_a, 2, T), q, rep(cst("cosT"), 2), ALU.mult).then_inc(dve_done, S.up("dve_done"))
                dve.wait_ge(dve_done, S.value("dve_done"))
                ins = dve.tensor_tensor(cut(rope_b, 2, T), cut(G[m], 2, T), rep(cst("sinT"), 2), ALU.mult)
                ins.then_inc(dve_done, S.up("dve_done"))
                dve.wait_ge(dve_done, S.value("dve_done"))
                signal = "dve_done" if not m else "dve_pe"
                dve.tensor_tensor(q, cut(rope_a, 2, T), cut(rope_b, 2, T), ALU.add).then_inc(sems[signal], S.up(signal))
                dve.wait_ge(sems[signal], S.value(signal))

        def scores_pe(S, h):
            part = slice(h % 2 * 64, h % 2 * 64 + 64)
            for c, at, n in ((0, 0, P), (1, P, T)):
                acc, tok = G[h % 2][:, at:at + n], slice(c * P, (c + 1) * P)
                pe.matmul(acc, qn[:, h, tok], kn[:, h, 0:n], start=True, stop=False, skip_group_check=True)
                last = pe.matmul(acc, qr[part, h // 2, tok], krT[part, 0:n], start=False, stop=True,
                                    skip_group_check=True)
            last.then_inc(pe_dve, S.up("pe_dve"))

        def attention_pe(S):
            pe.wait_ge(dve_pe, S.next("dve_pe"))
            scores_pe(S, 0)
            for h in range(H):
                if h == 0:
                    scores_pe(S, 1)
                    pe.wait_ge(dve_pe, S.next("dve_pe"))
                elif h + 1 < H:
                    scores_pe(S, h + 1)
                pe.wait_ge(dve_pe, S.next("dve_pe", 2 if h + 1 < H else 1))
                for i in range(3):
                    last = pe.transpose(N[h % 2][:, i * P:(i + 1) * P], pb[:, h % 2, i * P:(i + 1) * P], cst("ident"))
                last.then_inc(pe_act, S.up("pe_act"))
                pe.wait_ge(act_pe, S.next("act_pe"))
                v = [val[:, c, h * P:(h + 1) * P] for c in (0, 1)]
                p = [pt[:, h % 2, i * P:(i + 1) * P] for i in range(3)]
                if h >= 2:
                    pe.wait_ge(z_lo, S.value("z_lo", -(h - 1)))
                pe.matmul(Y[h % 2][:, 0:P], v[0], p[0], start=True, stop=True, skip_group_check=True)
                pe.matmul(Y[h % 2][:, P:T], v[0], p[1], start=True, stop=False, skip_group_check=True)
                ins = pe.matmul(Y[h % 2][:, P:T], v[1], p[2], start=False, stop=True, skip_group_check=True)
                ins.then_inc(pe_act, S.up("pe_act"))

        def exp_act(S, h):
            act.wait_ge(dve_act, S.next("dve_act"))
            act.activation(pb[:, h % 2, 0:P], ss[:, h % 2, 0:P], ACT.Exp, bias=nm[:, h % 2, 0:1],
                             accum_out=rs[:, h % 2, 0:1])
            act.activation(pb[:, h % 2, P:], ss[:, h % 2, P:], ACT.Exp, bias=nm[:, h % 2, 1:2],
                           accum_out=rs[:, h % 2, 1:2]).then_inc(act_dve, S.up("act_dve"))
            act.wait_ge(act_dve, S.value("act_dve"))

        def attention_act(S):
            exp_act(S, 0)
            for h in range(H):
                if h + 1 < H:
                    exp_act(S, h + 1)
                act.wait_ge(pe_act, S.next("pe_act"))
                act.activation(pt[:, h % 2, :], N[h % 2][:, 0:384], ACT.Copy).then_inc(act_pe, S.up("act_pe"))
                act.wait_ge(act_pe, S.value("act_pe"))
                act.wait_ge(pe_act, S.next("pe_act"))
                act.activation(zh[:, h, :], Y[h % 2][:, 0:T], ACT.Copy).then_inc(z_hi, S.up("z_hi"))

        def scale_dve(S, h):
            dve.wait_ge(pe_dve, S.next("pe_dve"))
            s = ss[:, h % 2, :]
            ins = dve.scalar_tensor_tensor(s, G[h % 2][:, 0:384], SCALE, cst("mask"), ALU.mult, ALU.add)
            ins.then_inc(dve_pe, S.up("dve_pe"))
            dve.wait_ge(dve_pe, S.value("dve_pe"))
            dve.tensor_reduce(nm[:, h % 2, 0:1], s[:, 0:P], AX.X, ALU.max, negate=True).then_inc(dve_done, S.up("dve_done"))
            dve.wait_ge(dve_done, S.value("dve_done"))
            ins = dve.tensor_reduce(nm[:, h % 2, 1:2], s[:, P:], AX.X, ALU.max, negate=True)
            ins.then_inc(dve_act, S.up("dve_act"))
            dve.wait_ge(dve_act, S.value("dve_act"))

        def probs_dve(S, h):
            dve.wait_ge(act_dve, S.next("act_dve"))
            r = rs[:, h % 2, :]
            dve.reciprocal(r, r).then_inc(dve_done, S.up("dve_done"))
            dve.wait_ge(dve_done, S.value("dve_done"))
            ins = dve.tensor_scalar(pb[:, h % 2, 0:P], pb[:, h % 2, 0:P], r[:, 0:1], None, ALU.mult)
            ins.then_inc(dve_done, S.up("dve_done"))
            dve.wait_ge(dve_done, S.value("dve_done"))
            ins = dve.tensor_scalar(pb[:, h % 2, P:], pb[:, h % 2, P:], r[:, 1:2], None, ALU.mult)
            ins.then_inc(dve_pe, S.up("dve_pe"))
            dve.wait_ge(dve_pe, S.value("dve_pe"))

        def attention_dve(S):
            scale_dve(S, 0)
            for h in range(H):
                if h + 1 < H:
                    scale_dve(S, h + 1)
                probs_dve(S, h)
                if h >= 1:
                    lo_dve(S, h - 1, Y[(h - 1) % 2][:, 0:T])
            lo_dve(S, H - 1, Y[(H - 1) % 2][:, 0:T])


        gt = area(2048, CONVT, T)
        at_ = area(8192, 16, P)
        uu, tt = area(10240, 16, P), area(12288, 16, P)
        kd = area(14336, 16, P)
        attn = cut(ht, 16, P)
        diag = cut(sq, 4, 4, P)
        tmp = [area(16384 + 512 * i, 4, P) for i in range(3)]
        lt = cut(sg, 4, P)
        er = cut(std, 4, P)
        state = area(16384, H, P)
        vn = cut(sq[:, 0:1024], H, P)
        o_t = area(8192, H, T)
        gs = [area(17920 + 16 * i, 16) for i in range(5)]
        g_t, beta_t, rkb, rq, sp_t = gs
        r_qk = area(18168, 2, 16)
        dec = area(18200, 2, 16)
        kbs, kds = area(18232, 16), area(18248, 16)
        cdk = area(18264, 16, 2)
        ea1 = area(18296, H)

        def block_of(c):
            return slice(c * 64, c * 64 + 64)

        def gdn_small_pe(S):
            pe.wait_ge(act_pe, S.next("act_pe"))
            for part in (0, 1):
                for i in range(16):
                    last = pe.matmul(N[0][:, part * 16 + i:part * 16 + i + 1], sq[:, i * P:(i + 1) * P],
                                        cst("ones", 0, 1), start=True, stop=True, skip_group_check=True)
                last.then_inc(pe_act, S.up("pe_act"))
                if not part:
                    pe.wait_ge(act_pe, S.next("act_pe"))
            pe.wait_ge(dve_pe, S.next("dve_pe"))
            pe.matmul(N[1][:, 0:16], cst("cum64"), g_t, start=True, stop=True, skip_group_check=True)
            ins = pe.matmul(N[1][:, 16:32], cst("all64"), g_t, start=True, stop=True, skip_group_check=True)
            ins.then_inc(pe_dve, S.up("pe_dve"))

        def gdn_small_act(S):
            for part in (0, 1):
                ins = act.activation(sq, gt[:, part * 8:part * 8 + 8, :].rearrange("p a b -> p (a b)"), ACT.Square)
                ins.then_inc(act_pe, S.up("act_pe"))
                act.wait_ge(pe_act, S.next("pe_act"))
            ins = act.activation(r_qk.rearrange("p a b -> p (a b)"), N[0][:, 0:32], ACT.Sqrt, bias=eps)
            ins.then_inc(act_done, S.up("act_done"))
            act.wait_ge(act_done, S.value("act_done"))
            ins = act.activation(cut(beta_t, H, 2), small[:, :, 72:80].rearrange("p t h -> p h t"), ACT.Sigmoid)
            ins.then_inc(act_done, S.up("act_done"))
            act.wait_ge(act_done, S.value("act_done"))
            act.wait_ge(dve_act, S.next("dve_act"))
            softplus_act(S, sp_t, dec[:, 0, :])
            act.activation(ea1, vec(v1, V1, "a_log"), ACT.Exp).then_inc(act_dve, S.up("act_dve"))
            act.wait_ge(dve_act, S.next("dve_act"))
            act.activation(dec, dec, ACT.Exp).then_inc(act_dve, S.up("act_dve"))

        def gdn_small_dve(S):
            dve.tensor_tensor(cut(sp_t, H, 2), small[:, :, 64:72].rearrange("p t h -> p h t"),
                              bc(vec(v1, V1, "dt_bias"), 2), ALU.add).then_inc(dve_act, S.up("dve_act"))
            dve.wait_ge(dve_act, S.value("dve_act"))
            dve.wait_ge(act_dve, S.next("act_dve"))
            dve.scalar_tensor_tensor(g_t, sp_t, 0.0, dec[:, 0, :], ALU.max, ALU.add).then_inc(dve_done, S.up("dve_done"))
            dve.wait_ge(dve_done, S.value("dve_done"))
            ins = dve.scalar_tensor_tensor(cut(g_t, H, 2), cut(g_t, H, 2), -1.0, bc(ea1, 2), ALU.mult, ALU.mult)
            ins.then_inc(dve_pe, S.up("dve_pe"))
            dve.wait_ge(dve_pe, S.value("dve_pe"))
            dve.reciprocal(r_qk, r_qk).then_inc(dve_done, S.up("dve_done"))
            dve.wait_ge(dve_done, S.value("dve_done"))
            rk = r_qk[:, 1, :]
            dve.tensor_scalar(rq, r_qk[:, 0, :], float(P) ** -0.5, None, ALU.mult).then_inc(dve_done, S.up("dve_done"))
            dve.wait_ge(dve_done, S.value("dve_done"))
            dve.tensor_tensor(rkb, rk, beta_t, ALU.mult).then_inc(dve_done, S.up("dve_done"))
            dve.wait_ge(dve_done, S.value("dve_done"))
            dve.wait_ge(pe_dve, S.next("pe_dve"))
            dve.tensor_copy(sp_t, N[1][:, 0:16]).then_inc(dve_done, S.up("dve_done"))
            dve.wait_ge(dve_done, S.value("dve_done"))
            dve.tensor_copy(dec[:, 0, :], sp_t).then_inc(dve_done, S.up("dve_done"))
            dve.wait_ge(dve_done, S.value("dve_done"))
            dve.tensor_tensor(dec[:, 1, :], N[1][:, 16:32], sp_t, ALU.subtract).then_inc(dve_act, S.up("dve_act"))
            dve.wait_ge(dve_act, S.value("dve_act"))
            dve.wait_ge(act_dve, S.next("act_dve"))
            dve.tensor_tensor(kbs, rkb, dec[:, 0, :], ALU.mult).then_inc(dve_done, S.up("dve_done"))
            dve.wait_ge(dve_done, S.value("dve_done"))
            dve.tensor_tensor(kds, rk, dec[:, 1, :], ALU.mult).then_inc(dve_done, S.up("dve_done"))
            dve.wait_ge(dve_done, S.value("dve_done"))

        def gdn_gram_pe(S):
            for p in range(4):
                pe.wait_ge(dve_pe, S.next("dve_pe"))
                for i in range(4):
                    last = pe.matmul(Y[i], cst("ones"), diag[:, i, :, :].rearrange("p a b -> p (a b)"), start=True,
                                        stop=True)
                last.then_inc(pe_dve, S.up("pe_dve"))
                pe.wait_ge(dve_pe, S.next("dve_pe"))
                for m in (0, 1):
                    for i in range(4):
                        last = pe.matmul(G[m][:, i * P:(i + 1) * P], tmp[1][:, i, :], tmp[2 if m == 0 else 0][:, i, :],
                                            start=True, stop=True, skip_group_check=True)
                for m in (0, 1):
                    for i in range(4):
                        h, c = 2 * p + i // 2, i % 2
                        last = pe.transpose(N[m][:, i * P:(i + 1) * P], gt[:, (m + 1) * H + h, c * P:(c + 1) * P],
                                               cst("ident"))
                last.then_inc(pe_dve, S.up("pe_dve"))

        def gdn_gram_act(S):
            for p in range(4):
                act.wait_ge(dve_act, S.next("dve_act"))
                act.activation(lt, lt, ACT.Exp).then_inc(act_done, S.up("act_done"))
                act.wait_ge(act_done, S.value("act_done"))
                act.activation(er.rearrange("p a b -> p (a b)"), Y[3], ACT.Exp).then_inc(act_dve, S.up("act_dve"))
                act.wait_ge(act_dve, S.value("act_dve"))

        def gdn_gram_dve(S):
            qn_, kn_, kb_ = tmp
            for p in range(4):
                of = slice(4 * p, 4 * p + 4)
                two = lambda m: gt[:, m * H + 2 * p:m * H + 2 * p + 2, :].rearrange("p a (b c) -> p (a b) c", b=2)
                for i, (m, v) in enumerate((("ident", rq), ("ident", r_qk[:, 1, :]), ("ident", rkb), ("cum64", g_t))):
                    signal = "dve_done" if i < 3 else "dve_pe"
                    ins = dve.tensor_tensor(diag[:, i, :, :], rep(cst(m), 4), bc(v[:, of], P), ALU.mult)
                    ins.then_inc(sems[signal], S.up(signal))
                    dve.wait_ge(sems[signal], S.value(signal))
                dve.wait_ge(pe_dve, S.next("pe_dve"))
                dve.tensor_tensor(qn_, two(0), cut(Y[0], 4, P), ALU.mult).then_inc(dve_done, S.up("dve_done"))
                dve.wait_ge(dve_done, S.value("dve_done"))
                dve.tensor_tensor(kn_, two(1), cut(Y[1], 4, P), ALU.mult).then_inc(dve_done, S.up("dve_done"))
                dve.wait_ge(dve_done, S.value("dve_done"))
                dve.tensor_tensor(kb_, two(1), cut(Y[2], 4, P), ALU.mult).then_inc(dve_pe, S.up("dve_pe"))
                dve.wait_ge(dve_pe, S.value("dve_pe"))
                dve.tensor_tensor(lt, cut(Y[3], 4, P), bc(sp_t[:, of], P), ALU.subtract).then_inc(dve_done, S.up("dve_done"))
                dve.wait_ge(dve_done, S.value("dve_done"))
                dve.tensor_scalar(lt, lt, 0.0, None, ALU.min).then_inc(dve_act, S.up("dve_act"))
                dve.wait_ge(dve_act, S.value("dve_act"))
                dve.wait_ge(act_dve, S.next("act_dve"))
                dve.tensor_tensor(lt, lt, rep(cst("cum64"), 4), ALU.mult).then_inc(dve_done, S.up("dve_done"))
                dve.wait_ge(dve_done, S.value("dve_done"))
                dve.tensor_copy(cdk[:, of, :], er[:, :, 63:P:64]).then_inc(dve_done, S.up("dve_done"))
                dve.wait_ge(dve_done, S.value("dve_done"))
                dve.wait_ge(pe_dve, S.next("pe_dve"))
                dve.tensor_tensor(two(0), qn_, er, ALU.mult).then_inc(dve_done, S.up("dve_done"))
                dve.wait_ge(dve_done, S.value("dve_done"))
                dve.tensor_tensor(at_[:, of, :], cut(G[0], 4, P), lt, ALU.mult).then_inc(dve_done, S.up("dve_done"))
                dve.wait_ge(dve_done, S.value("dve_done"))
                dve.tensor_tensor(attn[:, of, :], cut(G[1], 4, P), lt, ALU.mult).then_inc(dve_done, S.up("dve_done"))
                dve.wait_ge(dve_done, S.value("dve_done"))
                dve.tensor_tensor(kd[:, of, :], cut(N[0], 4, P), bc(kds[:, of], P), ALU.mult).then_inc(dve_done, S.up("dve_done"))
                dve.wait_ge(dve_done, S.value("dve_done"))
                dve.tensor_tensor(two(1), cut(N[0], 4, P), bc(kbs[:, of], P), ALU.mult).then_inc(dve_done, S.up("dve_done"))
                dve.wait_ge(dve_done, S.value("dve_done"))
                dve.tensor_tensor(two(2), cut(N[1], 4, P), bc(beta_t[:, of], P), ALU.mult).then_inc(dve_done, S.up("dve_done"))
                dve.wait_ge(dve_done, S.value("dve_done"))

        steps = [(level, p) for level in range(6) for p in range(4)]

        def inverse_pe(S):
            def couple(n):
                pe.wait_ge(dve_pe, S.next("dve_pe"))
                for i in range(4):
                    last = pe.matmul(Y[n % 2][:, i * P:(i + 1) * P], tmp[n % 2][:, i, :], tt[:, 4 * steps[n][1] + i, :],
                                        start=True, stop=True, skip_group_check=True)
                last.then_inc(pe_act, S.up("pe_act"))

            couple(0)
            for n, (_, p) in enumerate(steps):
                if n + 1 < len(steps):
                    couple(n + 1)
                pe.wait_ge(act_pe, S.next("act_pe"))
                for i in range(4):
                    a = diag[:, n % 2, i, :]
                    pe.matmul(G[n % 2][:, i * P:(i + 1) * P], uu[:, 4 * p + i, :], a, start=True, stop=True,
                                 skip_group_check=True)
                    last = pe.matmul(N[n % 2][:, i * P:(i + 1) * P], a, uu[:, 4 * p + i, :], start=True, stop=True,
                                        skip_group_check=True)
                last.then_inc(pe_dve, S.up("pe_dve"))
            pe.wait_ge(dve_pe, S.next("dve_pe"))
            for p in range(4):
                for i in range(4):
                    h, c = 2 * p + i // 2, i % 2
                    last = pe.matmul(Y[p][:, i * P:(i + 1) * P], gt[:, H + h, c * P:(c + 1) * P], uu[:, 4 * p + i, :],
                                        start=True, stop=True, skip_group_check=True)
            last.then_inc(pe_act, S.up("pe_act"))

        def inverse_act(S):
            for n in range(len(steps)):
                act.wait_ge(pe_act, S.next("pe_act"))
                act.activation(diag[:, n % 2, :, :], cut(Y[n % 2], 4, P), ACT.Copy).then_inc(act_pe, S.up("act_pe"))
                act.wait_ge(act_pe, S.value("act_pe"))
            act.wait_ge(pe_act, S.next("pe_act"))
            for p in range(4):
                last = act.activation(tt[:, 4 * p:4 * p + 4, :], cut(Y[p], 4, P), ACT.Copy, scale=-1.0)
            last.then_inc(act_pe, S.up("act_pe"))

        def inverse_dve(S):
            for m in (uu, tt):
                dve.tensor_copy(m, rep(cst("ident"), 16)).then_inc(dve_done, S.up("dve_done"))
                dve.wait_ge(dve_done, S.value("dve_done"))

            def coupling(n):
                level, p = steps[n]
                ins = dve.tensor_tensor(tmp[n % 2], at_[:, 4 * p:4 * p + 4, :], rep(cst(f"level{level}"), 4), ALU.mult)
                ins.then_inc(dve_pe, S.up("dve_pe"))
                dve.wait_ge(dve_pe, S.value("dve_pe"))

            coupling(0)
            for n, (_, p) in enumerate(steps):
                if n + 1 < len(steps):
                    coupling(n + 1)
                dve.wait_ge(pe_dve, S.next("pe_dve"))
                of = slice(4 * p, 4 * p + 4)
                ins = dve.tensor_tensor(tt[:, of, :], tt[:, of, :], cut(G[n % 2], 4, P), ALU.subtract)
                ins.then_inc(dve_done, S.up("dve_done"))
                dve.wait_ge(dve_done, S.value("dve_done"))
                signal = "dve_done" if n + 1 < len(steps) else "dve_pe"
                ins = dve.tensor_tensor(uu[:, of, :], uu[:, of, :], cut(N[n % 2], 4, P), ALU.subtract)
                ins.then_inc(sems[signal], S.up(signal))
                dve.wait_ge(sems[signal], S.value(signal))

        def scan_pe(S):
            pe.wait_ge(act_pe, S.next("act_pe"))
            for n in range(4):
                c, r = n // 2, block_of(n % 2)
                for b in (0, 1):
                    if n:
                        pe.wait_ge(dve_pe, S.next("dve_pe"))
                    for i in range(4):
                        h = 4 * b + i
                        acc = G[b][r, i * P:(i + 1) * P]
                        last = pe.matmul(acc, uu[r, 2 * h + c, r], gt[r, 2 * H + h, c * P:(c + 1) * P], start=True,
                                            stop=not n, skip_group_check=True)
                        if n:
                            last = pe.matmul(acc, tt[:, 2 * h + c, r], state[:, h, :], start=False, stop=True,
                                                skip_group_check=True)
                    last.then_inc(pe_act, S.up("pe_act"))
                for b in (0, 1):
                    pe.wait_ge(act_pe, S.next("act_pe"))
                    for i in range(4):
                        h = 4 * b + i
                        acc = N[b][:, i * 64:(i + 1) * 64]
                        last = pe.matmul(acc, vn[r, h, :], attn[r, 2 * h + c, r], start=True, stop=not n,
                                            skip_group_check=True)
                        if n:
                            last = pe.matmul(acc, state[:, h, :], gt[:, h, n * 64:(n + 1) * 64], start=False, stop=True,
                                                skip_group_check=True)
                        if n < 3:
                            last = pe.matmul(Y[b][:, i * P:(i + 1) * P], kd[r, 2 * h + c, :], vn[r, h, :], start=True,
                                                stop=True, skip_group_check=True)
                    last.then_inc(pe_dve, S.up("pe_dve"))

        def scan_act(S):
            for n in range(4):
                r = block_of(n % 2)
                for b in (0, 1):
                    act.wait_ge(pe_act, S.next("pe_act"))
                    ins = act.activation(vn[r, 4 * b:4 * b + 4, :], cut(G[b], 4, P)[r, :, :], ACT.Copy)
                    ins.then_inc(act_pe, S.up("act_pe"))
                    act.wait_ge(act_pe, S.value("act_pe"))

        def scan_dve(S):
            for n in range(4):
                for b in (0, 1):
                    dve.wait_ge(pe_dve, S.next("pe_dve"))
                    signal = "dve_done" if n < 3 else "dve_act"
                    ins = dve.tensor_copy(o_t[:, 4 * b:4 * b + 4, n * 64:(n + 1) * 64], cut(N[b][:, 0:T], 4, 64))
                    ins.then_inc(sems[signal], S.up(signal))
                    dve.wait_ge(sems[signal], S.value(signal))
                    for i in range(4 if n < 3 else 0):
                        h = 4 * b + i
                        got, name = Y[b][:, i * P:(i + 1) * P], "dve_pe" if i == 3 else "dve_done"
                        if n:
                            dve.scalar_tensor_tensor(state[:, h, :], state[:, h, :],
                                                     cdk[:, 2 * h + n // 2, n % 2:n % 2 + 1], got, ALU.mult,
                                                     ALU.add).then_inc(sems[name], S.up(name))
                            dve.wait_ge(sems[name], S.value(name))
                        else:
                            dve.tensor_copy(state[:, h, :], got).then_inc(sems[name], S.up(name))
                            dve.wait_ge(sems[name], S.value(name))

        def gdn_out_pe(S):
            pe.wait_ge(act_pe, S.next("act_pe"))
            for i in range(4):
                last = pe.matmul((G[0], G[1], N[0], N[1])[i], cst("ones"), sq[:, i * 512:(i + 1) * 512], start=True,
                                    stop=True)
            last.then_inc(pe_act, S.up("pe_act"))
            lin_pe(S, H, hh, hl)

        def gdn_out_act(S):
            act.wait_ge(dve_act, S.next("dve_act", 2))
            act.activation(sq, o_t.rearrange("p a b -> p (a b)"), ACT.Square).then_inc(act_pe, S.up("act_pe"))
            act.wait_ge(pe_act, S.next("pe_act"))
            for i in range(4):
                last = act.activation(ht[:, i * 512:(i + 1) * 512], (G[0], G[1], N[0], N[1])[i], ACT.Sqrt, bias=eps,
                                        scale=1.0 / P)
            last.then_inc(act_dve, S.up("act_dve"))
            for t in range(H):
                act.wait_ge(lin_ready, S.next("lin_ready"))
                act.activation(conv[:, t % 2, :], bank_of(S), ACT.Silu).then_inc(lin_evac, S.up("lin_evac"))
                split(S)
                hi_lo_act(S, t, o_t[:, t, :])

        def gdn_out_dve(S):
            dve.wait_ge(act_dve, S.next("act_dve"))
            dve.reciprocal(ht, ht).then_inc(dve_done, S.up("dve_done"))
            dve.wait_ge(dve_done, S.value("dve_done"))
            o = o_t.rearrange("p a b -> p (a b)")
            dve.scalar_tensor_tensor(o, o, vec(v1, V1, "g_out"), ht, ALU.mult, ALU.mult).then_inc(dve_done, S.up("dve_done"))
            dve.wait_ge(dve_done, S.value("dve_done"))
            for t in range(H):
                S.step("lin_ready")
                dve.wait_ge(lin_evac, S.next("lin_evac"))
                ins = dve.tensor_tensor(o_t[:, t, :], o_t[:, t, :], conv[:, t % 2, :], ALU.mult)
                ins.then_inc(dve_act, S.up("dve_act"))
                dve.wait_ge(dve_act, S.value("dve_act"))
                split(S)
                lo_dve(S, t, o_t[:, t, :])

        y_gdn = area(4096, DT, T)

        def block1_mixer_pe(S):
            norm_pe(S, DT)
            small_pe(S)
            lin_pe(S, QT + KVT, hh, hl)
            pe.wait_ge(dve_pe, S.next("dve_pe"))
            norm_pe(S, QT)
            norm_pe(S, KVT)
            lin_pe(S, H + H // 2, zh, zl, kt=QT, fresh="h_ready")
            lin_pe(S, H, zh[:, QT:QT + KVT, :], zl[:, QT:QT + KVT, :], kt=KVT, fresh="h_ready")
            values_pe(S)
            rope_pe(S)
            attention_pe(S)
            pe.wait_ge(z_lo, S.value("z_lo", -H))
            lin_pe(S, DT, zh, zl, fresh="z_lo")
            lin_pe_turns(S, 4, hh, hl)
            gdn_small_pe(S)
            gdn_gram_pe(S)
            inverse_pe(S)
            scan_pe(S)
            gdn_out_pe(S)
            lin_pe(S, DT, zh, zl, fresh="z_lo")
            lin_pe(S, 2 * DT, hh, hl)
            lin_pe(S, DT, zh, zl, fresh="z_lo")

        def block1_mixer_act(S):
            x_norm_act(S, hh, shifts[1])
            split(S)
            lin_copy(S, lat, QT + KVT)
            act.wait_ge(lin_evac, S.value("lin_evac"))
            norm_act(S, lat[:, 0:QT, :], QT, zh)
            norm_act(S, lat[:, QT:, :], KVT, zh[:, QT:QT + KVT, :])
            for t in range(H + H // 2):
                lin_copy_tile(S, qn[:, t, :] if t < H else qr[:, t - H, :], t, QT)
            lin_copy(S, kn, H, kt=KVT)
            values_act(S)
            attention_act(S)
            lin_copy(S, y_mla, DT)
            conv_act(S, gt)
            act.wait_ge(act_dve, S.value("act_dve"))
            gdn_small_act(S)
            gdn_gram_act(S)
            inverse_act(S)
            scan_act(S)
            gdn_out_act(S)
            lin_copy(S, y_gdn, DT)
            gates_act(S, y_mla, y_gdn)
            add_act(S)

        def block1_mixer_dve(S):
            x_norm_dve(S, gains[1], hh, hl, shifts[1])
            small_dve(S)
            lin_copy(S, lat, QT + KVT)
            norm_dve(S, lat[:, 0:QT, :], QT, vec(v1, V1, "g_q"), zh, zl)
            norm_dve(S, lat[:, QT:, :], KVT, vec(v1, V1, "g_kv"), zh[:, QT:QT + KVT, :], zl[:, QT:QT + KVT, :])
            lin_copy(S, qn, H + H // 2, kt=QT)
            lin_copy(S, kn, H, kt=KVT)
            split(S, 2)
            rope_dve(S)
            attention_dve(S)
            lin_copy(S, y_mla, DT)
            conv_dve(S, vec(v1, V1, "conv"))
            gdn_small_dve(S)
            gdn_gram_dve(S)
            inverse_dve(S)
            scan_dve(S)
            gdn_out_dve(S)
            lin_copy(S, y_gdn, DT)
            gates_dve(S, y_mla, y_gdn)
            add_dve(S, gate2)

        @block.sync
        def _(sp):
            S = Side(sems, "sp")
            for dst, src in ((v1, vec1), (con, consts), (v2, vec2), (x.rearrange("p a b -> p (a b)"), x_in)):
                sp.dma_start(dst, src).then_inc(loaded, 16)
            for s in range(RING):
                sp.dma_start(raw[:, s, :], stream[s]).then_inc(raw_loaded[s], 16)
            with sp.Fori(1, UNITS // RING) as turn:
                for s in range(RING):
                    sp.wait_ge(lo_ready, turn * RING + (s + 1 - RING))
                    sp.dma_start(raw[:, s, :], stream[bass.ds(turn * RING + s, 1), :, :].rearrange("a p n -> (a p) n"))\
                      .then_inc(raw_loaded[s], 16)
            sp.wait_ge(result_ready, 1)
            sp.dma_start(out, ht).then_inc(stored, 16)
            sp.wait_ge(stored, 16)
            for s in range(RING):
                sp.wait_ge(raw_loaded[s], 16 * (UNITS // RING))

        @block.gpsimd
        def _(pool):
            pool.memset(eps, EPS).then_inc(cleared, 1)
            pool.memset(pad, 0.0).then_inc(cleared, 1)
            pool.memset(padu, 0.0).then_inc(cleared, 1)

        @block.tensor
        def _(pe):
            S = Side(sems, "pe")
            pe.wait_ge(loaded, S.next("loaded", 64))
            ada_pe(S)
            norm_pe(S, DT)
            ffn_pe(S)
            block1_mixer_pe(S)
            norm_pe(S, DT)
            ffn_pe(S)
            filler_pe(S, BLOCK1_PAD)
            norm_pe(S, DT)
            with S.loop(pe, LAYERS, LAYER_PER["pe"]):
                norm_pe(S, DT)
                ffn_pe(S)
                layer_mixer_pe(S)
                norm_pe(S, DT)
                ffn_pe(S)
                ple_pe(S)
            norm_pe(S, DT)

        @block.scalar
        def _(act):
            S = Side(sems, "act")
            act.wait_ge(loaded, S.next("loaded", 64))
            act.wait_ge(cleared, S.next("cleared", 3))
            split(S, AHEAD)
            ada_act(S)
            x_norm_act(S, hh, shifts[0])
            ffn_act(S)
            block1_mixer_act(S)
            x_norm_act(S, hh, shifts[2], after="lin_evac")
            ffn_act(S)
            split(S, BLOCK1_PAD)
            x_norm_act(S)
            with S.loop(act, LAYERS, LAYER_PER["act"]):
                x_norm_act(S, hh)
                ffn_act(S)
                layer_mixer_act(S)
                x_norm_act(S, hh, after="lin_evac")
                ffn_act(S)
                x_norm_act(S, hh)
                ple_act(S)
            x_norm_act(S)

        @block.vector
        def _(dve):
            S = Side(sems, "dve")
            dve.wait_ge(loaded, S.next("loaded", 64))
            dve.wait_ge(cleared, S.next("cleared", 3))
            split(S, AHEAD)
            ada_dve(S)
            x_norm_dve(S, gains[0], hh, hl, shifts[0])
            ffn_dve(S, half_gate1)
            block1_mixer_dve(S)
            x_norm_dve(S, gains[2], hh, hl, shifts[2], after="lin_evac")
            ffn_dve(S, half_gate3)
            split(S, BLOCK1_PAD)
            x_norm_dve(S, vec(v1, V1, "g_final"), dst=x, done="x_ready")
            with S.loop(dve, LAYERS, LAYER_PER["dve"]) as layer:
                dve.tensor_copy(lv, v2[:, bass.ds(layer * V2_N, V2_N)]).then_inc(dve_done, S.up("dve_done"))
                dve.wait_ge(dve_done, S.value("dve_done"))
                x_norm_dve(S, vec(lv, V2, "ffn1"), hh, hl)
                ffn_dve(S, 0.5)
                layer_mixer_dve(S)
                x_norm_dve(S, vec(lv, V2, "ffn2"), hh, hl, after="lin_evac")
                ffn_dve(S, 0.5)
                x_norm_dve(S, vec(lv, V2, "ple"), hh, hl)
                ple_dve(S)
            x_norm_dve(S, vec(v1, V1, "final_norm"), done="result_ready")



def tiles(w):
    k, n = w.shape
    return w.reshape(k // P, P, n // P, P).transpose(2, 0, 1, 3).reshape(-1, P, P)


def units(*parts):
    t = np.concatenate(parts)
    t = np.concatenate([t, np.zeros((-len(t) % 8, P, P), np.float32)])
    return t.reshape(-1, 8, P, P).transpose(0, 2, 1, 3).reshape(-1, P, U)


def ffn_units(gate, up, down):
    g, u, d = units(tiles(gate)), units(tiles(up)), down.reshape(FT, P, D)
    order = [g[0], u[0]]
    for f in range(1, FT):
        order += [g[f], u[f], d[f - 1]]
    return np.stack([*order, d[FT - 1]])


def wide_units(w, n):
    out = np.zeros((1, P, U), np.float32)
    out[0, :, :DT * n] = w.reshape(DT, P, n).transpose(1, 0, 2).reshape(P, DT * n)
    return out


def cols(v):
    return np.asarray(v, np.float32).reshape(-1, P).T


def taps(w):
    return w.reshape(w.shape[0], -1, P).transpose(2, 1, 0).reshape(P, -1)


def rows(v):
    return np.broadcast_to(v.reshape(1, -1), (P, v.size))


def block1_units(a):
    w_in, w_uq, w_ukv = a["w_in"][0], a["w_uq"][0], a["w_ukv"][0]
    at = np.cumsum([0, 768, 256, 64, 1024, 1024, 1024, 8, 8, 1024, 2048])
    part = [w_in[:, p:q] for p, q in zip(at[:-1], at[1:])]
    uq = w_uq.reshape(768, H, 192)
    uq = np.concatenate([uq[:, :, :P].reshape(768, -1), uq[:, :, P:].reshape(768, -1)], 1)
    ukv = w_ukv.reshape(256, H, 256)
    gates = tiles(part[9]).reshape(2, DT, DT, P, P).transpose(1, 0, 2, 3, 4).reshape(-1, P, P)
    return [
        units(tiles(a["w_ada"][0])),
        ffn_units(a["w1_gate"][0], a["w1_up"][0], a["w1_down"][0]),
        wide_units(np.concatenate([part[2], part[6], part[7]], 1), SMALL1),
        units(tiles(part[0]), tiles(part[1])),
        units(tiles(uq)),
        units(tiles(ukv[:, :, :P].reshape(256, -1))),
        ukv[:, :, P:].reshape(2, P, U),
        units(tiles(a["w_o_mla"][0])),
        units(tiles(w_in[:, at[3]:at[6]])),
        units(tiles(part[8])),
        units(tiles(a["w_o_gdn"][0])),
        units(gates),
        units(tiles(a["w_out"][0])),
        ffn_units(a["w2_gate"][0], a["w2_up"][0], a["w2_down"][0]),
        np.zeros((BLOCK1_PAD, P, U), np.float32),
    ]


def layer_units(a, n):
    g = lambda name: a[name + "_2"][n]
    w_in = g("w_in")
    at = np.cumsum([0, 1024, 1024, 1024, 2048, 3072, 32, 1024, 1024])
    part = [w_in[:, p:q] for p, q in zip(at[:-1], at[1:])]
    each = lambda *ws: np.stack([tiles(w).reshape(-1, DT, P, P) for w in ws], 1).reshape(-1, P, P)
    p = np.zeros((1, P, U), np.float32)
    p[0, :, :2 * T] = g("p")[0].T.reshape(2, P, T).transpose(1, 0, 2).reshape(P, -1)
    return [
        ffn_units(g("ffn1_wg"), g("ffn1_wu"), g("ffn1_wd")),
        wide_units(part[5], SSM_H),
        units(each(part[2], part[1], part[0])),
        units(tiles(g("sc_w_out"))),
        units(tiles(part[4])),
        units(tiles(part[3])),
        units(tiles(g("m_w_out"))),
        units(each(part[6], part[7])),
        units(tiles(g("w_o"))),
        ffn_units(g("ffn2_wg"), g("ffn2_wu"), g("ffn2_wd")),
        p,
        units(tiles(g("ple_w_gate"))),
        units(tiles(g("ple_w_proj"))),
        np.zeros((LAYER_PAD, P, U), np.float32),
    ]


def kernel(**inputs):
    import concourse.bacc as bacc
    from concourse.bass_utils import run_bass_kernel_spmd as run

    a = {k: np.ascontiguousarray(v) for k, v in inputs.items()}
    parts = block1_units(a)
    assert sum(map(len, parts)) == BLOCK1_UNITS + BLOCK1_PAD
    for n in range(LAYERS):
        of_layer = layer_units(a, n)
        assert sum(map(len, of_layer)) == LAYER_UNITS + LAYER_PAD
        parts += of_layer
    parts.append(np.zeros((RING, P, U), np.float32))
    vec1 = np.concatenate([cols(a["c"]), cols(a["b_ada"]), cols(a["g_ffn1"]), cols(a["g_mix"]), cols(a["g_q_lat"]),
                           cols(a["g_kv_lat"]), taps(a["w_conv"][0]), cols(a["g_gdn_out"]), cols(a["g_ffn2"]),
                           cols(a["g_final"]), cols(a["final_norm_2"]), rows(a["dt_bias"]), rows(a["a_log"])], 1)
    vec2 = []
    for n in range(LAYERS):
        g = {k[:-2]: v[n] for k, v in a.items() if k.endswith("_2") and k != "final_norm_2"}
        vec2 += [cols(g["ffn1_norm"]), cols(g["mix_norm"]), taps(g["sc_conv_w"]), taps(g["m_conv_w"]),
                 cols(g["m_conv_b"]), cols(np.repeat(g["m_D"], 64)), cols(g["m_norm"]), cols(g["ffn2_norm"]),
                 cols(g["ple_norm"]), rows(g["m_dt_bias"]), rows(g["m_A_log"])]
    arrays = {
        "stream": np.concatenate(parts),
        "x": a["x"][0].T.reshape(DT, P, T).transpose(1, 0, 2).reshape(P, -1),
        "consts": constants(),
        "vec1": vec1,
        "vec2": np.concatenate(vec2, 1),
    }
    arrays = {k: np.ascontiguousarray(v, np.float32) for k, v in arrays.items()}
    nc = bacc.Bacc("TRN2", target_bir_lowering=False, num_devices=1)
    aps = [nc.dram_tensor(k, v.shape, F32, kind="ExternalInput").ap() for k, v in arrays.items()]
    out = nc.dram_tensor("out", (P, DT * T), F32, kind="ExternalOutput").ap()
    build(nc, *aps, out)
    r = run(nc, [arrays], core_ids=[0])
    y = r.results[0]["out"]
    return y.reshape(P, DT, T).transpose(2, 1, 0).reshape(1, T, D)
```

```python
from contextlib import ExitStack, contextmanager

import numpy as np

import concourse.bass as bass
from concourse import mybir

F32 = mybir.dt.float32
F32R = mybir.dt.float32r
ALU = mybir.AluOpType
ACT = mybir.ActivationFunctionType
AX = mybir.AxisListType

P = 128
T = 256
D = 1024
DT = D // P
FT = 2816 // P
N_ADA = 9 * DT
ADA_1 = 6 * DT
LAYERS = 2
EPS = 1e-6
H = 8
QT, KVT = 6, 2
ROPE = 64
SMALL1 = ROPE + 2 * H
SSM_H = 32
SSM_G = 4
XT = 16
CONVT = 24
RING = 3
AHEAD = 2
U = 8 * P
ARENA = 18400

FFN_UNITS = 3 * FT
BLOCK1_UNITS = N_ADA + 2 * FFN_UNITS + 1 + 8 + 9 + 2 + 2 + 8 + CONVT + 8 + 8 + 16 + 8
BLOCK1_PAD = -BLOCK1_UNITS % RING
LAYER_UNITS = 2 * FFN_UNITS + 1 + 24 + 8 + CONVT + 16 + 16 + 16 + 8 + 8 + 1 + 2
LAYER_PAD = -LAYER_UNITS % RING
UNITS = BLOCK1_UNITS + BLOCK1_PAD + LAYERS * (LAYER_UNITS + LAYER_PAD) + RING

PER_PE = {
    "lo_ready": 258, "units_begun": 258, "lin_ready": 120, "lin_evac": 120, "gu_ready": 44, "a_ready": 44,
    "a_lo": 44, "y_ready": 2, "sq_ready": 32, "ms_ready": 4, "h_ready": 32, "z_lo": 34,
    "pe_act": 4, "pe_dve": 44, "act_pe": 5, "dve_pe": 42,
}
PER_ACT = {
    "hi_ready": 258, "units_begun": 258, "lin_ready": 120, "lin_evac": 120, "gu_ready": 44, "sg_ready": 44,
    "a_ready": 44, "a_hi": 44, "sq_ready": 32, "ms_ready": 4, "std_ready": 4, "h_scaled": 32,
    "h_hi": 32, "x_ready": 24, "z_hi": 34, "pe_act": 4, "act_dve": 47, "dve_act": 68,
    "act_pe": 5, "act_done": 3,
}
PER_DVE = {
    "hi_ready": 258, "lo_ready": 258, "lin_ready": 120, "lin_evac": 120, "sg_ready": 44, "a_ready": 44,
    "a_hi": 44, "a_lo": 44, "y_ready": 2, "std_ready": 4, "h_scaled": 32, "h_hi": 32,
    "h_ready": 32, "x_ready": 24, "z_hi": 34, "z_lo": 34, "pe_dve": 44, "act_dve": 47,
    "dve_act": 68, "dve_pe": 42, "dve_done": 132,
}
LAYER_PER = {"pe": PER_PE, "act": PER_ACT, "dve": PER_DVE}


def columns(names):
    at, out = 0, {}
    for name, n in names:
        out[name] = (at, n)
        at += n
    return out, at


V1, V1_N = columns([("c", DT), ("b_ada", N_ADA), ("g_ffn1", DT), ("g_mix", DT), ("g_q", QT), ("g_kv", KVT),
                    ("conv", CONVT * 4), ("g_out", 1), ("g_ffn2", DT), ("g_final", DT), ("final_norm", DT),
                    ("dt_bias", H), ("a_log", H)])
V2, V2_N = columns([("ffn1", DT), ("mix", DT), ("sc_conv", DT * 3), ("conv", CONVT * 4), ("conv_b", CONVT),
                    ("m_D", XT), ("m_norm", XT), ("ffn2", DT), ("ple", DT), ("dt_bias", SSM_H), ("A_log", SSM_H)])
C, C_N = columns([("ident", P), ("ones", P), ("cum64", P), ("all64", P)] + [(f"level{i}", P) for i in range(6)]
                 + [("cum", P), ("after", P), ("swap", P), ("cosT", T), ("sinT", T), ("cos", 64), ("sin", 64),
                    ("mask", 384)])


def constants():
    j, i = np.mgrid[0:P, 0:P]
    same = j // 64 == i // 64
    inv_freq = np.float32(10000.0) ** (-np.arange(0, ROPE, 2, dtype=np.float32) / np.float32(ROPE))
    ang = np.arange(T, dtype=np.float32)[:, None] * inv_freq[None, :]
    cos, sin = np.cos(ang), np.sin(ang)
    parts = {
        "ident": j == i, "ones": j >= 0, "cum64": same & (j <= i), "all64": same, "cum": j <= i, "after": j > i,
        "swap": (j ^ 32) == i,
        "cosT": np.tile(cos.T, (4, 1)), "sinT": np.tile(np.concatenate([-sin.T, sin.T]), (2, 1)),
        "cos": cos.reshape(2, P, 32).transpose(1, 0, 2).reshape(P, 64),
        "sin": sin.reshape(2, P, 32).transpose(1, 0, 2).reshape(P, 64),
    }
    for n in range(6):
        parts[f"level{n}"] = (j >> (n + 1) == i >> (n + 1)) & (i >> n & 1 == 1) & (j >> n & 1 == 0)
    q, k = np.arange(P)[:, None], np.arange(T)[None, :]
    parts["mask"] = np.concatenate([np.where((k[:, :P] // 64) <= q // 64, 0.0, -1e30),
                                    np.where((k // 64) <= (q + P) // 64, 0.0, -1e30)], 1)
    return np.concatenate([np.asarray(parts[n], np.float32).reshape(P, -1) for n in C], 1)


class Side:

    def __init__(self, sems, who):
        self.n = dict.fromkeys(sems, 0)
        self.turns = []
        self.new_unit = False
        self.who = who

    def value(self, name, back=0):
        v = self.n[name] - back
        assert v > 0, name
        for reg, per in self.turns:
            if per.get(name, 0):
                v = reg * per[name] + v
        return v

    def step(self, name, k=1):
        self.n[name] += k

    def next(self, name, k=1):
        self.step(name, k)
        return self.value(name)

    def up(self, name, k=1):
        self.step(name, k)
        return k

    @contextmanager
    def loop(self, eng, turns, per):
        with eng.Fori(0, turns) as reg:
            before = dict(self.n)
            self.turns.append((reg, per))
            yield reg
            self.turns.pop()
            got = {k: v - before[k] for k, v in self.n.items() if v != before[k]}
            assert got == per, got
        for k, v in per.items():
            self.n[k] = before[k] + v * turns


def build(nc, stream, x_in, consts, vec1, vec2, out):
    ctx = ExitStack()
    with ctx:
        def sb(name, n, dt=F32):
            return ctx.enter_context(nc.sbuf_tensor("sb_" + name, [P, n], dt))[:, :]

        def cut(ap, *dims):
            names = "abcd"[:len(dims)]
            return ap.rearrange(f"p ({' '.join(names)}) -> p {' '.join(names)}", **dict(zip(names, dims)))

        def bank(name):
            return ctx.enter_context(nc.psum_tensor(name, [P, 512], F32))[:, :]

        raw = cut(sb("raw", RING * U), RING, U)
        w_hi, w_lo = (cut(sb(n, RING * U, F32R), RING, U) for n in ("w_hi", "w_lo"))
        x = cut(sb("x", DT * T), DT, T)
        hh, hl = (cut(sb(n, DT * T, F32R), DT, T) for n in ("h_hi", "h_lo"))
        con, v1, v2 = sb("con", C_N), sb("v1", V1_N), sb("v2", LAYERS * V2_N)
        lv = sb("layer_vec", V2_N)
        sq, ht = sb("sq", DT * T), sb("ht", DT * T)
        std, rstd = sb("std", 512), sb("rstd", 512)
        sg = sb("silu_gate", 512)
        padu = sb("padu", 258)
        conv = cut(sb("conv_out", 2 * T), 2, T)
        eps, spare = sb("eps", 1), sb("spare", 1)
        cs, ada, cc = sb("c_silu", DT), sb("ada", N_ADA), cut(sb("c_cut", 2 * DT, F32R), DT, 2)
        gsc = sb("gains", 5 * DT)
        ar = sb("arena", ARENA)
        with nc.sbuf_tensor("sb_z_hi", [P, XT * T], F32R) as a, nc.sbuf_tensor("sb_z_lo", [P, XT * T], F32R) as b:
            zh, zl = cut(a[:, :], XT, T), cut(b[:, :], XT, T)
        kept_a, kept_b = (cut(sb(n, XT * T), XT, T) for n in ("kept_a", "kept_b"))
        banks = [bank(f"bank{i}") for i in range(8)]
        Y, G, N = banks[0:4], banks[4:6], banks[6:8]

        def vec(table, where, name, i=0, n=None):
            at, size = where[name]
            return table[:, at + i:at + i + (size if n is None else n)]

        def cst(name, i=0, n=None):
            return vec(con, C, name, i, n)

        def bc(ap, n):
            return ap.unsqueeze(len(ap.shape)).broadcast_to([*ap.shape, n])

        def rep(ap, n):
            return ap.unsqueeze(1).broadcast_to([ap.shape[0], n, *ap.shape[1:]])

        sems = {}

        def sem(name):
            sems[name] = ctx.enter_context(nc.semaphore(name))
            return sems[name]

        loaded = sem("loaded")
        cleared = sem("cleared")
        hi_ready = sem("hi_ready")
        lo_ready = sem("lo_ready")
        units_begun = sem("units_begun")
        lin_ready = sem("lin_ready")
        lin_evac = sem("lin_evac")
        gu_ready = sem("gu_ready")
        sg_ready = sem("sg_ready")
        a_ready = sem("a_ready")
        a_hi = sem("a_hi")
        a_lo = sem("a_lo")
        y_ready = sem("y_ready")
        sq_ready = sem("sq_ready")
        ms_ready = sem("ms_ready")
        std_ready = sem("std_ready")
        h_scaled = sem("h_scaled")
        h_hi = sem("h_hi")
        h_ready = sem("h_ready")
        x_ready = sem("x_ready")
        z_hi = sem("z_hi")
        z_lo = sem("z_lo")
        pe_act = sem("pe_act")
        pe_dve = sem("pe_dve")
        act_dve = sem("act_dve")
        dve_act = sem("dve_act")
        act_pe = sem("act_pe")
        dve_pe = sem("dve_pe")
        act_done = sem("act_done")
        dve_done = sem("dve_done")
        result_ready = sem("result_ready")
        stored = sem("stored")
        raw_loaded = [ctx.enter_context(nc.semaphore(f"raw_loaded{i}")) for i in range(RING)]
        block = ctx.enter_context(nc.Block())
        pe, act, dve = nc.tensor, nc.scalar, nc.vector


        def split_act(S):
            u = S.n["hi_ready"]
            v = 16 * (u // RING + 1)
            for reg, per in S.turns:
                v = reg * (16 * per["hi_ready"] // RING) + v
            act.wait_ge(raw_loaded[u % RING], v)
            S.n["units_begun"] = u
            if u > 1:
                act.wait_ge(units_begun, S.value("units_begun", 1))
            act.activation(w_hi[:, u % RING, :], raw[:, u % RING, :], ACT.Copy).then_inc(hi_ready, S.up("hi_ready"))

        def split_dve(S):
            u = S.n["lo_ready"]
            dve.wait_ge(hi_ready, S.next("hi_ready"))
            dve.tensor_tensor(w_lo[:, u % RING, :], raw[:, u % RING, :],
                              w_hi[:, u % RING, :].bitcast(F32), ALU.subtract).then_inc(lo_ready, S.up("lo_ready"))

        def unit(S):
            pe.wait_ge(lo_ready, S.next("lo_ready"))
            S.new_unit = True
            return (S.n["lo_ready"] - 1) % RING

        def begun(S, ins):
            if S.new_unit:
                ins.then_inc(units_begun, S.up("units_begun"))
                S.new_unit = False

        def product(S, acc, slot, tile, hi, lo, start, stop):
            a, b = w_hi[:, slot, tile * P:(tile + 1) * P], w_lo[:, slot, tile * P:(tile + 1) * P]
            begun(S, pe.matmul(acc, a, hi, start=start, stop=False, skip_group_check=True))
            pe.matmul(acc, a, lo, start=False, stop=False, skip_group_check=True)
            return pe.matmul(acc, b, hi, start=False, stop=stop, skip_group_check=True)

        def turned(S, acc, slot, at, n, hi, lo, start, stop):
            a, b = w_hi[:, slot, at:at + n], w_lo[:, slot, at:at + n]
            begun(S, pe.matmul(acc, hi, a, start=start, stop=False, skip_group_check=True))
            pe.matmul(acc, lo, a, start=False, stop=False, skip_group_check=True)
            return pe.matmul(acc, hi, b, start=False, stop=stop, skip_group_check=True)

        def filler_pe(S, n):
            for _ in range(n):
                slot = unit(S)
                begun(S, pe.matmul(N[1][:, 0:2], w_hi[:, slot, 0:P], w_lo[:, slot, 0:2], start=True, stop=True,
                                      skip_group_check=True))

        def split(S, n=1):
            for _ in range(n):
                (split_act if "act" == S.who else split_dve)(S)


        def lin_pe(S, tiles, hi, lo, kt=DT, fresh=None):
            slot = 0
            for t in range(tiles):
                acc = Y[S.n["lin_ready"] % 3][:, 0:T]
                S.step("lin_evac")
                if S.n["lin_evac"] > 3:
                    pe.wait_ge(lin_evac, S.value("lin_evac", 3))
                for k in range(kt):
                    if (t * kt + k) % 8 == 0:
                        slot = unit(S)
                    if t == 0 and fresh:
                        pe.wait_ge(sems[fresh], S.next(fresh))
                    last = product(S, acc, slot, (t * kt + k) % 8, hi[:, k, :], lo[:, k, :], k == 0, k == kt - 1)
                last.then_inc(lin_ready, S.up("lin_ready"))

        def bank_of(S):
            return Y[(S.n["lin_ready"] - 1) % 3][:, 0:T]

        def lin_copy_tile(S, dst, t, kt):
            if S.who == "act":
                act.wait_ge(lin_ready, S.next("lin_ready"))
                act.activation(dst, bank_of(S), ACT.Copy).then_inc(lin_evac, S.up("lin_evac"))
            else:
                S.step("lin_ready")
                S.step("lin_evac")
            split(S, (t + 1) * kt // 8 - t * kt // 8)

        def lin_copy(S, dst, tiles, kt=DT):
            for t in range(tiles):
                lin_copy_tile(S, None if S.who == "dve" else dst[:, t, :], t, kt)


        def root_act(S, src, nt, after=None):
            act.activation(spare, eps, ACT.Sqrt)
            for t in range(nt):
                if after is not None:
                    act.wait_ge(sems[after], S.value(after, nt - 1 - t))
                act.activation(sq[:, t * T:(t + 1) * T], src[:, t, :], ACT.Square).then_inc(sq_ready, S.up("sq_ready"))
            act.wait_ge(ms_ready, S.next("ms_ready"))
            ins = act.activation(std[:, 0:T], N[0][:, 0:T], ACT.Sqrt, bias=eps, scale=1.0 / (nt * P))
            ins.then_inc(std_ready, S.up("std_ready"))

        def norm_act(S, src, nt, hi=None, shift=None, after=None):
            root_act(S, src, nt, after)
            scaled_act(S, nt, hi, shift)

        def scaled_act(S, nt, hi=None, shift=None):
            if hi is None:
                return
            for t in range(nt):
                act.wait_ge(h_scaled, S.next("h_scaled"))
                if shift is None:
                    act.activation(hi[:, t, :], ht[:, t * T:(t + 1) * T], ACT.Copy).then_inc(h_hi, S.up("h_hi"))
                else:
                    ins = act.activation(hi[:, t, :], ht[:, t * T:(t + 1) * T], ACT.Identity, bias=shift[:, t:t + 1])
                    ins.then_inc(h_hi, S.up("h_hi"))

        def norm_pe(S, nt):
            for t in range(nt):
                pe.wait_ge(sq_ready, S.next("sq_ready"))
                last = pe.matmul(N[0][:, 0:T], cst("ones"), sq[:, t * T:(t + 1) * T], start=t == 0, stop=t == nt - 1)
            last.then_inc(ms_ready, S.up("ms_ready"))

        def norm_dve(S, src, nt, g, hi=None, lo=None, shift=None, dst=None, done="h_scaled"):
            dve.wait_ge(std_ready, S.next("std_ready"))
            dve.reciprocal(rstd[:, 0:T], std[:, 0:T]).then_inc(dve_done, S.up("dve_done"))
            dve.wait_ge(dve_done, S.value("dve_done"))
            for t in range(nt):
                to = ht[:, t * T:(t + 1) * T] if dst is None else dst[:, t, :]
                last = dve.scalar_tensor_tensor(to, src[:, t, :], g[:, t:t + 1], rstd[:, 0:T], ALU.mult, ALU.mult)
                if hi is not None or done == "x_ready" or t == nt - 1:
                    last.then_inc(sems[done], S.up(done))
            if hi is None:
                return
            for t in range(nt):
                dve.wait_ge(h_hi, S.next("h_hi"))
                h, a = ht[:, t * T:(t + 1) * T], hi[:, t, :].bitcast(F32)
                if shift is None:
                    dve.tensor_tensor(lo[:, t, :], h, a, ALU.subtract).then_inc(h_ready, S.up("h_ready"))
                else:
                    ins = dve.scalar_tensor_tensor(lo[:, t, :], h, shift[:, t:t + 1], a, ALU.add, ALU.subtract)
                    ins.then_inc(h_ready, S.up("h_ready"))


        sg_t, at_t = sg[:, 0:T], sg[:, T:2 * T]

        def gate_up_pe(S, par, first=False):
            S.step("a_ready")
            if S.n["a_ready"] > 2:
                pe.wait_ge(a_ready, S.value("a_ready", 2))
            for half in (0, 1):
                slot = unit(S)
                for k in range(DT):
                    if first and not half:
                        pe.wait_ge(h_ready, S.next("h_ready"))
                    last = product(S, G[par][:, half * T:(half + 1) * T], slot, k, hh[:, k, :], hl[:, k, :],
                                   k == 0, k == DT - 1)
            last.then_inc(gu_ready, S.up("gu_ready"))

        def down_pe(S, par, first=False, final=False):
            slot = unit(S)
            pe.wait_ge(a_lo, S.next("a_lo"))
            for o in range(DT):
                last = product(S, Y[o // 2][:, o % 2 * T:(o % 2 + 1) * T], slot, o, zh[:, par, :], zl[:, par, :],
                               first and o % 2 == 0, final)
            if final:
                last.then_inc(y_ready, S.up("y_ready"))

        PAIR = dict(hi_ready=6, lo_ready=6, units_begun=6, gu_ready=2, sg_ready=2, a_ready=2, a_hi=2, a_lo=2)

        def per(*names, **more):
            return {n: PAIR[n] for n in names} | more

        def ffn_pe(S):
            gate_up_pe(S, 0, True)
            gate_up_pe(S, 1)
            down_pe(S, 0, first=True)
            with S.loop(pe, FT // 2 - 1, per("lo_ready", "units_begun", "gu_ready", "a_ready", "a_lo")):
                for par in (0, 1):
                    gate_up_pe(S, par)
                    down_pe(S, 1 - par)
            down_pe(S, 1, final=True)

        def ffn_step_act(S, par, units=3):
            split(S, 2)
            act.wait_ge(gu_ready, S.next("gu_ready"))
            act.activation(sg_t, G[par][:, 0:T], ACT.Silu).then_inc(sg_ready, S.up("sg_ready"))
            split(S, units - 2)
            act.wait_ge(a_ready, S.next("a_ready"))
            act.activation(zh[:, par, :], at_t, ACT.Copy).then_inc(a_hi, S.up("a_hi"))

        def ffn_act(S):
            ffn_step_act(S, 0, 2)
            ffn_step_act(S, 1)
            with S.loop(act, FT // 2 - 1, per("hi_ready", "units_begun", "gu_ready", "sg_ready", "a_ready", "a_hi")):
                ffn_step_act(S, 0)
                ffn_step_act(S, 1)
            split(S)

        def ffn_step_dve(S, par, units=3):
            split(S, 2)
            dve.wait_ge(sg_ready, S.next("sg_ready"))
            if S.n["a_lo"]:
                dve.wait_ge(a_lo, S.value("a_lo"))
            dve.tensor_tensor(at_t, sg_t, G[par][:, T:2 * T], ALU.mult).then_inc(a_ready, S.up("a_ready"))
            dve.wait_ge(a_ready, S.value("a_ready"))
            split(S, units - 2)
            dve.wait_ge(a_hi, S.next("a_hi"))
            ins = dve.tensor_tensor(zl[:, par, :], at_t, zh[:, par, :].bitcast(F32), ALU.subtract)
            ins.then_inc(a_lo, S.up("a_lo"))

        def ffn_dve(S, scale):
            ffn_step_dve(S, 0, 2)
            ffn_step_dve(S, 1)
            with S.loop(dve, FT // 2 - 1, per("hi_ready", "lo_ready", "sg_ready", "a_ready", "a_hi", "a_lo")):
                ffn_step_dve(S, 0)
                ffn_step_dve(S, 1)
            split(S)
            dve.wait_ge(y_ready, S.next("y_ready"))
            for o in range(DT):
                s = scale if isinstance(scale, float) else scale[:, o:o + 1]
                dve.scalar_tensor_tensor(x[:, o, :], Y[o // 2][:, o % 2 * T:(o % 2 + 1) * T], s, x[:, o, :],
                                         ALU.mult, ALU.add).then_inc(x_ready, S.up("x_ready"))

        def x_norm_act(S, hi=None, shift=None, after="x_ready"):
            if after == "x_ready":
                S.step(after, DT)
            norm_act(S, x, DT, hi, shift, after)

        def x_norm_dve(S, g, hi=None, lo=None, shift=None, dst=None, after="x_ready", done="h_scaled"):
            dve.wait_ge(sems[after], S.value(after))
            norm_dve(S, x, DT, g, hi, lo, shift, dst, done)


        ada_rows = ar[:, 0:ADA_1 * P]
        late_rows = ar[:, 14080:14080 + (N_ADA - ADA_1) * P]

        def rows_pe(S, acc):
            for j in range(4):
                slot = unit(S)
                for k in (0, 1):
                    for part in (w_hi, w_lo):
                        ins = pe.matmul(acc, cc[:, 2 * j + k, :], part[:, slot, k * 512:(k + 1) * 512],
                                        start=not j and not k and part is w_hi,
                                        stop=j == 3 and k == 1 and part is w_lo, skip_group_check=True)
                        begun(S, ins)
            ins.then_inc(lin_ready, S.up("lin_ready"))

        def columns_pe(S, rows, first, n):
            pe.wait_ge(lin_evac, S.value("lin_evac"))
            for t in range(n):
                last = pe.matmul(N[1][:, first + t:first + t + 1], rows[0:2, t * P:(t + 1) * P],
                                 cst("ones", 0, 1)[0:2, :], start=True, stop=True, skip_group_check=True)
            last.then_inc(pe_dve, S.up("pe_dve"))

        def ada_pe(S):
            pe.wait_ge(dve_pe, S.next("dve_pe"))

            def groups(first):
                for g in range(3):
                    acc = Y[g][0:2, :]
                    S.step("lin_evac")
                    if not first:
                        pe.wait_ge(lin_evac, S.value("lin_evac", 3))
                    rows_pe(S, acc)

            groups(True)
            with S.loop(pe, ADA_1 // 12 - 1, dict(lo_ready=12, units_begun=12, lin_ready=3, lin_evac=3)):
                groups(False)
            columns_pe(S, ada_rows, 0, ADA_1)

        def ada_act(S):
            act.activation(cs, vec(v1, V1, "c"), ACT.Silu).then_inc(act_done, S.up("act_done"))
            act.wait_ge(act_done, S.value("act_done"))
            act.activation(cc[:, :, 0], cs, ACT.Copy).then_inc(act_dve, S.up("act_dve"))
            with S.loop(act, ADA_1 // 12, dict(hi_ready=12, units_begun=12, lin_ready=3, lin_evac=3)) as turn:
                for g in range(3):
                    split(S, 4)
                    act.wait_ge(lin_ready, S.next("lin_ready"))
                    ins = act.activation(ada_rows[0:2, bass.ds(turn * 1536 + g * 512, 512)], Y[g][0:2, :], ACT.Copy)
                    ins.then_inc(lin_evac, S.up("lin_evac"))

        def ada_dve(S):
            dve.wait_ge(act_dve, S.next("act_dve"))
            ins = dve.tensor_tensor(cc[:, :, 1], cs, cc[:, :, 0].bitcast(F32), ALU.subtract)
            ins.then_inc(dve_pe, S.up("dve_pe"))
            with S.loop(dve, ADA_1 // 12, dict(hi_ready=12, lo_ready=12)):
                split(S, 12)
            S.step("lin_ready", ADA_1 // 4)
            S.step("lin_evac", ADA_1 // 4)
            added_dve(S, 0, ADA_1)
            gain_dve(0, "g_ffn1")
            gain_dve(1, "g_mix")
            dve.tensor_scalar(half_gate1, ada[:, 2 * DT:3 * DT], 0.5, None, ALU.mult).then_inc(x_ready, S.up("x_ready"))
            dve.wait_ge(x_ready, S.value("x_ready"))

        def added_dve(S, first, n):
            dve.wait_ge(pe_dve, S.next("pe_dve"))
            ins = dve.tensor_tensor(ada[:, first:first + n], N[1][:, first:first + n], vec(v1, V1, "b_ada", first, n), ALU.add)
            ins.then_inc(dve_done, S.up("dve_done"))
            dve.wait_ge(dve_done, S.value("dve_done"))

        def gain_dve(n, g):
            dve.scalar_tensor_tensor(gains[n], ada[:, (3 * n + 1) * DT:(3 * n + 2) * DT], 1.0, vec(v1, V1, g), ALU.add,
                                     ALU.mult)

        def late_act(S, g):
            split(S, 4)
            act.wait_ge(lin_ready, S.next("lin_ready"))
            ins = act.activation(late_rows[0:2, g * 512:(g + 1) * 512], Y[2 + g % 2][0:2, :], ACT.Copy)
            ins.then_inc(lin_evac, S.up("lin_evac"))

        def late_dve(S):
            added_dve(S, ADA_1, N_ADA - ADA_1)
            gain_dve(2, "g_ffn2")
            ins = dve.tensor_scalar(half_gate3, ada[:, 8 * DT:9 * DT], 0.5, None, ALU.mult)
            ins.then_inc(dve_done, S.up("dve_done"))
            dve.wait_ge(dve_done, S.value("dve_done"))

        shifts = [ada[:, 3 * n * DT:(3 * n + 1) * DT] for n in range(3)]
        gains = [gsc[:, n * DT:(n + 1) * DT] for n in range(3)]
        half_gate1, half_gate3 = gsc[:, 3 * DT:4 * DT], gsc[:, 4 * DT:5 * DT]
        gate2 = ada[:, 5 * DT:6 * DT]


        def area(at, *dims):
            n = int(np.prod(dims))
            assert at + n <= ARENA, (at, dims)
            return cut(ar[:, at:at + n], *dims) if len(dims) > 1 else ar[:, at:at + n]

        pad6, conv6 = area(8192, 6, T + 3), area(9760, 6, T)

        def pads_dve(S):
            dve.memset(pad6[:, :, 0:3], 0.0).then_inc(dve_done, S.up("dve_done"))

        def hi_lo_act(S, t, src, after="dve_act"):
            act.wait_ge(sems[after], S.next(after))
            act.activation(zh[:, t, :], src, ACT.Copy).then_inc(z_hi, S.up("z_hi"))

        def lo_dve(S, t, src):
            dve.wait_ge(z_hi, S.next("z_hi"))
            dve.tensor_tensor(zl[:, t, :], src, zh[:, t, :].bitcast(F32), ALU.subtract).then_inc(z_lo, S.up("z_lo"))
            dve.wait_ge(z_lo, S.value("z_lo"))

        PER6 = dict(hi_ready=6, lo_ready=6, units_begun=6, lin_ready=6, lin_evac=6, act_dve=6, dve_act=6, dve_done=12)

        def six(*names):
            return {n: PER6[n] for n in names}

        def conv_act(S, dst, w, bias=None):
            def silus(turn, pair):
                for k in (2 * pair, 2 * pair + 1):
                    act.wait_ge(dve_act, S.next("dve_act"))
                    b = 0.0 if bias is None else bias[:, bass.ds(turn * 6 + k, 1)]
                    ins = act.activation(dst[:, turn * 6 + k, :], conv6[:, k, :], ACT.Silu, bias=b)
                    ins.then_inc(act_dve, S.up("act_dve"))

            with S.loop(act, CONVT // 6, six("hi_ready", "units_begun", "lin_ready", "lin_evac", "act_dve",
                                             "dve_act")) as turn:
                for pair in range(3):
                    for k in (2 * pair, 2 * pair + 1):
                        split(S)
                        act.wait_ge(lin_ready, S.next("lin_ready"))
                        act.activation(pad6[:, k, 3:], bank_of(S), ACT.Copy)
                        last_tap = w[:, bass.ds(turn * 24 + k * 4 + 3, 1)]
                        ins = act.activation(conv6[:, k, :], bank_of(S), ACT.Copy, scale=last_tap)
                        ins.then_inc(lin_evac, S.up("lin_evac"))
                    if pair:
                        silus(turn, pair - 1)
                silus(turn, 2)

        def conv_dve(S, w):
            with S.loop(dve, CONVT // 6, six("hi_ready", "lo_ready", "lin_ready", "lin_evac", "act_dve", "dve_act",
                                             "dve_done")) as turn:
                for pair in range(3):
                    tiles = (2 * pair, 2 * pair + 1)
                    split(S, 2)
                    S.step("lin_ready", 2)
                    dve.wait_ge(dve_done, S.value("dve_done"))
                    dve.wait_ge(lin_evac, S.next("lin_evac", 2))
                    for j in (0, 1, 2):
                        for k in tiles:
                            signal = "dve_done" if j < 2 else "dve_act"
                            if j:
                                dve.wait_ge(dve_done, S.value("dve_done", 1 if j < 2 or k == tiles[0] else 0))
                            dve.scalar_tensor_tensor(conv6[:, k, :], pad6[:, k, j:j + T],
                                                     w[:, bass.ds(turn * 24 + k * 4 + j, 1)], conv6[:, k, :],
                                                     ALU.mult, ALU.add).then_inc(sems[signal], S.up(signal))
                S.step("act_dve", 6)

        def lin_pe_turns(S, turns, hi, lo, fresh=None):
            lin_pe(S, 6, hi, lo, fresh=fresh)
            with S.loop(pe, turns - 1, dict(lo_ready=6, units_begun=6, lin_ready=6, lin_evac=6)):
                lin_pe(S, 6, hi, lo)

        def keep_act(S, dst):
            act.wait_ge(lin_ready, S.next("lin_ready"))
            act.activation(dst, bank_of(S), ACT.Copy).then_inc(lin_evac, S.up("lin_evac"))
            split(S)

        def merge_act(S, ya, kt):
            for t in range(DT):
                S.step("lin_ready")
                S.step("lin_evac")
                split(S, kt // 8)
                act.wait_ge(dve_act, S.next("dve_act"))
                act.activation(hh[:, t, :], ya[:, t, :], ACT.Copy).then_inc(z_hi, S.up("z_hi"))

        def merge_dve(S, ya, gate, kt):
            for t in range(DT):
                split(S, kt // 8)
                dve.wait_ge(lin_ready, S.next("lin_ready"))
                gated = conv[:, t % 2, :]
                dve.tensor_tensor(gated, bank_of(S), gate[:, t, :], ALU.mult).then_inc(lin_evac, S.up("lin_evac"))
                dve.wait_ge(lin_evac, S.value("lin_evac"))
                dve.tensor_tensor(ya[:, t, :], ya[:, t, :], gated, ALU.add).then_inc(dve_act, S.up("dve_act"))
                dve.wait_ge(dve_act, S.value("dve_act"))
                dve.wait_ge(z_hi, S.next("z_hi"))
                ins = dve.tensor_tensor(hl[:, t, :], ya[:, t, :], hh[:, t, :].bitcast(F32), ALU.subtract)
                ins.then_inc(z_lo, S.up("z_lo"))

        def add_act(S):
            for t in range(DT):
                S.step("lin_ready")
                S.step("lin_evac")
                split(S)

        def add_dve(S, scale=1.0):
            for t in range(DT):
                dve.wait_ge(lin_ready, S.next("lin_ready"))
                s = scale if isinstance(scale, float) else scale[:, t:t + 1]
                ins = dve.scalar_tensor_tensor(x[:, t, :], bank_of(S), s, x[:, t, :], ALU.mult, ALU.add)
                ins.then_inc(lin_evac, S.up("lin_evac"))
                dve.wait_ge(lin_evac, S.value("lin_evac"))
                split(S)


        xs = area(0, CONVT, T)
        y_sc = area(6144, DT, T)
        xdt = area(8192, 2, SSM_H, 64)
        gates = area(8192, 2 * DT, T)
        z_raw, gates_raw = kept_b, kept_a
        STEPS = T // P * SSM_H // 4
        xe = cut(sq, SSM_H, 64)
        st = ht
        b_tok = area(12288, 4 * P)
        cb = area(12800, 2, 4, P)
        au = area(13824, 4, P)
        gg = area(14336, 2, 4, P)
        cd = area(16800, 2, 4, P)
        d_t, dt_t, a_t, e_t = (area(15872 + 64 * i, 2, SSM_H) for i in range(4))
        acum = area(16128, 96)
        dte, ea = area(16224, SSM_H), area(16256, SSM_H)
        xs_tmp = area(16288, T)
        ya_tmp = area(16544, T)
        gate_ple = area(0, DT, T)
        ple_tmp = area(2048, T)

        def dt_pe(S):
            for half in (0, 1):
                for k in range(DT):
                    if not half:
                        if not k:
                            slot = unit(S)
                        pe.wait_ge(h_ready, S.next("h_ready"))
                    last = turned(S, N[1][:, half * SSM_H:(half + 1) * SSM_H], slot, k * SSM_H, SSM_H,
                                  hh[:, k, half * P:(half + 1) * P], hl[:, k, half * P:(half + 1) * P],
                                  k == 0, k == DT - 1)
            last.then_inc(pe_dve, S.up("pe_dve"))

        def dt_sums_pe(S):
            pe.wait_ge(dve_pe, S.next("dve_pe"))
            pe.matmul(N[0][:, 0:64], cst("cum"), a_t.rearrange("p a b -> p (a b)"), start=True, stop=True,
                         skip_group_check=True)
            pe.matmul(N[0][:, 64:96], cst("after"), a_t[:, 0, :], start=True, stop=True,
                      skip_group_check=True).then_inc(pe_dve, S.up("pe_dve"))

        def softplus_act(S, src, tmp):
            act.activation(tmp, src, ACT.Abs).then_inc(act_done, S.up("act_done"))
            act.wait_ge(act_done, S.value("act_done"))
            act.activation(tmp, tmp, ACT.Exp, scale=-1.0).then_inc(act_done, S.up("act_done"))
            act.wait_ge(act_done, S.value("act_done"))
            act.activation(tmp, tmp, ACT.Ln, bias=1.0).then_inc(act_done, S.up("act_done"))
            act.wait_ge(act_done, S.value("act_done"))

        def dt_act(S):
            split(S)
            act.wait_ge(dve_act, S.next("dve_act"))
            softplus_act(S, d_t, e_t)
            act.activation(ea, vec(lv, V2, "A_log"), ACT.Exp).then_inc(act_dve, S.up("act_dve"))

        def dt_sums_act(S):
            act.wait_ge(dve_act, S.next("dve_act"))
            act.activation(dte, acum[:, 64:96], ACT.Exp).then_inc(act_dve, S.up("act_dve"))

        def dt_dve(S):
            split(S)
            dve.wait_ge(pe_dve, S.next("pe_dve"))
            ins = dve.tensor_tensor(d_t, cut(N[1][:, 0:64], 2, SSM_H), rep(vec(lv, V2, "dt_bias"), 2), ALU.add)
            ins.then_inc(dve_act, S.up("dve_act"))
            dve.wait_ge(dve_act, S.value("dve_act"))
            dve.wait_ge(act_dve, S.next("act_dve"))
            dve.scalar_tensor_tensor(dt_t, d_t, 0.0, e_t, ALU.max, ALU.add).then_inc(dve_done, S.up("dve_done"))
            dve.wait_ge(dve_done, S.value("dve_done"))
            dve.scalar_tensor_tensor(a_t, dt_t, -1.0, rep(ea, 2), ALU.mult, ALU.mult).then_inc(dve_pe, S.up("dve_pe"))

        def dt_sums_dve(S):
            dve.wait_ge(pe_dve, S.next("pe_dve"))
            dve.tensor_copy(acum, N[0][:, 0:96]).then_inc(dve_act, S.up("dve_act"))
            S.step("act_dve")

        SC = dict(hi_ready=6, lo_ready=6, units_begun=6, lin_ready=6, lin_evac=6, z_hi=2, z_lo=2, dve_done=6)

        def sc_act(S):
            per = {n: SC[n] for n in ("hi_ready", "units_begun", "lin_ready", "lin_evac", "z_hi")}
            with S.loop(act, DT // 2, per) as turn:
                for k in (0, 1):
                    act.wait_ge(lin_ready, S.next("lin_ready"))
                    act.activation(xs_tmp, bank_of(S), ACT.Copy).then_inc(lin_evac, S.up("lin_evac"))
                    split(S)
                    S.step("lin_ready", 2)
                    S.step("lin_evac", 2)
                    split(S, 2)
                    act.wait_ge(lin_evac, S.value("lin_evac"))
                    act.activation(zh[:, turn * 2 + k, :], ya_tmp, ACT.Copy).then_inc(z_hi, S.up("z_hi"))

        def sc_dve(S):
            w = vec(lv, V2, "sc_conv")
            per = {n: SC[n] for n in ("hi_ready", "lo_ready", "lin_ready", "lin_evac", "z_hi", "z_lo", "dve_done")}
            with S.loop(dve, DT // 2, per) as turn:
                for k in (0, 1):
                    t = turn * 2 + k
                    S.step("lin_ready")
                    dve.wait_ge(lin_evac, S.next("lin_evac"))
                    split(S)
                    dve.wait_ge(lin_ready, S.next("lin_ready"))
                    dve.tensor_tensor(padu[:, 2:], bank_of(S), xs_tmp, ALU.mult).then_inc(lin_evac, S.up("lin_evac"))
                    dve.wait_ge(lin_evac, S.value("lin_evac"))
                    split(S)
                    to = sc_conv
                    ins = dve.tensor_scalar(to, padu[:, 0:T], w[:, bass.ds(t * 3, 1)], None, ALU.mult)
                    ins.then_inc(dve_done, S.up("dve_done"))
                    dve.wait_ge(dve_done, S.value("dve_done"))
                    for j in (1, 2):
                        dve.scalar_tensor_tensor(to, padu[:, j:j + T], w[:, bass.ds(t * 3 + j, 1)], to,
                                                 ALU.mult, ALU.add).then_inc(dve_done, S.up("dve_done"))
                        dve.wait_ge(dve_done, S.value("dve_done"))
                    split(S)
                    dve.wait_ge(lin_ready, S.next("lin_ready"))
                    dve.tensor_tensor(ya_tmp, bank_of(S), to, ALU.mult).then_inc(lin_evac, S.up("lin_evac"))
                    dve.wait_ge(lin_evac, S.value("lin_evac"))
                    dve.wait_ge(z_hi, S.next("z_hi"))
                    ins = dve.tensor_tensor(zl[:, t, :], ya_tmp, zh[:, t, :].bitcast(F32), ALU.subtract)
                    ins.then_inc(z_lo, S.up("z_lo"))
                    dve.wait_ge(z_lo, S.value("z_lo"))

        sc_conv = conv[:, 0, :]

        def ssd_pe(S):
            n = 0
            for c in (0, 1):
                for q in range(XT // 4):
                    for i in range(4):
                        last = pe.transpose(Y[n % 4][:, i * P:(i + 1) * P], xs[:, 4 * q + i, c * P:(c + 1) * P],
                                               cst("ident"))
                    last.then_inc(pe_dve, S.up("pe_dve"))
                    n += 1
                    if n >= 4:
                        pe.wait_ge(dve_pe, S.next("dve_pe"))
            pe.wait_ge(dve_pe, S.next("dve_pe", 3))
            for g in range(SSM_G):
                last = pe.transpose(N[0][:, g * P:(g + 1) * P], xs[:, XT + g, 0:P], cst("ident"))
            last.then_inc(pe_act, S.up("pe_act"))
            for c in (0, 1):
                for g in range(SSM_G):
                    last = pe.matmul(G[c][:, g * P:(g + 1) * P], xs[:, XT + g, c * P:(c + 1) * P],
                                        xs[:, XT + SSM_G + g, c * P:(c + 1) * P], start=True, stop=True,
                                        skip_group_check=True)
                last.then_inc(pe_dve, S.up("pe_dve"))
            pe.wait_ge(act_pe, S.next("act_pe"))
            pe.wait_ge(dve_pe, S.next("dve_pe"))
            for g in range(SSM_G):
                last = pe.matmul(Y[g], b_tok[:, g * P:(g + 1) * P],
                                    xe.rearrange("p a b -> p (a b)")[:, g * 512:(g + 1) * 512], start=True, stop=True)
            last.then_inc(pe_act, S.up("pe_act"))
            pe.wait_ge(act_pe, S.next("act_pe"))
            def sums_of(n):
                pe.wait_ge(dve_pe, S.next("dve_pe"))
                ins = pe.matmul(G[n % 2], cst("ones"), au.rearrange("p a b -> p (a b)"), start=True, stop=True)
                ins.then_inc(pe_dve, S.up("pe_dve"))

            sums_of(0)
            for n in range(STEPS):
                c, q = divmod(n, SSM_H // 4)
                lin_pe(S, 1, hh, hl)
                if n + 1 < STEPS:
                    sums_of(n + 1)
                lin_pe(S, 1, hh, hl)
                pe.wait_ge(dve_pe, S.next("dve_pe"))
                for i in range(4):
                    h, part = 4 * q + i, slice(i % 2 * 64, i % 2 * 64 + 64)
                    acc = N[n % 2][part, i // 2 * P:(i // 2 + 1) * P]
                    last = pe.matmul(acc, xdt[:, c, h, :], gg[:, n % 2, i, :], start=True, stop=c == 0,
                                     skip_group_check=True)
                    if c:
                        last = pe.matmul(acc, st[:, h * 64:(h + 1) * 64], cd[:, n % 2, i, :], start=False, stop=True,
                                         skip_group_check=True)
                last.then_inc(pe_dve, S.up("pe_dve"))

        def ssd_act(S):
            act.wait_ge(pe_act, S.next("pe_act"))
            act.activation(b_tok, N[0], ACT.Copy).then_inc(act_pe, S.up("act_pe"))
            act.wait_ge(pe_act, S.next("pe_act"))
            for g in range(SSM_G):
                last = act.activation(st[:, g * 512:(g + 1) * 512], Y[g], ACT.Copy)
            last.then_inc(act_pe, S.up("act_pe"))
            for n in range(STEPS):
                act.wait_ge(dve_act, S.next("dve_act"))
                flat = gg[:, n % 2, :, :].rearrange("p a b -> p (a b)")
                if n < STEPS // 2:
                    act.activation(flat, flat, ACT.Exp).then_inc(act_dve, S.up("act_dve"))
                else:
                    act.activation(flat, flat, ACT.Exp)
                    ins = act.activation(cd[:, n % 2, :, :].rearrange("p a b -> p (a b)"), G[n % 2], ACT.Exp)
                    ins.then_inc(act_dve, S.up("act_dve"))
                keep_act(S, z_raw[:, n, :])
                keep_act(S, gates_raw[:, n, :])

        def ssd_dve(S):
            n = 0
            for c in (0, 1):
                for q in range(XT // 4):
                    dve.wait_ge(pe_dve, S.next("pe_dve"))
                    dve.tensor_tensor(xdt[:, c, 8 * q:8 * q + 8, :], cut(Y[n % 4], 8, 64),
                                      bc(dt_t[:, c, 8 * q:8 * q + 8], 64), ALU.mult).then_inc(dve_pe, S.up("dve_pe"))
                    dve.wait_ge(dve_pe, S.value("dve_pe"))
                    n += 1
            dve.tensor_tensor(xe, xdt[:, 0, :, :], bc(dte, 64), ALU.mult).then_inc(dve_pe, S.up("dve_pe"))
            dve.wait_ge(dve_pe, S.value("dve_pe"))
            for c in (0, 1):
                dve.wait_ge(pe_dve, S.next("pe_dve"))
                ins = dve.tensor_tensor(cb[:, c, :, :], cut(G[c], 4, P), rep(cst("cum"), 4), ALU.mult)
                ins.then_inc(dve_done, S.up("dve_done"))
                dve.wait_ge(dve_done, S.value("dve_done"))
            def masked(n):
                c, q = divmod(n, SSM_H // 4)
                ins = dve.tensor_tensor(au, rep(cst("cum"), 4), bc(a_t[:, c, 4 * q:4 * q + 4], P), ALU.mult)
                ins.then_inc(dve_pe, S.up("dve_pe"))

            def difference(n):
                c, q = divmod(n, SSM_H // 4)
                dve.wait_ge(pe_dve, S.next("pe_dve"))
                g = gg[:, n % 2, :, :]
                sums = acum[:, c * SSM_H + 4 * q:c * SSM_H + 4 * q + 4]
                dve.tensor_tensor(g, cut(G[n % 2], 4, P), bc(sums, P), ALU.subtract).then_inc(dve_done, S.up("dve_done"))
                dve.wait_ge(dve_done, S.value("dve_done"))
                dve.tensor_scalar(g, g, 0.0, None, ALU.min).then_inc(dve_act, S.up("dve_act"))

            masked(0)
            difference(0)
            masked(1)
            for n in range(STEPS):
                c, q = divmod(n, SSM_H // 4)
                g, grp = gg[:, n % 2, :, :], q // 2
                split(S)
                dve.wait_ge(act_dve, S.next("act_dve"))
                if c:
                    dve.tensor_tensor(cd[:, n % 2, :, :], cd[:, n % 2, :, :], rep(xs[:, XT + SSM_G + grp, P:T], 4), ALU.mult)
                dve.tensor_tensor(g, g, rep(cb[:, c, grp, :], 4), ALU.mult).then_inc(dve_pe, S.up("dve_pe"))
                if n + 1 < STEPS:
                    difference(n + 1)
                if n + 2 < STEPS:
                    masked(n + 2)
                split(S)
                S.step("lin_ready", 2)
                S.step("lin_evac", 2)
                dve.wait_ge(pe_dve, S.next("pe_dve"))
                for i in (0, 1):
                    t = 2 * q + i
                    part = xs[:, t, c * P:(c + 1) * P]
                    ins = dve.scalar_tensor_tensor(part, part, vec(lv, V2, "m_D", t, 1),
                                                   N[n % 2][:, i * P:(i + 1) * P], ALU.mult, ALU.add)
                    ins.then_inc(dve_done, S.up("dve_done"))
            dve.wait_ge(dve_done, S.value("dve_done"))

        squares, roots = (sq, ht), (std, sg)

        def z_act(S):
            act.wait_ge(lin_evac, S.value("lin_evac"))
            for half in (0, 1):
                z = z_raw[:, half * 8:half * 8 + 8, :]
                act.activation(z, z, ACT.Silu).then_inc(act_dve, S.up("act_dve"))
            for half in (0, 1):
                act.wait_ge(dve_act, S.next("dve_act"))
                ins = act.activation(squares[half], xs[:, half * 8:half * 8 + 8, :].rearrange("p a b -> p (a b)"), ACT.Square)
                ins.then_inc(act_pe, S.up("act_pe"))
            for half in (0, 1):
                act.wait_ge(pe_act, S.next("pe_act"))
                ins = act.activation(roots[half], N[half], ACT.Sqrt, bias=eps, scale=1.0 / 512)
                ins.then_inc(act_dve, S.up("act_dve"))
            act.activation(gates, gates_raw, ACT.Sigmoid).then_inc(act_dve, S.up("act_dve"))
            act.wait_ge(act_dve, S.value("act_dve"))
            for t in range(XT):
                act.wait_ge(dve_act, S.next("dve_act"))
                act.activation(zh[:, t, :], xs[:, t, :], ACT.Copy).then_inc(z_hi, S.up("z_hi"))

        def z_dve(S):
            for half in (0, 1):
                dve.wait_ge(act_dve, S.next("act_dve"))
                y = xs[:, half * 8:half * 8 + 8, :]
                dve.tensor_tensor(y, y, z_raw[:, half * 8:half * 8 + 8, :], ALU.mult).then_inc(dve_act, S.up("dve_act"))
            for half in (0, 1):
                dve.wait_ge(act_dve, S.next("act_dve"))
                dve.reciprocal(rstd, roots[half]).then_inc(dve_done, S.up("dve_done"))
                dve.wait_ge(dve_done, S.value("dve_done"))
                for t in range(half * 8, half * 8 + 8):
                    r = rstd[:, t % 8 // 4 * T:(t % 8 // 4 + 1) * T]
                    dve.scalar_tensor_tensor(xs[:, t, :], xs[:, t, :], vec(lv, V2, "m_norm", t, 1), r,
                                             ALU.mult, ALU.mult).then_inc(dve_act, S.up("dve_act"))
                dve.wait_ge(dve_act, S.value("dve_act"))
            for t in range(XT):
                dve.wait_ge(z_hi, S.next("z_hi"))
                ins = dve.tensor_tensor(zl[:, t, :], xs[:, t, :], zh[:, t, :].bitcast(F32), ALU.subtract)
                ins.then_inc(z_lo, S.up("z_lo"))
            dve.wait_ge(act_dve, S.next("act_dve"))
            dve.tensor_tensor(y_sc, y_sc, gates[:, 0:DT, :], ALU.mult).then_inc(dve_done, S.up("dve_done"))
            dve.wait_ge(dve_done, S.value("dve_done"))

        def z_pe(S):
            for half in (0, 1):
                pe.wait_ge(act_pe, S.next("act_pe"))
                for g in (0, 1):
                    for i in range(4):
                        k = g * 4 + i
                        last = pe.matmul(N[half][:, g * T:(g + 1) * T], cst("ones"), squares[half][:, k * T:(k + 1) * T],
                                            start=i == 0, stop=i == 3, skip_group_check=True)
                last.then_inc(pe_act, S.up("pe_act"))

        def layer_mixer_pe(S):
            norm_pe(S, DT)
            dt_pe(S)
            lin_pe_turns(S, 4, hh, hl)
            dt_sums_pe(S)
            lin_pe(S, DT, zh, zl, fresh="z_lo")
            lin_pe_turns(S, 4, hh, hl)
            pe.wait_ge(act_pe, S.next("act_pe"))
            ssd_pe(S)
            z_pe(S)
            lin_pe(S, DT, zh, zl, kt=XT, fresh="z_lo")
            lin_pe(S, DT, hh, hl, fresh="z_lo")

        def layer_mixer_act(S):
            x_norm_act(S, hh)
            dt_act(S)
            sc_act(S)
            dt_sums_act(S)
            lin_copy(S, y_sc, DT)
            conv_act(S, xs, vec(lv, V2, "conv"), vec(lv, V2, "conv_b"))
            act.drain().then_inc(act_pe, S.up("act_pe"))
            ssd_act(S)
            z_act(S)
            merge_act(S, y_sc, XT)
            add_act(S)

        def layer_mixer_dve(S):
            x_norm_dve(S, vec(lv, V2, "mix"), hh, hl)
            dt_dve(S)
            sc_dve(S)
            dt_sums_dve(S)
            pads_dve(S)
            lin_copy(S, y_sc, DT)
            conv_dve(S, vec(lv, V2, "conv"))
            ssd_dve(S)
            z_dve(S)
            merge_dve(S, y_sc, gates[:, DT:, :], XT)
            add_dve(S)


        def ple_pe(S):
            norm_pe(S, DT)
            filler_pe(S, 1)
            pe.wait_ge(z_lo, S.next("z_lo", 2))
            lin_pe(S, DT, hh, hl, fresh="h_ready")
            lin_pe(S, DT, zh[:, 8:10, :], zl[:, 8:10, :], kt=2)
            filler_pe(S, LAYER_PAD)

        def ple_act(S):
            slot = (S.n["hi_ready"] - AHEAD) % RING
            act.wait_ge(hi_ready, S.value("hi_ready", AHEAD - 1))
            for k in (0, 1):
                ins = act.activation(zh[:, 8 + k, :], w_hi[:, slot, k * T:(k + 1) * T].bitcast(F32), ACT.Copy)
                ins.then_inc(z_hi, S.up("z_hi"))
            split(S)
            for t in range(DT):
                act.wait_ge(lin_ready, S.next("lin_ready"))
                act.activation(gate_ple[:, t, :], bank_of(S), ACT.Sigmoid).then_inc(lin_evac, S.up("lin_evac"))
                split(S)
            for t in range(DT):
                S.step("lin_ready")
                S.step("lin_evac")
                split(S, 2 * (t + 1) // 8 - 2 * t // 8)
            split(S, LAYER_PAD)

        def ple_dve(S):
            slot = (S.n["lo_ready"] - AHEAD) % RING
            dve.wait_ge(lo_ready, S.value("lo_ready", AHEAD - 1))
            for k in (0, 1):
                dve.wait_ge(z_hi, S.next("z_hi"))
                ins = dve.tensor_copy(zl[:, 8 + k, :], w_lo[:, slot, k * T:(k + 1) * T].bitcast(F32))
                ins.then_inc(z_lo, S.up("z_lo"))
            split(S)
            for t in range(DT):
                S.step("lin_ready")
                S.step("lin_evac")
                split(S)
            dve.wait_ge(lin_evac, S.value("lin_evac"))
            for t in range(DT):
                dve.wait_ge(lin_ready, S.next("lin_ready"))
                S.step("lin_evac")
                dve.tensor_tensor(ple_tmp, bank_of(S), gate_ple[:, t, :], ALU.mult).then_inc(lin_evac, 1)
                dve.wait_ge(lin_evac, S.value("lin_evac"))
                dve.tensor_tensor(x[:, t, :], x[:, t, :], ple_tmp, ALU.add).then_inc(x_ready, S.up("x_ready"))
                dve.wait_ge(x_ready, S.value("x_ready"))
                split(S, 2 * (t + 1) // 8 - 2 * t // 8)
            split(S, LAYER_PAD)


        y_mla = area(0, DT, T)
        lat = area(2048, QT + KVT, T)
        qn = area(4096, H, T)
        qr = area(6144, H // 2, T)
        kn = area(7168, H, T)
        val = area(9216, 2, D)
        ss, pb, pt = (area(11264 + 768 * i, 2, 384) for i in range(3))
        kr2, krT = area(13568, 2, P), area(13824, T)
        rope_a, rope_b = area(14080, 512), area(14592, 512)
        small = area(18000, 2, SMALL1)
        nm, rs = area(18160, 2, 2), area(18164, 2, 2)
        SCALE = float(P + ROPE) ** -0.5

        def small_pe(S):
            for half in (0, 1):
                for k in range(DT):
                    if not half:
                        if not k:
                            slot = unit(S)
                        pe.wait_ge(h_ready, S.next("h_ready"))
                    last = turned(S, N[1][:, half * SMALL1:(half + 1) * SMALL1], slot, k * SMALL1, SMALL1,
                                  hh[:, k, half * P:(half + 1) * P], hl[:, k, half * P:(half + 1) * P],
                                  k == 0, k == DT - 1)
            last.then_inc(pe_dve, S.up("pe_dve"))

        def k_pe_pe(S):
            pe.wait_ge(dve_pe, S.next("dve_pe"))
            for c in (0, 1):
                last = pe.transpose(N[0][:, c * P:(c + 1) * P], kr2[:, c, :], cst("ident"))
            last.then_inc(pe_dve, S.up("pe_dve"))

        def small_dve(S):
            split(S)
            dve.wait_ge(pe_dve, S.next("pe_dve"))
            dve.tensor_copy(small, cut(N[1][:, 0:2 * SMALL1], 2, SMALL1)).then_inc(dve_done, S.up("dve_done"))
            dve.wait_ge(dve_done, S.value("dve_done"))
            k1, k2 = small[:, :, 0:32], small[:, :, 32:64]
            cos, sin = cut(cst("cos"), 2, 32), cut(cst("sin"), 2, 32)
            a, b = cut(rope_a[:, 0:64], 2, 32), cut(rope_b[:, 0:64], 2, 32)
            for to, u, v, op in ((kr2[:, :, 0:32], k1, k2, ALU.subtract), (kr2[:, :, 32:64], k2, k1, ALU.add)):
                dve.tensor_tensor(a, u, cos, ALU.mult).then_inc(dve_done, S.up("dve_done"))
                dve.wait_ge(dve_done, S.value("dve_done"))
                dve.tensor_tensor(b, v, sin, ALU.mult).then_inc(dve_done, S.up("dve_done"))
                dve.wait_ge(dve_done, S.value("dve_done"))
                dve.tensor_tensor(to, a, b, op).then_inc(dve_done, S.up("dve_done"))
                dve.wait_ge(dve_done, S.value("dve_done"))
            dve.tensor_copy(kr2[:, :, 64:128], kr2[:, :, 0:64]).then_inc(dve_pe, S.up("dve_pe"))
            dve.wait_ge(dve_pe, S.value("dve_pe"))

        def k_pe_dve(S):
            dve.wait_ge(pe_dve, S.next("pe_dve"))
            dve.tensor_copy(krT, N[0][:, 0:T]).then_inc(dve_pe, S.up("dve_pe"))
            dve.wait_ge(dve_pe, S.value("dve_pe"))

        def values_pe(S):
            for k in (0, 1):
                slot = unit(S)
                for c in (0, 1):
                    for half in (0, 1):
                        last = turned(S, (G[0], G[1], N[0], N[1])[2 * c + half], slot, half * 512, 512,
                                      zh[:, QT + k, c * P:(c + 1) * P], zl[:, QT + k, c * P:(c + 1) * P],
                                      k == 0, k == 1)
            last.then_inc(pe_act, S.up("pe_act"))

        def values_act(S):
            act.wait_ge(pe_act, S.next("pe_act"))
            for c in (0, 1):
                for half in (0, 1):
                    last = act.activation(val[:, c, half * 512:(half + 1) * 512], (G[0], G[1], N[0], N[1])[2 * c + half],
                                            ACT.Copy)
            last.then_inc(act_pe, S.up("act_pe"))
            split(S, 2)

        def rope_pe(S):
            pe.wait_ge(act_pe, S.next("act_pe"))
            for m in range(4):
                last = pe.matmul(G[m // 2][:, m % 2 * T:(m % 2 + 1) * T], cst("swap"), qr[:, m, :], start=True,
                                    stop=True, skip_group_check=True)
            last.then_inc(pe_dve, S.up("pe_dve"))

        def rope_dve(S):
            dve.wait_ge(pe_dve, S.next("pe_dve"))
            for m in (0, 1):
                q = qr[:, 2 * m:2 * m + 2, :]
                dve.tensor_tensor(cut(rope_a, 2, T), q, rep(cst("cosT"), 2), ALU.mult).then_inc(dve_done, S.up("dve_done"))
                dve.wait_ge(dve_done, S.value("dve_done"))
                ins = dve.tensor_tensor(cut(rope_b, 2, T), cut(G[m], 2, T), rep(cst("sinT"), 2), ALU.mult)
                ins.then_inc(dve_done, S.up("dve_done"))
                dve.wait_ge(dve_done, S.value("dve_done"))
                signal = "dve_done" if not m else "dve_pe"
                dve.tensor_tensor(q, cut(rope_a, 2, T), cut(rope_b, 2, T), ALU.add).then_inc(sems[signal], S.up(signal))
                dve.wait_ge(sems[signal], S.value(signal))

        def scores_pe(S, h):
            part = slice(h % 2 * 64, h % 2 * 64 + 64)
            for c, at, n in ((0, 0, P), (1, P, T)):
                acc, tok = G[h % 2][:, at:at + n], slice(c * P, (c + 1) * P)
                pe.matmul(acc, qn[:, h, tok], kn[:, h, 0:n], start=True, stop=False, skip_group_check=True)
                last = pe.matmul(acc, qr[part, h // 2, tok], krT[part, 0:n], start=False, stop=True,
                                    skip_group_check=True)
            last.then_inc(pe_dve, S.up("pe_dve"))

        LATE = (N_ADA - ADA_1) // 4

        def attention_pe(S):
            pe.wait_ge(dve_pe, S.next("dve_pe"))
            scores_pe(S, 0)
            for h in range(H):
                if h == 0:
                    scores_pe(S, 1)
                    pe.wait_ge(dve_pe, S.next("dve_pe"))
                elif h + 1 < H:
                    scores_pe(S, h + 1)
                pe.wait_ge(dve_pe, S.next("dve_pe", 2 if h + 1 < H else 1))
                for i in range(3):
                    last = pe.transpose(N[h % 2][:, i * P:(i + 1) * P], pb[:, h % 2, i * P:(i + 1) * P], cst("ident"))
                last.then_inc(pe_act, S.up("pe_act"))
                if h < LATE:
                    S.step("lin_evac")
                    if h >= 2:
                        pe.wait_ge(lin_evac, S.value("lin_evac", 2))
                    rows_pe(S, Y[2 + h % 2][0:2, :])
                pe.wait_ge(act_pe, S.next("act_pe"))
                v = [val[:, c, h * P:(h + 1) * P] for c in (0, 1)]
                p = [pt[:, h % 2, i * P:(i + 1) * P] for i in range(3)]
                if h >= 2:
                    pe.wait_ge(z_lo, S.value("z_lo", -(h - 1)))
                pe.matmul(Y[h % 2][:, 0:P], v[0], p[0], start=True, stop=True, skip_group_check=True)
                pe.matmul(Y[h % 2][:, P:T], v[0], p[1], start=True, stop=False, skip_group_check=True)
                ins = pe.matmul(Y[h % 2][:, P:T], v[1], p[2], start=False, stop=True, skip_group_check=True)
                ins.then_inc(pe_act, S.up("pe_act"))

        def exp_act(S, h):
            act.wait_ge(dve_act, S.next("dve_act"))
            act.activation(pb[:, h % 2, 0:P], ss[:, h % 2, 0:P], ACT.Exp, bias=nm[:, h % 2, 0:1],
                             accum_out=rs[:, h % 2, 0:1])
            act.activation(pb[:, h % 2, P:], ss[:, h % 2, P:], ACT.Exp, bias=nm[:, h % 2, 1:2],
                           accum_out=rs[:, h % 2, 1:2]).then_inc(act_dve, S.up("act_dve"))
            act.wait_ge(act_dve, S.value("act_dve"))

        def attention_act(S):
            exp_act(S, 0)
            for h in range(H):
                if h + 1 < H:
                    exp_act(S, h + 1)
                act.wait_ge(pe_act, S.next("pe_act"))
                act.activation(pt[:, h % 2, :], N[h % 2][:, 0:384], ACT.Copy).then_inc(act_pe, S.up("act_pe"))
                if h < LATE:
                    late_act(S, h)
                act.wait_ge(pe_act, S.next("pe_act"))
                act.activation(zh[:, h, :], Y[h % 2][:, 0:T], ACT.Copy).then_inc(z_hi, S.up("z_hi"))

        def scale_dve(S, h):
            dve.wait_ge(pe_dve, S.next("pe_dve"))
            s = ss[:, h % 2, :]
            ins = dve.scalar_tensor_tensor(s, G[h % 2][:, 0:384], SCALE, cst("mask"), ALU.mult, ALU.add)
            ins.then_inc(dve_pe, S.up("dve_pe"))
            dve.wait_ge(dve_pe, S.value("dve_pe"))
            dve.tensor_reduce(nm[:, h % 2, 0:1], s[:, 0:P], AX.X, ALU.max, negate=True).then_inc(dve_done, S.up("dve_done"))
            dve.wait_ge(dve_done, S.value("dve_done"))
            ins = dve.tensor_reduce(nm[:, h % 2, 1:2], s[:, P:], AX.X, ALU.max, negate=True)
            ins.then_inc(dve_act, S.up("dve_act"))
            dve.wait_ge(dve_act, S.value("dve_act"))

        def probs_dve(S, h):
            dve.wait_ge(act_dve, S.next("act_dve"))
            r = rs[:, h % 2, :]
            dve.reciprocal(r, r).then_inc(dve_done, S.up("dve_done"))
            dve.wait_ge(dve_done, S.value("dve_done"))
            ins = dve.tensor_scalar(pb[:, h % 2, 0:P], pb[:, h % 2, 0:P], r[:, 0:1], None, ALU.mult)
            ins.then_inc(dve_done, S.up("dve_done"))
            dve.wait_ge(dve_done, S.value("dve_done"))
            ins = dve.tensor_scalar(pb[:, h % 2, P:], pb[:, h % 2, P:], r[:, 1:2], None, ALU.mult)
            ins.then_inc(dve_pe, S.up("dve_pe"))
            dve.wait_ge(dve_pe, S.value("dve_pe"))

        def attention_dve(S):
            scale_dve(S, 0)
            for h in range(H):
                if h + 1 < H:
                    scale_dve(S, h + 1)
                probs_dve(S, h)
                if h < LATE:
                    split(S, 4)
                    S.step("lin_ready")
                    S.step("lin_evac")
                if h >= 1:
                    lo_dve(S, h - 1, Y[(h - 1) % 2][:, 0:T])
            lo_dve(S, H - 1, Y[(H - 1) % 2][:, 0:T])


        gt = area(2048, CONVT, T)
        at_ = area(8192, 16, P)
        uu, tt = area(10240, 16, P), area(12288, 16, P)
        kd = area(14336, 16, P)
        attn = cut(ht, 16, P)
        diag = cut(sq, 4, 4, P)
        tmp = [area(16384 + 512 * i, 4, P) for i in range(3)]
        lt = cut(sg, 4, P)
        er = cut(std, 4, P)
        state = area(16384, H, P)
        vn = cut(sq[:, 0:1024], H, P)
        o_t = area(8192, H, T)
        gs = [area(17920 + 16 * i, 16) for i in range(5)]
        g_t, beta_t, rkb, rq, sp_t = gs
        r_qk = area(18168, 2, 16)
        dec = area(18200, 2, 16)
        kbs, kds = area(18232, 16), area(18248, 16)
        cdk = area(18264, 16, 2)
        ea1 = area(18296, H)

        def block_of(c):
            return slice(c * 64, c * 64 + 64)

        def gdn_small_pe(S):
            pe.wait_ge(act_pe, S.next("act_pe"))
            for part in (0, 1):
                for i in range(16):
                    last = pe.matmul(N[0][:, part * 16 + i:part * 16 + i + 1], sq[:, i * P:(i + 1) * P],
                                        cst("ones", 0, 1), start=True, stop=True, skip_group_check=True)
                last.then_inc(pe_act, S.up("pe_act"))
                if not part:
                    pe.wait_ge(act_pe, S.next("act_pe"))

        def decay_pe(S):
            pe.wait_ge(dve_pe, S.next("dve_pe"))
            pe.matmul(N[1][:, 0:16], cst("cum64"), g_t, start=True, stop=True, skip_group_check=True)
            ins = pe.matmul(N[1][:, 16:32], cst("all64"), g_t, start=True, stop=True, skip_group_check=True)
            ins.then_inc(pe_dve, S.up("pe_dve"))

        def gdn_small_act(S):
            for part in (0, 1):
                ins = act.activation(sq, gt[:, part * 8:part * 8 + 8, :].rearrange("p a b -> p (a b)"), ACT.Square)
                ins.then_inc(act_pe, S.up("act_pe"))
                act.wait_ge(pe_act, S.next("pe_act"))
            ins = act.activation(r_qk.rearrange("p a b -> p (a b)"), N[0][:, 0:32], ACT.Sqrt, bias=eps)
            ins.then_inc(act_dve, S.up("act_dve"))

        def decay_act(S):
            ins = act.activation(cut(beta_t, H, 2), small[:, :, 72:80].rearrange("p t h -> p h t"), ACT.Sigmoid)
            ins.then_inc(act_done, S.up("act_done"))
            act.wait_ge(act_done, S.value("act_done"))
            act.wait_ge(dve_act, S.next("dve_act"))
            softplus_act(S, sp_t, dec[:, 0, :])
            act.activation(ea1, vec(v1, V1, "a_log"), ACT.Exp).then_inc(act_dve, S.up("act_dve"))

        def decayed_act(S):
            act.wait_ge(dve_act, S.next("dve_act"))
            act.activation(dec, dec, ACT.Exp).then_inc(act_dve, S.up("act_dve"))

        def decay_dve(S):
            dve.wait_ge(act_dve, S.next("act_dve"))
            dve.scalar_tensor_tensor(g_t, sp_t, 0.0, dec[:, 0, :], ALU.max, ALU.add).then_inc(dve_done, S.up("dve_done"))
            dve.wait_ge(dve_done, S.value("dve_done"))
            ins = dve.scalar_tensor_tensor(cut(g_t, H, 2), cut(g_t, H, 2), -1.0, bc(ea1, 2), ALU.mult, ALU.mult)
            ins.then_inc(dve_pe, S.up("dve_pe"))
            dve.wait_ge(pe_dve, S.next("pe_dve"))
            dve.tensor_copy(sp_t, N[1][:, 0:16]).then_inc(dve_done, S.up("dve_done"))
            dve.wait_ge(dve_done, S.value("dve_done"))
            dve.tensor_copy(dec[:, 0, :], sp_t).then_inc(dve_done, S.up("dve_done"))
            dve.wait_ge(dve_done, S.value("dve_done"))
            dve.tensor_tensor(dec[:, 1, :], N[1][:, 16:32], sp_t, ALU.subtract).then_inc(dve_act, S.up("dve_act"))
            S.step("act_dve")

        def bias_dve(S):
            dve.tensor_tensor(cut(sp_t, H, 2), small[:, :, 64:72].rearrange("p t h -> p h t"),
                              bc(vec(v1, V1, "dt_bias"), 2), ALU.add).then_inc(dve_act, S.up("dve_act"))

        def gdn_small_dve(S):
            dve.wait_ge(act_dve, S.next("act_dve"))
            dve.reciprocal(r_qk, r_qk).then_inc(dve_done, S.up("dve_done"))
            dve.wait_ge(dve_done, S.value("dve_done"))
            rk = r_qk[:, 1, :]
            dve.tensor_scalar(rq, r_qk[:, 0, :], float(P) ** -0.5, None, ALU.mult)
            dve.tensor_tensor(rkb, rk, beta_t, ALU.mult).then_inc(dve_done, S.up("dve_done"))
            dve.wait_ge(dve_done, S.value("dve_done"))
            dve.tensor_tensor(kbs, rkb, dec[:, 0, :], ALU.mult)
            dve.tensor_tensor(kds, rk, dec[:, 1, :], ALU.mult).then_inc(dve_done, S.up("dve_done"))
            dve.wait_ge(dve_done, S.value("dve_done"))

        def gdn_gram_pe(S):
            for p in range(4):
                pe.wait_ge(dve_pe, S.next("dve_pe"))
                for i in range(4):
                    last = pe.matmul(Y[i], cst("ones"), diag[:, i, :, :].rearrange("p a b -> p (a b)"), start=True,
                                        stop=True)
                last.then_inc(pe_dve, S.up("pe_dve"))
                pe.wait_ge(dve_pe, S.next("dve_pe"))
                for m in (0, 1):
                    for i in range(4):
                        last = pe.matmul(G[m][:, i * P:(i + 1) * P], tmp[1][:, i, :], tmp[2 if m == 0 else 0][:, i, :],
                                            start=True, stop=True, skip_group_check=True)
                for m in (0, 1):
                    for i in range(4):
                        h, c = 2 * p + i // 2, i % 2
                        last = pe.transpose(N[m][:, i * P:(i + 1) * P], gt[:, (m + 1) * H + h, c * P:(c + 1) * P],
                                               cst("ident"))
                last.then_inc(pe_dve, S.up("pe_dve"))

        def gdn_gram_act(S):
            for p in range(4):
                act.wait_ge(dve_act, S.next("dve_act"))
                act.activation(lt, lt, ACT.Exp).then_inc(act_done, S.up("act_done"))
                act.wait_ge(act_done, S.value("act_done"))
                act.activation(er.rearrange("p a b -> p (a b)"), Y[3], ACT.Exp).then_inc(act_dve, S.up("act_dve"))
                act.wait_ge(act_dve, S.value("act_dve"))

        def gdn_gram_dve(S):
            qn_, kn_, kb_ = tmp

            def factors(p):
                of = slice(4 * p, 4 * p + 4)
                for i, v in enumerate((rq, r_qk[:, 1, :], rkb)):
                    dve.tensor_tensor(diag[:, i, :, :], rep(cst("ident"), 4), bc(v[:, of], P), ALU.mult)
                if p:
                    dve.wait_ge(act_dve, S.next("act_dve"))
                ins = dve.tensor_tensor(diag[:, 3, :, :], rep(cst("cum64"), 4), bc(g_t[:, of], P), ALU.mult)
                ins.then_inc(dve_pe, S.up("dve_pe"))

            factors(0)
            for p in range(4):
                of = slice(4 * p, 4 * p + 4)
                two = lambda m: gt[:, m * H + 2 * p:m * H + 2 * p + 2, :].rearrange("p a (b c) -> p (a b) c", b=2)
                dve.wait_ge(pe_dve, S.next("pe_dve"))
                dve.tensor_tensor(qn_, two(0), cut(Y[0], 4, P), ALU.mult).then_inc(dve_done, S.up("dve_done"))
                dve.tensor_tensor(kn_, two(1), cut(Y[1], 4, P), ALU.mult).then_inc(dve_done, S.up("dve_done"))
                dve.tensor_tensor(kb_, two(1), cut(Y[2], 4, P), ALU.mult).then_inc(dve_pe, S.up("dve_pe"))
                dve.wait_ge(dve_pe, S.value("dve_pe"))
                dve.tensor_tensor(lt, cut(Y[3], 4, P), bc(sp_t[:, of], P), ALU.subtract).then_inc(dve_done, S.up("dve_done"))
                dve.wait_ge(dve_done, S.value("dve_done"))
                dve.tensor_scalar(lt, lt, 0.0, None, ALU.min).then_inc(dve_act, S.up("dve_act"))
                dve.wait_ge(dve_act, S.value("dve_act"))
                if p < 3:
                    factors(p + 1)
                else:
                    dve.wait_ge(act_dve, S.next("act_dve"))
                dve.tensor_tensor(lt, lt, rep(cst("cum64"), 4), ALU.mult).then_inc(dve_done, S.up("dve_done"))
                dve.wait_ge(dve_done, S.value("dve_done"))
                dve.tensor_copy(cdk[:, of, :], er[:, :, 63:P:64]).then_inc(dve_done, S.up("dve_done"))
                dve.wait_ge(dve_done, S.value("dve_done"))
                dve.wait_ge(pe_dve, S.next("pe_dve"))
                dve.tensor_tensor(two(0), qn_, er, ALU.mult).then_inc(dve_done, S.up("dve_done"))
                dve.tensor_tensor(at_[:, of, :], cut(G[0], 4, P), lt, ALU.mult).then_inc(dve_done, S.up("dve_done"))
                dve.tensor_tensor(attn[:, of, :], cut(G[1], 4, P), lt, ALU.mult).then_inc(dve_done, S.up("dve_done"))
                dve.tensor_tensor(kd[:, of, :], cut(N[0], 4, P), bc(kds[:, of], P), ALU.mult).then_inc(dve_done, S.up("dve_done"))
                dve.tensor_tensor(two(1), cut(N[0], 4, P), bc(kbs[:, of], P), ALU.mult).then_inc(dve_done, S.up("dve_done"))
                dve.tensor_tensor(two(2), cut(N[1], 4, P), bc(beta_t[:, of], P), ALU.mult).then_inc(dve_done, S.up("dve_done"))
                dve.wait_ge(dve_done, S.value("dve_done"))

        z_silu, gate_a, gate_b = kept_b[:, 0:8, :], kept_b[:, 8:16, :], kept_a[:, 8:16, :]
        kept = [part[:, t, :] for part in (z_silu, gate_a, gate_b) for t in range(8)]
        steps = [(level, p) for level in range(6) for p in range(4)]

        def inverse_pe(S):
            def couple(n):
                pe.wait_ge(dve_pe, S.next("dve_pe"))
                for i in range(4):
                    last = pe.matmul(Y[3][:, i * P:(i + 1) * P], tmp[n % 2][:, i, :], tt[:, 4 * steps[n][1] + i, :],
                                        start=True, stop=True, skip_group_check=True)
                last.then_inc(pe_act, S.up("pe_act"))

            couple(0)
            for n, (_, p) in enumerate(steps):
                lin_pe(S, 1, hh, hl)
                pe.wait_ge(act_pe, S.next("act_pe"))
                if n + 1 < len(steps):
                    couple(n + 1)
                for i in range(4):
                    a = diag[:, n % 2, i, :]
                    pe.matmul(G[n % 2][:, i * P:(i + 1) * P], uu[:, 4 * p + i, :], a, start=True, stop=True,
                              skip_group_check=True)
                    last = pe.matmul(N[n % 2][:, i * P:(i + 1) * P], a, uu[:, 4 * p + i, :], start=True, stop=True,
                                     skip_group_check=True)
                last.then_inc(pe_dve, S.up("pe_dve"))
            pe.wait_ge(lin_evac, S.value("lin_evac"))
            pe.wait_ge(dve_pe, S.next("dve_pe"))
            for p in range(4):
                for i in range(4):
                    h, c = 2 * p + i // 2, i % 2
                    last = pe.matmul(Y[p][:, i * P:(i + 1) * P], gt[:, H + h, c * P:(c + 1) * P], uu[:, 4 * p + i, :],
                                        start=True, stop=True, skip_group_check=True)
            last.then_inc(pe_act, S.up("pe_act"))

        def inverse_act(S):
            for n in range(len(steps)):
                act.wait_ge(pe_act, S.next("pe_act"))
                act.activation(diag[:, n % 2, :, :], cut(Y[3], 4, P), ACT.Copy).then_inc(act_pe, S.up("act_pe"))
                keep_act(S, kept[n])
            act.wait_ge(pe_act, S.next("pe_act"))
            for p in range(4):
                last = act.activation(tt[:, 4 * p:4 * p + 4, :], cut(Y[p], 4, P), ACT.Copy, scale=-1.0)
            last.then_inc(act_pe, S.up("act_pe"))
            act.wait_ge(lin_evac, S.value("lin_evac"))
            act.activation(z_silu, z_silu, ACT.Silu)
            act.activation(gate_a, gate_a, ACT.Sigmoid)
            act.activation(gate_b, gate_b, ACT.Sigmoid).then_inc(act_dve, S.up("act_dve"))

        def inverse_dve(S):
            for m in (uu, tt):
                dve.tensor_copy(m, rep(cst("ident"), 16)).then_inc(dve_done, S.up("dve_done"))
                dve.wait_ge(dve_done, S.value("dve_done"))

            def coupling(n):
                level, p = steps[n]
                ins = dve.tensor_tensor(tmp[n % 2], at_[:, 4 * p:4 * p + 4, :], rep(cst(f"level{level}"), 4), ALU.mult)
                ins.then_inc(dve_pe, S.up("dve_pe"))
                dve.wait_ge(dve_pe, S.value("dve_pe"))

            coupling(0)
            for n, (_, p) in enumerate(steps):
                if n + 1 < len(steps):
                    coupling(n + 1)
                split(S)
                S.step("lin_ready")
                S.step("lin_evac")
                dve.wait_ge(pe_dve, S.next("pe_dve"))
                of = slice(4 * p, 4 * p + 4)
                ins = dve.tensor_tensor(tt[:, of, :], tt[:, of, :], cut(G[n % 2], 4, P), ALU.subtract)
                ins.then_inc(dve_done, S.up("dve_done"))
                dve.wait_ge(dve_done, S.value("dve_done"))
                signal = "dve_done" if n + 1 < len(steps) else "dve_pe"
                ins = dve.tensor_tensor(uu[:, of, :], uu[:, of, :], cut(N[n % 2], 4, P), ALU.subtract)
                ins.then_inc(sems[signal], S.up(signal))
                dve.wait_ge(sems[signal], S.value(signal))

        def scan_pe(S):
            pe.wait_ge(act_pe, S.next("act_pe"))
            for n in range(4):
                c, r = n // 2, block_of(n % 2)
                for b in (0, 1):
                    if n:
                        pe.wait_ge(dve_pe, S.next("dve_pe"))
                    for i in range(4):
                        h = 4 * b + i
                        acc = G[b][r, i * P:(i + 1) * P]
                        last = pe.matmul(acc, uu[r, 2 * h + c, r], gt[r, 2 * H + h, c * P:(c + 1) * P], start=True,
                                            stop=not n, skip_group_check=True)
                        if n:
                            last = pe.matmul(acc, tt[:, 2 * h + c, r], state[:, h, :], start=False, stop=True,
                                                skip_group_check=True)
                    last.then_inc(pe_act, S.up("pe_act"))
                for b in (0, 1):
                    pe.wait_ge(act_pe, S.next("act_pe"))
                    for i in range(4):
                        h = 4 * b + i
                        acc = N[b][:, i * 64:(i + 1) * 64]
                        last = pe.matmul(acc, vn[r, h, :], attn[r, 2 * h + c, r], start=True, stop=not n,
                                            skip_group_check=True)
                        if n:
                            last = pe.matmul(acc, state[:, h, :], gt[:, h, n * 64:(n + 1) * 64], start=False, stop=True,
                                                skip_group_check=True)
                        if n < 3:
                            last = pe.matmul(Y[b][:, i * P:(i + 1) * P], kd[r, 2 * h + c, :], vn[r, h, :], start=True,
                                                stop=True, skip_group_check=True)
                    last.then_inc(pe_dve, S.up("pe_dve"))

        def scan_act(S):
            for n in range(4):
                r = block_of(n % 2)
                for b in (0, 1):
                    act.wait_ge(pe_act, S.next("pe_act"))
                    ins = act.activation(vn[r, 4 * b:4 * b + 4, :], cut(G[b], 4, P)[r, :, :], ACT.Copy)
                    ins.then_inc(act_pe, S.up("act_pe"))
                    act.wait_ge(act_pe, S.value("act_pe"))

        def scan_dve(S):
            for n in range(4):
                for b in (0, 1):
                    dve.wait_ge(pe_dve, S.next("pe_dve"))
                    signal = "dve_done" if n < 3 else "dve_act"
                    ins = dve.tensor_copy(o_t[:, 4 * b:4 * b + 4, n * 64:(n + 1) * 64], cut(N[b][:, 0:T], 4, 64))
                    ins.then_inc(sems[signal], S.up(signal))
                    dve.wait_ge(sems[signal], S.value(signal))
                    if n:
                        dve.wait_ge(dve_pe, S.value("dve_pe"))
                    for i in range(4 if n < 3 else 0):
                        h = 4 * b + i
                        got, name = Y[b][:, i * P:(i + 1) * P], "dve_pe" if i == 3 else "dve_done"
                        if n:
                            dve.scalar_tensor_tensor(state[:, h, :], state[:, h, :],
                                                     cdk[:, 2 * h + n // 2, n % 2:n % 2 + 1], got, ALU.mult,
                                                     ALU.add).then_inc(sems[name], S.up(name))
                        else:
                            dve.tensor_copy(state[:, h, :], got).then_inc(sems[name], S.up(name))

        def gdn_out_pe(S):
            pe.wait_ge(act_pe, S.next("act_pe"))
            for i in range(16):
                last = pe.matmul(N[0][:, i:i + 1], sq[:, i * P:(i + 1) * P], cst("ones", 0, 1), start=True, stop=True,
                                 skip_group_check=True)
            last.then_inc(pe_act, S.up("pe_act"))
            for i in range(4):
                pe.wait_ge(dve_pe, S.next("dve_pe"))
                ins = pe.matmul(Y[i], cst("ones"), sq[:, i * 512:(i + 1) * 512], start=True, stop=True)
                ins.then_inc(pe_dve, S.up("pe_dve"))

        def gdn_out_act(S):
            act.wait_ge(dve_act, S.next("dve_act", 2))
            act.activation(sq, o_t.rearrange("p a b -> p (a b)"), ACT.Square).then_inc(act_pe, S.up("act_pe"))
            act.wait_ge(pe_act, S.next("pe_act"))
            act.activation(rq, N[0][:, 0:16], ACT.Sqrt, bias=eps, scale=1.0 / P).then_inc(act_dve, S.up("act_dve"))
            act.wait_ge(dve_act, S.next("dve_act"))
            for t in range(H):
                act.activation(zh[:, t, :], o_t[:, t, :], ACT.Copy).then_inc(z_hi, S.up("z_hi"))

        def gdn_out_dve(S):
            S.step("act_dve")
            dve.wait_ge(act_dve, S.next("act_dve"))
            dve.reciprocal(rq, rq).then_inc(dve_done, S.up("dve_done"))
            dve.wait_ge(dve_done, S.value("dve_done"))
            for i in range(4):
                ins = dve.tensor_tensor(cut(sq[:, i * 512:(i + 1) * 512], 4, P), rep(cst("ident"), 4),
                                        bc(rq[:, 4 * i:4 * i + 4], P), ALU.mult)
                ins.then_inc(dve_pe, S.up("dve_pe"))
            for i in range(4):
                dve.wait_ge(pe_dve, S.next("pe_dve"))
                o = o_t[:, 2 * i:2 * i + 2, :]
                ins = dve.scalar_tensor_tensor(o, o, vec(v1, V1, "g_out"), cut(Y[i], 2, T), ALU.mult, ALU.mult)
                ins.then_inc(dve_done, S.up("dve_done"))
            dve.wait_ge(dve_done, S.value("dve_done"))
            dve.tensor_tensor(o_t, o_t, z_silu, ALU.mult).then_inc(dve_act, S.up("dve_act"))
            dve.wait_ge(dve_act, S.value("dve_act"))
            for t in range(H):
                lo_dve(S, t, o_t[:, t, :])
            dve.tensor_tensor(y_mla, y_mla, gate_a, ALU.mult).then_inc(dve_done, S.up("dve_done"))
            dve.wait_ge(dve_done, S.value("dve_done"))

        def block1_mixer_pe(S):
            norm_pe(S, DT)
            small_pe(S)
            lin_pe(S, QT + KVT, hh, hl)
            k_pe_pe(S)
            pe.wait_ge(dve_pe, S.next("dve_pe"))
            norm_pe(S, QT)
            norm_pe(S, KVT)
            lin_pe(S, H + H // 2, zh, zl, kt=QT, fresh="h_ready")
            lin_pe(S, H, zh[:, QT:QT + KVT, :], zl[:, QT:QT + KVT, :], kt=KVT, fresh="h_ready")
            values_pe(S)
            rope_pe(S)
            attention_pe(S)
            pe.wait_ge(z_lo, S.value("z_lo", -H))
            lin_pe(S, DT, zh, zl, fresh="z_lo")
            columns_pe(S, late_rows, ADA_1, N_ADA - ADA_1)
            decay_pe(S)
            lin_pe_turns(S, 4, hh, hl)
            gdn_small_pe(S)
            gdn_gram_pe(S)
            inverse_pe(S)
            scan_pe(S)
            gdn_out_pe(S)
            lin_pe(S, DT, zh, zl, fresh="z_lo")
            lin_pe(S, DT, hh, hl, fresh="z_lo")

        def block1_mixer_act(S):
            x_norm_act(S, hh, shifts[1])
            split(S)
            lin_copy(S, lat, QT + KVT)
            act.wait_ge(lin_evac, S.value("lin_evac"))
            norm_act(S, lat[:, 0:QT, :], QT, zh)
            norm_act(S, lat[:, QT:, :], KVT, zh[:, QT:QT + KVT, :])
            for t in range(H + H // 2):
                lin_copy_tile(S, qn[:, t, :] if t < H else qr[:, t - H, :], t, QT)
            lin_copy(S, kn, H, kt=KVT)
            values_act(S)
            attention_act(S)
            decay_act(S)
            lin_copy(S, y_mla, DT)
            decayed_act(S)
            conv_act(S, gt, vec(v1, V1, "conv"))
            act.wait_ge(act_dve, S.value("act_dve"))
            gdn_small_act(S)
            gdn_gram_act(S)
            inverse_act(S)
            scan_act(S)
            gdn_out_act(S)
            merge_act(S, y_mla, DT)
            add_act(S)

        def block1_mixer_dve(S):
            x_norm_dve(S, gains[1], hh, hl, shifts[1])
            small_dve(S)
            lin_copy(S, lat, QT + KVT)
            k_pe_dve(S)
            norm_dve(S, lat[:, 0:QT, :], QT, vec(v1, V1, "g_q"), zh, zl)
            norm_dve(S, lat[:, QT:, :], KVT, vec(v1, V1, "g_kv"), zh[:, QT:QT + KVT, :], zl[:, QT:QT + KVT, :])
            lin_copy(S, qn, H + H // 2, kt=QT)
            lin_copy(S, kn, H, kt=KVT)
            split(S, 2)
            rope_dve(S)
            attention_dve(S)
            bias_dve(S)
            lin_copy(S, y_mla, DT)
            late_dve(S)
            decay_dve(S)
            pads_dve(S)
            conv_dve(S, vec(v1, V1, "conv"))
            gdn_small_dve(S)
            gdn_gram_dve(S)
            inverse_dve(S)
            scan_dve(S)
            gdn_out_dve(S)
            merge_dve(S, y_mla, gate_b, DT)
            add_dve(S, gate2)

        @block.sync
        def _(sp):
            S = Side(sems, "sp")
            for dst, src in ((v1, vec1), (con, consts), (v2, vec2), (x.rearrange("p a b -> p (a b)"), x_in)):
                sp.dma_start(dst, src).then_inc(loaded, 16)
            for s in range(RING):
                sp.dma_start(raw[:, s, :], stream[s]).then_inc(raw_loaded[s], 16)
            with sp.Fori(1, UNITS // RING) as turn:
                for s in range(RING):
                    sp.wait_ge(lo_ready, turn * RING + (s + 1 - RING))
                    sp.dma_start(raw[:, s, :], stream[bass.ds(turn * RING + s, 1), :, :].rearrange("a p n -> (a p) n"))\
                      .then_inc(raw_loaded[s], 16)
            sp.wait_ge(result_ready, 1)
            sp.dma_start(out, ht).then_inc(stored, 16)
            sp.wait_ge(stored, 16)
            for s in range(RING):
                sp.wait_ge(raw_loaded[s], 16 * (UNITS // RING))

        @block.gpsimd
        def _(pool):
            pool.memset(eps, EPS).then_inc(cleared, 1)
            pool.memset(padu, 0.0).then_inc(cleared, 1)

        @block.tensor
        def _(pe):
            S = Side(sems, "pe")
            pe.wait_ge(loaded, S.next("loaded", 64))
            norm_pe(S, DT)
            ada_pe(S)
            ffn_pe(S)
            block1_mixer_pe(S)
            norm_pe(S, DT)
            ffn_pe(S)
            filler_pe(S, BLOCK1_PAD)
            norm_pe(S, DT)
            with S.loop(pe, LAYERS, LAYER_PER["pe"]):
                norm_pe(S, DT)
                ffn_pe(S)
                layer_mixer_pe(S)
                norm_pe(S, DT)
                ffn_pe(S)
                ple_pe(S)
            norm_pe(S, DT)

        @block.scalar
        def _(act):
            S = Side(sems, "act")
            act.wait_ge(loaded, S.next("loaded", 64))
            act.wait_ge(cleared, S.next("cleared", 2))
            split(S, AHEAD)
            root_act(S, x, DT)
            ada_act(S)
            S.step("x_ready")
            scaled_act(S, DT, hh, shifts[0])
            ffn_act(S)
            block1_mixer_act(S)
            x_norm_act(S, hh, shifts[2], after="lin_evac")
            ffn_act(S)
            split(S, BLOCK1_PAD)
            x_norm_act(S)
            with S.loop(act, LAYERS, LAYER_PER["act"]):
                x_norm_act(S, hh)
                ffn_act(S)
                layer_mixer_act(S)
                x_norm_act(S, hh, after="lin_evac")
                ffn_act(S)
                x_norm_act(S, hh)
                ple_act(S)
            x_norm_act(S)

        @block.vector
        def _(dve):
            S = Side(sems, "dve")
            dve.wait_ge(loaded, S.next("loaded", 64))
            dve.wait_ge(cleared, S.next("cleared", 2))
            split(S, AHEAD)
            ada_dve(S)
            x_norm_dve(S, gains[0], hh, hl, shifts[0])
            ffn_dve(S, half_gate1)
            block1_mixer_dve(S)
            x_norm_dve(S, gains[2], hh, hl, shifts[2], after="lin_evac")
            ffn_dve(S, half_gate3)
            split(S, BLOCK1_PAD)
            x_norm_dve(S, vec(v1, V1, "g_final"), dst=x, done="x_ready")
            with S.loop(dve, LAYERS, LAYER_PER["dve"]) as layer:
                dve.tensor_copy(lv, v2[:, bass.ds(layer * V2_N, V2_N)]).then_inc(dve_done, S.up("dve_done"))
                dve.wait_ge(dve_done, S.value("dve_done"))
                x_norm_dve(S, vec(lv, V2, "ffn1"), hh, hl)
                ffn_dve(S, 0.5)
                layer_mixer_dve(S)
                x_norm_dve(S, vec(lv, V2, "ffn2"), hh, hl, after="lin_evac")
                ffn_dve(S, 0.5)
                x_norm_dve(S, vec(lv, V2, "ple"), hh, hl)
                ple_dve(S)
            x_norm_dve(S, vec(v1, V1, "final_norm"), done="result_ready")



def tiles(w):
    k, n = w.shape
    return w.reshape(k // P, P, n // P, P).transpose(2, 0, 1, 3).reshape(-1, P, P)


def units(*parts):
    t = np.concatenate(parts)
    t = np.concatenate([t, np.zeros((-len(t) % 8, P, P), np.float32)])
    return t.reshape(-1, 8, P, P).transpose(0, 2, 1, 3).reshape(-1, P, U)


def ffn_units(gate, up, down):
    g, u, d = units(tiles(gate)), units(tiles(up)), down.reshape(FT, P, D)
    order = [g[0], u[0]]
    for f in range(1, FT):
        order += [g[f], u[f], d[f - 1]]
    return np.stack([*order, d[FT - 1]])


def wide_units(w, n):
    out = np.zeros((1, P, U), np.float32)
    out[0, :, :DT * n] = w.reshape(DT, P, n).transpose(1, 0, 2).reshape(P, DT * n)
    return out


def cols(v):
    return np.asarray(v, np.float32).reshape(-1, P).T


def taps(w):
    return w.reshape(w.shape[0], -1, P).transpose(2, 1, 0).reshape(P, -1)


def rows(v):
    return np.broadcast_to(v.reshape(1, -1), (P, v.size))


def block1_units(a):
    w_in, w_uq, w_ukv = a["w_in"][0], a["w_uq"][0], a["w_ukv"][0]
    at = np.cumsum([0, 768, 256, 64, 1024, 1024, 1024, 8, 8, 1024, 2048])
    part = [w_in[:, p:q] for p, q in zip(at[:-1], at[1:])]
    uq = w_uq.reshape(768, H, 192)
    uq = np.concatenate([uq[:, :, :P].reshape(768, -1), uq[:, :, P:].reshape(768, -1)], 1)
    ukv = w_ukv.reshape(256, H, 256)
    ada = a["w_ada"][0].reshape(DT // 2, 2, P, N_ADA // 4, 512).transpose(3, 0, 2, 1, 4).reshape(-1, P, U)
    return [
        ada[:ADA_1],
        ffn_units(a["w1_gate"][0], a["w1_up"][0], a["w1_down"][0]),
        wide_units(np.concatenate([part[2], part[6], part[7]], 1), SMALL1),
        units(tiles(part[0]), tiles(part[1])),
        units(tiles(uq)),
        units(tiles(ukv[:, :, :P].reshape(256, -1))),
        ukv[:, :, P:].reshape(2, P, U),
        ada[ADA_1:],
        units(tiles(a["w_o_mla"][0])),
        units(tiles(w_in[:, at[3]:at[6]])),
        units(tiles(part[8])),
        units(tiles(part[9])),
        units(tiles(a["w_o_gdn"][0])),
        units(tiles(a["w_out"][0])),
        ffn_units(a["w2_gate"][0], a["w2_up"][0], a["w2_down"][0]),
        np.zeros((BLOCK1_PAD, P, U), np.float32),
    ]


def layer_units(a, n):
    g = lambda name: a[name + "_2"][n]
    w_in = g("w_in")
    at = np.cumsum([0, 1024, 1024, 1024, 2048, 3072, 32, 1024, 1024])
    part = [w_in[:, p:q] for p, q in zip(at[:-1], at[1:])]
    each = lambda *ws: np.stack([tiles(w).reshape(-1, DT, P, P) for w in ws], 1).reshape(-1, P, P)
    p = np.zeros((1, P, U), np.float32)
    p[0, :, :2 * T] = g("p")[0].T.reshape(2, P, T).transpose(1, 0, 2).reshape(P, -1)
    return [
        ffn_units(g("ffn1_wg"), g("ffn1_wu"), g("ffn1_wd")),
        wide_units(part[5], SSM_H),
        units(each(part[2], part[1], part[0])),
        units(tiles(g("sc_w_out"))),
        units(tiles(part[4])),
        units(each(part[3], np.concatenate([part[6], part[7]], 1))),
        units(tiles(g("m_w_out"))),
        units(tiles(g("w_o"))),
        ffn_units(g("ffn2_wg"), g("ffn2_wu"), g("ffn2_wd")),
        p,
        units(tiles(g("ple_w_gate"))),
        units(tiles(g("ple_w_proj"))),
        np.zeros((LAYER_PAD, P, U), np.float32),
    ]


def kernel(**inputs):
    import concourse.bacc as bacc
    from concourse.bass_utils import run_bass_kernel_spmd as run

    a = {k: np.ascontiguousarray(v) for k, v in inputs.items()}
    parts = block1_units(a)
    assert sum(map(len, parts)) == BLOCK1_UNITS + BLOCK1_PAD
    for n in range(LAYERS):
        of_layer = layer_units(a, n)
        assert sum(map(len, of_layer)) == LAYER_UNITS + LAYER_PAD
        parts += of_layer
    parts.append(np.zeros((RING, P, U), np.float32))
    vec1 = np.concatenate([cols(a["c"]), cols(a["b_ada"]), cols(a["g_ffn1"]), cols(a["g_mix"]), cols(a["g_q_lat"]),
                           cols(a["g_kv_lat"]), taps(a["w_conv"][0]), cols(a["g_gdn_out"]), cols(a["g_ffn2"]),
                           cols(a["g_final"]), cols(a["final_norm_2"]), rows(a["dt_bias"]), rows(a["a_log"])], 1)
    vec2 = []
    for n in range(LAYERS):
        g = {k[:-2]: v[n] for k, v in a.items() if k.endswith("_2") and k != "final_norm_2"}
        vec2 += [cols(g["ffn1_norm"]), cols(g["mix_norm"]), taps(g["sc_conv_w"]), taps(g["m_conv_w"]),
                 cols(g["m_conv_b"]), cols(np.repeat(g["m_D"], 64)), cols(g["m_norm"]), cols(g["ffn2_norm"]),
                 cols(g["ple_norm"]), rows(g["m_dt_bias"]), rows(g["m_A_log"])]
    arrays = {
        "stream": np.concatenate(parts),
        "x": a["x"][0].T.reshape(DT, P, T).transpose(1, 0, 2).reshape(P, -1),
        "consts": constants(),
        "vec1": vec1,
        "vec2": np.concatenate(vec2, 1),
    }
    arrays = {k: np.ascontiguousarray(v, np.float32) for k, v in arrays.items()}
    nc = bacc.Bacc("TRN2", target_bir_lowering=False, num_devices=1)
    aps = [nc.dram_tensor(k, v.shape, F32, kind="ExternalInput").ap() for k, v in arrays.items()]
    out = nc.dram_tensor("out", (P, DT * T), F32, kind="ExternalOutput").ap()
    build(nc, *aps, out)
    r = run(nc, [arrays], core_ids=[0])
    y = r.results[0]["out"]
    return y.reshape(P, DT, T).transpose(2, 1, 0).reshape(1, T, D)
```
